# Optimizing a Trainium2 kernel written in Bass

```python
import jax, jax.numpy as jnp
from jax import lax
import numpy as np
import math

D_MODEL = 1024
BATCH = 1
SEQ = 512
DEPTH = 2

N_MIXERS = 3
POOL_WINDOWS = (2, 4, 8, 16)
POOL_GROUPS = len(POOL_WINDOWS)
POOL_GROUP_DIM = D_MODEL // POOL_GROUPS
SGU_CHUNK = 128
SGU_WIDTH = D_MODEL
SGU_HEAD_DIM = 128
SGU_HEADS = SGU_WIDTH // SGU_HEAD_DIM
MLA_HEADS = 16
MLA_Q_LORA = 256
MLA_KV_LORA = 128
MLA_NOPE = 128
MLA_ROPE = 64
MLA_V = 128
ROPE_THETA = 10000.0
Q_BLOCK = 128
D_FF = 4 * D_MODEL
RMS_EPS = 1e-6
LN_EPS = 1e-5
MAX_POS_OFFSET = 4096
N_POOL_LAYERS = len(range(0, DEPTH, N_MIXERS))
N_SGU_LAYERS = len(range(1, DEPTH, N_MIXERS))
N_MLA_LAYERS = len(range(2, DEPTH, N_MIXERS))


def rmsnorm(x, g):
    xf = x.astype(jnp.float32)
    y = xf * lax.rsqrt(jnp.mean(xf * xf, axis=-1, keepdims=True) + RMS_EPS)
    return (y * g.astype(jnp.float32)).astype(x.dtype)

def layernorm(x, g, b):
    xf = x.astype(jnp.float32)
    mu = jnp.mean(xf, axis=-1, keepdims=True)
    xc = xf - mu
    var = jnp.mean(xc * xc, axis=-1, keepdims=True)
    y = xc * lax.rsqrt(var + LN_EPS)
    return (y * g.astype(jnp.float32) + b.astype(jnp.float32)).astype(x.dtype)

def modulate(h, shift, scale):
    return h * (1.0 + scale[:, None, :]) + shift[:, None, :]

def pool_mixer(h, w, scale):
    B_, S_, _ = h.shape
    hf = h.astype(jnp.float32).reshape(B_, S_, POOL_GROUPS, POOL_GROUP_DIM)
    cs = jnp.cumsum(hf, axis=1)
    cs = jnp.concatenate([jnp.zeros_like(cs[:, :1]), cs], axis=1)
    t = jnp.arange(S_, dtype=jnp.float32)
    outs = []
    for gi, win in enumerate(POOL_WINDOWS):
        csg = cs[:, :, gi]
        upper = csg[:, 1:]
        lower = jnp.concatenate([jnp.zeros_like(csg[:, :win - 1]), csg[:, :S_ - win + 1]], axis=1)
        count = jnp.minimum(t + 1.0, float(win))[None, :, None]
        outs.append((upper - lower) / count - hf[:, :, gi])
    pooled = jnp.stack(outs, axis=2).astype(h.dtype)
    y = jnp.einsum('bsgc,gcd->bsgd', pooled, w).reshape(B_, S_, D_MODEL)
    return y * scale

def sgu_mixer(h, w_in, ln_g, ln_b, w_s, b_s, w_out):
    B_, S_, _ = h.shape
    z = jax.nn.gelu(h @ w_in, approximate=False)
    u, v = jnp.split(z, 2, axis=-1)
    v = layernorm(v, ln_g, ln_b)
    nc = S_ // SGU_CHUNK
    v = v.reshape(B_, nc, SGU_CHUNK, SGU_HEADS, SGU_HEAD_DIM)
    mask = jnp.tril(jnp.ones((SGU_CHUNK, SGU_CHUNK), dtype=bool))
    ws = jnp.where(mask[None], w_s, 0)
    mixed = jnp.einsum('hts,bnshc->bnthc', ws, v) + b_s.T[None, None, :, :, None]
    gated = u * mixed.reshape(B_, S_, SGU_WIDTH)
    return gated @ w_out

def apply_rope(x, cos, sin):
    x1, x2 = jnp.split(x, 2, axis=-1)
    return jnp.concatenate([x1 * cos - x2 * sin, x2 * cos + x1 * sin], axis=-1)

def mla_mixer(h, positions, w_dq_dkv, q_norm_g, kv_norm_g, w_uq, w_ukv, w_o):
    B_, S_, _ = h.shape
    lat = h @ w_dq_dkv
    c_q, c_kv, k_rope = jnp.split(lat, [MLA_Q_LORA, MLA_Q_LORA + MLA_KV_LORA], axis=-1)
    c_q = rmsnorm(c_q, q_norm_g)
    c_kv = rmsnorm(c_kv, kv_norm_g)
    q = (c_q @ w_uq).reshape(B_, S_, MLA_HEADS, MLA_NOPE + MLA_ROPE)
    q_nope, q_rope = jnp.split(q, [MLA_NOPE], axis=-1)
    kv = (c_kv @ w_ukv).reshape(B_, S_, MLA_HEADS, MLA_NOPE + MLA_V)
    k_nope, v = jnp.split(kv, [MLA_NOPE], axis=-1)
    inv_freq = ROPE_THETA ** (-jnp.arange(0, MLA_ROPE, 2, dtype=jnp.float32) / MLA_ROPE)
    ang = positions.astype(jnp.float32)[..., None] * inv_freq
    cos, sin = jnp.cos(ang), jnp.sin(ang)
    q_rope = apply_rope(q_rope.astype(jnp.float32), cos[:, :, None], sin[:, :, None]).astype(h.dtype)
    k_rope = apply_rope(k_rope.astype(jnp.float32), cos, sin).astype(h.dtype)
    sm_scale = (MLA_NOPE + MLA_ROPE) ** -0.5
    nb = S_ // Q_BLOCK

    def to_blocks(t):
        return jnp.moveaxis(t.reshape(B_, nb, Q_BLOCK, *t.shape[2:]), 1, 0)

    k_idx = jnp.arange(S_)

    def attend_block(args):
        qn, qr, blk = args
        s = jnp.einsum('bqhd,bkhd->bhqk', qn, k_nope, preferred_element_type=jnp.float32)
        s = s + jnp.einsum('bqhr,bkr->bhqk', qr, k_rope, preferred_element_type=jnp.float32)
        q_idx = blk * Q_BLOCK + jnp.arange(Q_BLOCK)
        causal = k_idx[None, :] <= q_idx[:, None]
        s = jnp.where(causal[None, None], s * sm_scale, -1e30)
        p = jax.nn.softmax(s, axis=-1).astype(v.dtype)
        return jnp.einsum('bhqk,bkhd->bqhd', p, v)

    out = lax.map(attend_block, (to_blocks(q_nope), to_blocks(q_rope), jnp.arange(nb)))
    out = jnp.moveaxis(out, 0, 1).reshape(B_, S_, MLA_HEADS * MLA_V)
    return out @ w_o

def sq_relu_mlp(h, w1, w2):
    return jnp.square(jax.nn.relu(h @ w1)) @ w2

def first_inputs(seed: int = 0) -> dict:
    key = jax.random.key(seed)
    ks = jax.random.split(key, 32)
    f32 = jnp.float32

    def nrm(k, shape, std):
        return jax.random.normal(k, shape, f32) * std

    def gain(k, shape):
        return 1.0 + 0.1 * jax.random.normal(k, shape, f32)

    x = jax.random.normal(ks[0], (BATCH, SEQ, D_MODEL), f32)
    c = jax.random.normal(ks[1], (BATCH, D_MODEL), f32)
    offset = jax.random.randint(ks[2], (BATCH, 1), 0, MAX_POS_OFFSET, dtype=jnp.int32)
    positions = (offset + jnp.arange(SEQ, dtype=jnp.int32)[None, :]).astype(jnp.int32)
    return {
        'x': x,
        'c': c,
        'positions': positions,
        'ada_w': nrm(ks[3], (DEPTH, D_MODEL, 6 * D_MODEL), 0.5 * D_MODEL ** -0.5),
        'ada_b': nrm(ks[4], (DEPTH, 6 * D_MODEL), 0.02),
        'norm_mix_g': gain(ks[5], (DEPTH, D_MODEL)),
        'norm_mlp_g': gain(ks[6], (DEPTH, D_MODEL)),
        'pool_w': nrm(ks[7], (N_POOL_LAYERS, POOL_GROUPS, POOL_GROUP_DIM, POOL_GROUP_DIM), POOL_GROUP_DIM ** -0.5),
        'pool_scale': gain(ks[8], (N_POOL_LAYERS, D_MODEL)),
        'sgu_w_in': nrm(ks[9], (N_SGU_LAYERS, D_MODEL, 2 * SGU_WIDTH), D_MODEL ** -0.5),
        'sgu_ln_g': gain(ks[10], (N_SGU_LAYERS, SGU_WIDTH)),
        'sgu_ln_b': nrm(ks[11], (N_SGU_LAYERS, SGU_WIDTH), 0.02),
        'sgu_w_s': nrm(ks[12], (N_SGU_LAYERS, SGU_HEADS, SGU_CHUNK, SGU_CHUNK), SGU_CHUNK ** -0.5),
        'sgu_b_s': gain(ks[13], (N_SGU_LAYERS, SGU_HEADS, SGU_CHUNK)),
        'sgu_w_out': nrm(ks[14], (N_SGU_LAYERS, SGU_WIDTH, D_MODEL), SGU_WIDTH ** -0.5),
        'mla_w_dq_dkv': nrm(ks[15], (N_MLA_LAYERS, D_MODEL, MLA_Q_LORA + MLA_KV_LORA + MLA_ROPE), D_MODEL ** -0.5),
        'mla_q_norm_g': gain(ks[16], (N_MLA_LAYERS, MLA_Q_LORA)),
        'mla_kv_norm_g': gain(ks[17], (N_MLA_LAYERS, MLA_KV_LORA)),
        'mla_w_uq': nrm(ks[18], (N_MLA_LAYERS, MLA_Q_LORA, MLA_HEADS * (MLA_NOPE + MLA_ROPE)), MLA_Q_LORA ** -0.5),
        'mla_w_ukv': nrm(ks[19], (N_MLA_LAYERS, MLA_KV_LORA, MLA_HEADS * (MLA_NOPE + MLA_V)), MLA_KV_LORA ** -0.5),
        'mla_w_o': nrm(ks[20], (N_MLA_LAYERS, MLA_HEADS * MLA_V, D_MODEL), (MLA_HEADS * MLA_V) ** -0.5),
        'mlp_w1': nrm(ks[21], (DEPTH, D_MODEL, D_FF), D_MODEL ** -0.5),
        'mlp_w2': nrm(ks[22], (DEPTH, D_FF, D_MODEL), D_FF ** -0.5),
        'final_g': gain(ks[23], (D_MODEL,)),
    }

def first_block(x, c, positions, ada_w, ada_b, norm_mix_g, norm_mlp_g, pool_w, pool_scale,
              sgu_w_in, sgu_ln_g, sgu_ln_b, sgu_w_s, sgu_b_s, sgu_w_out,
              mla_w_dq_dkv, mla_q_norm_g, mla_kv_norm_g, mla_w_uq, mla_w_ukv, mla_w_o,
              mlp_w1, mlp_w2, final_g):
    c_act = jax.nn.silu(c)
    for i in range(DEPTH):
        mod = c_act @ ada_w[i] + ada_b[i]
        sh1, sc1, g1, sh2, sc2, g2 = jnp.split(mod, 6, axis=-1)
        h = modulate(rmsnorm(x, norm_mix_g[i]), sh1, sc1)
        kind, j = i % N_MIXERS, i // N_MIXERS
        if kind == 0:
            y = pool_mixer(h, pool_w[j], pool_scale[j])
        elif kind == 1:
            y = sgu_mixer(h, sgu_w_in[j], sgu_ln_g[j], sgu_ln_b[j], sgu_w_s[j], sgu_b_s[j], sgu_w_out[j])
        else:
            y = mla_mixer(h, positions, mla_w_dq_dkv[j], mla_q_norm_g[j], mla_kv_norm_g[j],
                          mla_w_uq[j], mla_w_ukv[j], mla_w_o[j])
        x = x + g1[:, None, :] * y
        h = modulate(rmsnorm(x, norm_mlp_g[i]), sh2, sc2)
        x = x + g2[:, None, :] * sq_relu_mlp(h, mlp_w1[i], mlp_w2[i])
    return rmsnorm(x, final_g)


DEPTH_2 = 1

HEAD_DIM = 64
D_ATTN = D_MODEL // 2
D_RWKV = D_MODEL - D_ATTN
N_Q_HEADS = D_ATTN // HEAD_DIM
N_KV_HEADS = max(1, N_Q_HEADS // 4)
Q_PER_KV = N_Q_HEADS // N_KV_HEADS
D_KV = N_KV_HEADS * HEAD_DIM
WINDOW = 128
BLOCK = 128
N_BUCKETS = 32
MAX_DISTANCE = 128
N_RWKV_HEADS = D_RWKV // HEAD_DIM
LORA_DECAY = 64
LORA_ICLR = 64
LORA_GATE = 128
RWKV_COLS = 3 * D_RWKV + LORA_DECAY + LORA_ICLR + LORA_GATE
RWKV_SPLITS = (D_RWKV, 2 * D_RWKV, 3 * D_RWKV, 3 * D_RWKV + LORA_DECAY, 3 * D_RWKV + LORA_DECAY + LORA_ICLR)
D_IN = D_ATTN + 2 * D_KV + RWKV_COLS
D_FF_2 = 4 * D_MODEL
CONV_WIDTH = 3
NORM_EPS = 1e-6
GN_EPS = 64e-5
NEG_INF = -1e30


def rms_norm(x, g):
    xf = x.astype(jnp.float32)
    y = xf * lax.rsqrt(jnp.mean(xf * xf, axis=-1, keepdims=True) + NORM_EPS) * g.astype(jnp.float32)
    return y.astype(x.dtype)

def t5_bucket(rel):
    n = jnp.maximum(rel, 0)
    max_exact = N_BUCKETS // 2
    large = max_exact + (jnp.log(jnp.maximum(n, 1).astype(jnp.float32) / max_exact)
                         / math.log(MAX_DISTANCE / max_exact) * (N_BUCKETS - max_exact)).astype(jnp.int32)
    large = jnp.minimum(large, N_BUCKETS - 1)
    return jnp.where(n < max_exact, n, large)

def sliding_window_sink_attention(q, k, v, rel_bias, sinks):
    B, S, _ = q.shape
    NB = S // BLOCK
    q = q.reshape(B, NB, BLOCK, N_KV_HEADS, Q_PER_KV, HEAD_DIM)

    def band(t):
        t = t.reshape(B, NB, BLOCK, N_KV_HEADS, HEAD_DIM)
        prev = jnp.concatenate([jnp.zeros_like(t[:, :1]), t[:, :-1]], axis=1)
        return jnp.concatenate([prev, t], axis=2)

    kb, vb = band(k), band(v)
    rel = (jnp.arange(BLOCK)[:, None] + BLOCK) - jnp.arange(2 * BLOCK)[None, :]
    in_window = (rel >= 0) & (rel < WINDOW)
    key_pos = (jnp.arange(NB)[:, None] - 1) * BLOCK + jnp.arange(2 * BLOCK)[None, :]
    mask = in_window[None] & (key_pos >= 0)[:, None, :]
    bias = rel_bias.astype(jnp.float32)[t5_bucket(rel)]
    bias = bias.transpose(2, 0, 1).reshape(N_KV_HEADS, Q_PER_KV, BLOCK, 2 * BLOCK)
    scores = jnp.einsum('bnqhgd,bnkhd->bnhgqk', q, kb).astype(jnp.float32) * (HEAD_DIM ** -0.5) + bias
    scores = jnp.where(mask[None, :, None, None], scores, NEG_INF)
    sink = sinks.astype(jnp.float32).reshape(N_KV_HEADS, Q_PER_KV)[:, :, None, None]
    m = jnp.maximum(scores.max(axis=-1, keepdims=True), sink)
    p = jnp.exp(scores - m)
    probs = p / (p.sum(axis=-1, keepdims=True) + jnp.exp(sink - m))
    out = jnp.einsum('bnhgqk,bnkhd->bnqhgd', probs.astype(v.dtype), vb)
    return out.reshape(B, S, D_ATTN)

def rwkv7_time_mix(p, w0, w_decay_up, a0, w_iclr_up, w_gate_up, k_k, k_a, r_k, ln_x_g, ln_x_b):
    B, S, _ = p.shape
    H, N = N_RWKV_HEADS, HEAD_DIM
    p = p.astype(jnp.float32)
    r, k, v, zw, za, zg = jnp.split(p, RWKV_SPLITS, axis=-1)
    w_log = -jax.nn.softplus(-(w0 + jnp.tanh(zw) @ w_decay_up)) - 0.5
    decay = jnp.exp(-jnp.exp(w_log))
    a = jax.nn.sigmoid(a0 + za @ w_iclr_up)
    g = jax.nn.sigmoid(zg) @ w_gate_up
    kk = (k * k_k).reshape(B, S, H, N)
    kk = kk / jnp.maximum(jnp.sqrt(jnp.sum(kk * kk, axis=-1, keepdims=True)), 1e-12)
    k = k * (1.0 + (a - 1.0) * k_a)

    def heads(t):
        return t.reshape(B, S, H, N)

    def tmaj(t):
        return t.swapaxes(0, 1)

    rh, kh, vh = heads(r), heads(k), heads(v)

    def step(state, inp):
        r_t, w_t, k_t, v_t, kk_t, a_t = inp
        sa = jnp.einsum('bhvk,bhk->bhv', state, -kk_t)
        state = (state * w_t[:, :, None, :]
                 + sa[..., None] * (kk_t * a_t)[:, :, None, :]
                 + v_t[..., None] * k_t[:, :, None, :])
        return state, jnp.einsum('bhvk,bhk->bhv', state, r_t)

    state0 = jnp.zeros((B, H, N, N), jnp.float32)
    _, o = lax.scan(step, state0, (tmaj(rh), tmaj(heads(decay)), tmaj(kh), tmaj(vh), tmaj(kk), tmaj(heads(a))))
    o = o.swapaxes(0, 1)
    mu = jnp.mean(o, axis=-1, keepdims=True)
    var = jnp.mean(jnp.square(o - mu), axis=-1, keepdims=True)
    o = ((o - mu) * lax.rsqrt(var + GN_EPS)).reshape(B, S, D_RWKV) * ln_x_g + ln_x_b
    bonus = jnp.sum(rh * kh * r_k, axis=-1, keepdims=True) * vh
    o = o + bonus.reshape(B, S, D_RWKV)
    return o * g

def conv_gated_ffn(h, w_up, conv_w, conv_b, w_down):
    S = h.shape[1]
    u = h @ w_up
    u_pad = jnp.pad(u, ((0, 0), (CONV_WIDTH - 1, 0), (0, 0)))
    u = conv_b + sum(conv_w[j] * u_pad[:, j:j + S] for j in range(CONV_WIDTH))
    gate, val = jnp.split(u, 2, axis=-1)
    return (jax.nn.gelu(gate, approximate=True) * val) @ w_down

def second_inputs(seed: int = 0) -> dict:
    key = jax.random.key(seed)
    ks = jax.random.split(key, 24)
    L = DEPTH_2
    nrm = lambda k, shape, s: jax.random.normal(k, shape, jnp.float32) * s
    return {
        "x": jax.random.normal(ks[0], (BATCH, SEQ, D_MODEL), jnp.float32),
        "norm_mix_pre": 1.0 + nrm(ks[1], (L, D_MODEL), 0.02),
        "norm_mix_post": 1.0 + nrm(ks[2], (L, D_MODEL), 0.02),
        "norm_ffn_pre": 1.0 + nrm(ks[3], (L, D_MODEL), 0.02),
        "norm_ffn_post": 1.0 + nrm(ks[4], (L, D_MODEL), 0.02),
        "w_in": nrm(ks[5], (L, D_MODEL, D_IN), D_MODEL ** -0.5),
        "rel_bias": nrm(ks[6], (N_BUCKETS, N_Q_HEADS), 0.5),
        "sinks": nrm(ks[7], (L, N_Q_HEADS), 0.5),
        "rwkv_shift_mix": jax.random.uniform(ks[8], (L, RWKV_COLS), jnp.float32),
        "w0": jax.random.uniform(ks[9], (L, D_RWKV), jnp.float32, -5.0, 0.0),
        "w_decay_up": nrm(ks[10], (L, LORA_DECAY, D_RWKV), 0.5 * LORA_DECAY ** -0.5),
        "a0": nrm(ks[11], (L, D_RWKV), 0.1),
        "w_iclr_up": nrm(ks[12], (L, LORA_ICLR, D_RWKV), 0.5 * LORA_ICLR ** -0.5),
        "w_gate_up": nrm(ks[13], (L, LORA_GATE, D_RWKV), LORA_GATE ** -0.5),
        "k_k": 0.85 + nrm(ks[14], (L, D_RWKV), 0.05),
        "k_a": 1.0 + nrm(ks[15], (L, D_RWKV), 0.05),
        "r_k": nrm(ks[16], (L, N_RWKV_HEADS, HEAD_DIM), 0.1),
        "ln_x_g": 1.0 + nrm(ks[17], (L, D_RWKV), 0.02),
        "ln_x_b": nrm(ks[18], (L, D_RWKV), 0.02),
        "w_out": nrm(ks[19], (L, D_MODEL, D_MODEL), D_MODEL ** -0.5),
        "w_ffn_up": nrm(ks[20], (L, D_MODEL, 2 * D_FF_2), D_MODEL ** -0.5),
        "conv_w": nrm(ks[21], (L, CONV_WIDTH, 2 * D_FF_2), CONV_WIDTH ** -0.5),
        "conv_b": nrm(ks[22], (L, 2 * D_FF_2), 0.02),
        "w_ffn_down": nrm(ks[23], (L, D_FF_2, D_MODEL), D_FF_2 ** -0.5),
    }

def second_block(x, norm_mix_pre, norm_mix_post, norm_ffn_pre, norm_ffn_post, w_in, rel_bias, sinks,
              rwkv_shift_mix, w0, w_decay_up, a0, w_iclr_up, w_gate_up, k_k, k_a, r_k, ln_x_g, ln_x_b,
              w_out, w_ffn_up, conv_w, conv_b, w_ffn_down):
    for l in range(DEPTH_2):
        h = rms_norm(x, norm_mix_pre[l])
        proj = h @ w_in[l]
        q, k, v, p = jnp.split(proj, (D_ATTN, D_ATTN + D_KV, D_ATTN + 2 * D_KV), axis=-1)
        attn = sliding_window_sink_attention(q, k, v, rel_bias, sinks[l])
        p_prev = jnp.concatenate([jnp.zeros_like(p[:, :1]), p[:, :-1]], axis=1)
        p = p + (p_prev - p) * rwkv_shift_mix[l]
        rw = rwkv7_time_mix(p, w0[l], w_decay_up[l], a0[l], w_iclr_up[l], w_gate_up[l],
                            k_k[l], k_a[l], r_k[l], ln_x_g[l], ln_x_b[l])
        mix = jnp.concatenate([attn, rw.astype(x.dtype)], axis=-1) @ w_out[l]
        x = x + rms_norm(mix, norm_mix_post[l])
        f = conv_gated_ffn(rms_norm(x, norm_ffn_pre[l]), w_ffn_up[l], conv_w[l], conv_b[l], w_ffn_down[l])
        x = x + rms_norm(f, norm_ffn_post[l])
    return x


def setup_inputs(seed=0):
    out = dict(first_inputs(seed))
    for name, value in second_inputs(seed + 1).items():
        if name != "x":
            out[name + "_2"] = value
    return out


def reference(
    x, c, positions, ada_w, ada_b, norm_mix_g, norm_mlp_g, pool_w, pool_scale, sgu_w_in,
    sgu_ln_g, sgu_ln_b, sgu_w_s, sgu_b_s, sgu_w_out, mla_w_dq_dkv, mla_q_norm_g, mla_kv_norm_g,
    mla_w_uq, mla_w_ukv, mla_w_o, mlp_w1, mlp_w2, final_g, norm_mix_pre_2, norm_mix_post_2,
    norm_ffn_pre_2, norm_ffn_post_2, w_in_2, rel_bias_2, sinks_2, rwkv_shift_mix_2, w0_2,
    w_decay_up_2, a0_2, w_iclr_up_2, w_gate_up_2, k_k_2, k_a_2, r_k_2, ln_x_g_2, ln_x_b_2,
    w_out_2, w_ffn_up_2, conv_w_2, conv_b_2, w_ffn_down_2,
):
    x = first_block(
        x, c, positions, ada_w, ada_b, norm_mix_g, norm_mlp_g, pool_w, pool_scale, sgu_w_in,
        sgu_ln_g, sgu_ln_b, sgu_w_s, sgu_b_s, sgu_w_out, mla_w_dq_dkv, mla_q_norm_g,
        mla_kv_norm_g, mla_w_uq, mla_w_ukv, mla_w_o, mlp_w1, mlp_w2, final_g,
    )
    return second_block(
        x, norm_mix_pre_2, norm_mix_post_2, norm_ffn_pre_2, norm_ffn_post_2, w_in_2, rel_bias_2,
        sinks_2, rwkv_shift_mix_2, w0_2, w_decay_up_2, a0_2, w_iclr_up_2, w_gate_up_2, k_k_2,
        k_a_2, r_k_2, ln_x_g_2, ln_x_b_2, w_out_2, w_ffn_up_2, conv_w_2, conv_b_2, w_ffn_down_2,
    )


_drawn_inputs = setup_inputs


def setup_inputs(seed=0):
    import zlib

    import numpy as np

    out = dict(_drawn_inputs(seed))
    spreads = {}
    factors = {'sgu_ln_g': 2.818,
     'sgu_ln_b': 8.0,
     'norm_mix_post_2': 3.461,
     'norm_ffn_pre_2': 3.413,
     'norm_ffn_post_2': 4.987,
     'sinks_2': 8.0,
     'ln_x_g_2': 4.145,
     'ln_x_b_2': 4.465,
     'conv_b_2': 3.446}
    for name, (base, spread) in spreads.items():
        noise = np.random.default_rng([zlib.crc32(name.encode()), seed]).standard_normal(out[name].shape)
        drawn = base * np.exp(spread * noise) if base else spread * noise
        out[name] = __import__('jax').numpy.asarray(drawn.astype(out[name].dtype))
    for name, factor in factors.items():
        out[name] = (out[name] * factor).astype(out[name].dtype)
    return out
```

```python
import math
from contextlib import ExitStack

import numpy as np

import concourse.bass as bass
from concourse import mybir

F32 = mybir.dt.float32
FR = mybir.dt.float32r
ACT = mybir.ActivationFunctionType
ALU = mybir.AluOpType
AX = mybir.AxisListType.X
PE, ACTE, DVE, SP = (mybir.EngineType.PE, mybir.EngineType.Activation, mybir.EngineType.DVE,
                     mybir.EngineType.SP)

P = 128
D = 1024
DT = D // P
T = 512
DFF = 4096
POOL_WINDOWS = (2, 4, 8, 16)
RMS_EPS = 1e-6
LN_EPS = 1e-5
GN_EPS = 64e-5
EXP_M_HALF = math.exp(-0.5)
MASKED = -1e30

VECS = [("c", 8), ("ada_b", 96), ("norm_mix_g", 16), ("norm_mlp_g", 16), ("pool_scale", 8),
        ("sgu_ln_g", 8), ("sgu_ln_b", 8), ("final_g", 8), ("norm_mix_pre_2", 8),
        ("norm_mix_post_2", 8), ("norm_ffn_pre_2", 8), ("norm_ffn_post_2", 8),
        ("rwkv_shift_mix_2", 14), ("w0_2", 4), ("a0_2", 4), ("k_k_2", 4), ("k_a_2", 4),
        ("r_k_2", 4), ("ln_x_g_2", 4), ("ln_x_b_2", 4), ("conv_w_2", 192), ("conv_b_2", 64)]
VEC_AT = {}
_at = 0
for _name, _rows in VECS:
    VEC_AT[_name] = _at
    _at += _rows
assert _at <= 512

CONSTS = [("ident", 128), ("head_ones", 128), ("reverse", 128), ("tril_T", 128), ("level0", 128),
          ("levels_T", 6 * 128), ("pair_masks", 256), ("chunk_start", 512), ("pool_inv", 64)]
CONST_AT = {}
_at = 0
for _name, _cols in CONSTS:
    CONST_AT[_name] = _at
    _at += _cols
CONST_COLS = _at


def constants():
    r = np.arange(P)
    row, col = r[:, None], r[None, :]
    out = np.zeros((P, CONST_COLS), np.float32)

    def put(name, a, k=0):
        out[:, CONST_AT[name] + k:CONST_AT[name] + k + a.shape[1]] = a

    same = row // 64 == col // 64
    put("ident", row == col)
    put("head_ones", same)
    put("reverse", row + col == P - 1)
    put("tril_T", row <= col)

    def lower(b):
        return (row // (2 * b) == col // (2 * b)) & (row % (2 * b) >= b) & (col % (2 * b) < b)

    put("level0", lower(1))
    for n in range(6):
        put("levels_T", lower(2 ** n).T, n * P)
    put("pair_masks", same & (row < col))
    put("pair_masks", same & (row <= col), P)
    put("chunk_start", np.broadcast_to(np.arange(T) % 64 != 0, (P, T)))
    t = np.arange(16)
    for g, w in enumerate(POOL_WINDOWS):
        put("pool_inv", np.broadcast_to((1.0 / np.minimum(t + 1.0, w)).astype(np.float32), (P, 16)), 16 * g)

    table = np.zeros((33, 384), np.float32)
    for i in range(383):
        rel = 255 - i
        if 0 <= rel < 128:
            n = np.float32(max(rel, 1))
            large = 16 + int(np.float32(np.log(n / np.float32(16))) / np.float32(math.log(8)) * np.float32(16)) \
                if rel >= 16 else 0
            table[rel if rel < 16 else min(large, 31), i] = 1
        else:
            table[32, i] = 1
    return out, table


class Counter:

    def __init__(self, nc, name):
        self.sem = nc.alloc_semaphore(name)
        self.n = 0
        self.loop = None

    def after(self, ins, by=1):
        ins.then_inc(self.sem, by)
        self.n += by
        return (self, self.n, self.loop)


class Loop:

    def __init__(self, nc, turns, per, engines):
        self.nc, self.turns, self.per, self.engines = nc, turns, per, engines

    def __enter__(self):
        self.base = {c: c.n for c in self.per}
        for c in self.per:
            c.loop = self
        self.fori = self.nc.Fori(0, self.turns, engines=self.engines)
        self.i = self.fori.__enter__()
        return self

    def __exit__(self, *e):
        self.fori.__exit__(*e)
        if e[0]:
            return
        for c, per in self.per.items():
            assert c.n == self.base[c] + per, (c.sem, c.n - self.base[c], per)
            c.n = self.base[c] + per * self.turns
            c.loop = None


def wait(eng, *marks):
    for counter, n, loop in marks:
        if loop is not None and counter.loop is loop:
            eng.wait_ge(counter.sem, loop.i * loop.per[counter] + n)
        elif loop is not None:
            eng.wait_ge(counter.sem, n + loop.per[counter] * (loop.turns - 1))
        else:
            eng.wait_ge(counter.sem, n)


def before(mark):
    counter, n, loop = mark
    return (counter, n - loop.per[counter], loop)


def program(nc, t, out, stop=None):
    pe, act, dve, pool = (Counter(nc, n) for n in ("pe_done", "act_done", "dve_done", "pool_done"))
    hi_made, lo_made, slab_used = (Counter(nc, n) for n in ("hi_made", "lo_made", "slab_used"))
    landed = [nc.alloc_semaphore(f"slab_landed{i}") for i in range(2)]
    te, se, ve, ge, sy = nc.tensor, nc.scalar, nc.vector, nc.gpsimd, nc.sync
    te.sem_inc(slab_used.sem, 1)
    slab_used.n = 1

    def sb(name, shape, dt=F32):
        return nc.sbuf_tensor(name, shape, dt)

    def alloc(name, shape, dt=F32):
        return nc.alloc_sbuf_tensor(name, shape, dt)

    xT = alloc("xT", [P, DT, T])
    raw = alloc("raw", [P, 2, 4, 512])
    w_hi = alloc("w_hi", [P, 2, 4, 512], FR)
    w_lo = alloc("w_lo", [P, 2, 4, 512], FR)
    const = alloc("const", [P, CONST_COLS])
    vec = alloc("vec", [P, 512])
    mod = alloc("mod", [P, 96])
    gain = alloc("gain", [P, 48])
    rstd = alloc("rstd", [P, T])
    tmp = alloc("tmp", [P, 2, T])
    mean_ones = alloc("mean_ones", [P, P])
    ones = alloc("ones", [P, P])
    eps = alloc("eps", [P, 3])
    bank = nc.alloc_psum_tensor("bank", [P, 8, 512], F32)

    def cst(name, k=0, n=None):
        a = CONST_AT[name] + k
        return const[:, a:a + (n or dict(CONSTS)[name])]

    def col(name, k):
        return vec[:, VEC_AT[name] + k:VEC_AT[name] + k + 1]

    ident = cst("ident")

    slabs = {"sent": 0, "split": 0, "used": 0}
    limit = {None: 999, "pool": 1, "mlp0": 33, "sgu": 45, "block1": 77, "attn": 87, "scan": 87, "mix": 87,
             "mixer": 91}[stop]

    def send(src, index=None, base=None):
        s = slabs["sent"]
        if s >= limit:
            return
        if index is None:
            if s >= 2:
                sy.wait_ge(hi_made.sem, s - 1)
                sy.wait_ge(lo_made.sem, s - 1)
        else:
            sy.wait_ge(hi_made.sem, index * 2 + (s - 1))
            sy.wait_ge(lo_made.sem, index * 2 + (s - 1))
        parts = src if isinstance(src, list) else [(slice(0, 512), src)]
        if len(parts) == 1:
            a = parts[0][1]
            parts = [(0, 2, slice(0, 512), a[:, 0:2]), (2, 4, slice(0, 512), a[:, 2:4])]
        else:
            parts = [(0, 4, c, a) for c, a in parts]
        for k0, k1, c, a in parts:
            sy.dma_start(raw[:, s % 2, k0:k1, c], a).then_inc(landed[s % 2], 16)
        slabs["sent"] += 1

    def rows(w, k, cols):
        return w[512 * k:512 * k + 512, cols].rearrange("(k p) n -> p k n", p=P)

    def send_linear(w, kslabs, groups, k0=0):
        for g in groups:
            for k in range(kslabs):
                send(rows(w, k0 + k, slice(512 * g, 512 * g + 512)))

    def send_loop(turns, source):
        s0 = slabs["sent"]
        if s0 >= limit:
            return
        if limit < s0 + 2 * turns:
            return send(source(0, 0))
        if s0 == 0:
            for k in range(2):
                send(source(k, 0))
            slabs["sent"] = 0
        with nc.Fori(1 if s0 == 0 else 0, turns, engines=[SP]) as i:
            for k in range(2):
                send(source(k, i), index=i)
        slabs["sent"] = s0 + 2 * turns

    def split_next():
        s = slabs["split"]
        slot = s % 2
        loop = hi_made.loop
        i = 0 if loop is None else loop.i
        for eng in (se, ve):
            eng.wait_ge(landed[slot], i * 32 + 32 * (s // 2 + 1))
            if s >= 1:
                eng.wait_ge(slab_used.sem, i * 2 + s)
        made = hi_made.after(se.activation(w_hi[:, slot], raw[:, slot], ACT.Copy))
        wait(ve, made)
        lo_made.after(ve.tensor_tensor(w_lo[:, slot], raw[:, slot], w_hi[:, slot].bitcast(F32), ALU.subtract))
        slabs["split"] += 1

    TOTAL_SLABS = 2 * 32 + 8 + 4 + 10 + 4 + 32 + 16

    def slab_products(moving, banks, free, ready, first, last, weights_stationary=True):
        s = slabs["used"]
        slot = s % 2
        loop = slab_used.loop
        i = 0 if loop is None else loop.i
        te.wait_ge(hi_made.sem, i * 2 + (s + 1))
        te.wait_ge(lo_made.sem, i * 2 + (s + 1))
        hi, lo = moving
        full = []
        for n in range(4):
            if first:
                wait(te, *free[n])
            tile = slice(P * n, P * n + P)
            for k in range(4):
                if n == 0 and ready is not None:
                    wait(te, *ready[k])
                if weights_stationary:
                    three = ((w_hi[:, slot, k, tile], hi[:, k]), (w_hi[:, slot, k, tile], lo[:, k]),
                             (w_lo[:, slot, k, tile], hi[:, k]))
                else:
                    three = ((hi[:, k, tile], w_hi[:, slot, k]), (hi[:, k, tile], w_lo[:, slot, k]),
                             (lo[:, k, tile], w_hi[:, slot, k]))
                for j, (a, b) in enumerate(three):
                    mm = te.matmul(bank[:, banks[n]], a, b, start=first and k == 0 and j == 0,
                                   stop=last and k == 3 and j == 2)
            if last and n < 3:
                full.append(pe.after(mm))
        full.append(slab_used.after(mm))
        slabs["used"] += 1
        return full

    def step(*args, **kw):
        if slabs["split"] < TOTAL_SLABS:
            split_next()
        return slab_products(*args, **kw)

    def slab_loop(turns, per):
        per = {**per, hi_made: 2, lo_made: 2, slab_used: 2}
        return Loop(nc, turns, per, [PE, ACTE, DVE])

    def end_loop(turns):
        for k in ("split", "used"):
            slabs[k] += 2 * (turns - 1)

    def all_slabs():
        for layer in range(2):
            if layer == 1:
                send_linear(t["sgu_w_in"], 2, range(4))
                send_linear(t["sgu_w_out"], 2, range(2))
            for half in range(2):
                w1, w2 = t["mlp_w1"][layer], t["mlp_w2"][layer]
                send_loop(4, lambda k, i: w1[512 * k:512 * k + 512, bass.ds(i * 512 + 2048 * half, 512)]
                          .rearrange("(k p) n -> p k n", p=P))
                send_linear(w2, 4, range(2), k0=4 * half)
        send_linear(t["w_in_2"], 2, range(5))
        send_linear(t["w_out_2"], 2, range(2))
        for half in range(2):
            w = t["w_ffn_up_2"]
            send_loop(8, lambda k, i: [
                (slice(256 * v, 256 * v + 256),
                 w[512 * k:512 * k + 512, bass.ds(i * 256 + (2048 * half + DFF * v), 256)]
                 .rearrange("(k p) n -> p k n", p=P)) for v in range(2)])
            send_linear(t["w_ffn_down_2"], 4, range(2), k0=4 * half)
        assert stop or slabs["sent"] == TOTAL_SLABS

    def act_(*a, **k):
        return act.after(se.activation(*a, **k))

    def tt(o, a, b, op):
        return dve.after(ve.tensor_tensor(o, a, b, op))

    def ts(o, a, s1, s2, op0, op1=None):
        return dve.after(ve.tensor_scalar(o, a, s1, s2, op0, op1) if op1 else ve.tensor_scalar(o, a, s1, None, op0))

    def stt(o, a, s, b, op0, op1):
        return dve.after(ve.scalar_tensor_tensor(out=o, in0=a, scalar=s, in1=b, op0=op0, op1=op1))

    def rms(src, ready, sq, sumbank, free):
        squares = []
        for k in range(DT):
            wait(se, *ready[k])
            squares.append(act_(sq[:, k], src[:, k], ACT.Square))
        wait(te, *free)
        for k in range(DT):
            wait(te, squares[k])
            mm = te.matmul(bank[:, sumbank], mean_ones[:, :], sq[:, k], start=k == 0, stop=k == DT - 1)
        summed = pe.after(mm)
        wait(se, summed)
        root = act_(rstd[:, :], bank[:, sumbank], ACT.Sqrt, bias=eps[:, 0:1])
        wait(ve, root)
        return dve.after(ve.reciprocal(rstd[:, :], rstd[:, :]))

    def normalise(src, inv, g, shift, hi, lo, tiles=DT, free=()):
        done, used = [], [None, None]
        wait(se, *free)
        wait(ve, *free)
        for k in range(tiles):
            wait(ve, inv)
            if used[k % 2]:
                wait(ve, *used[k % 2])
            scaled = stt(tmp[:, k % 2], src[:, k], g(k), rstd[:, :], ALU.mult, ALU.mult)
            wait(se, scaled)
            wait(ve, scaled)
            if shift:
                made = act_(hi[:, k], tmp[:, k % 2], ACT.Identity, bias=shift(k))
                wait(ve, made)
                rest = stt(lo[:, k], tmp[:, k % 2], shift(k), hi[:, k].bitcast(F32), ALU.add, ALU.subtract)
            else:
                made = act_(hi[:, k], tmp[:, k % 2], ACT.Copy)
                wait(ve, made)
                rest = tt(lo[:, k], tmp[:, k % 2], hi[:, k].bitcast(F32), ALU.subtract)
            used[k % 2] = (made, rest)
            done.append((made, rest))
        return done

    def split_into(hi, lo, src, ready):
        wait(se, *ready)
        made = act_(hi, src, ACT.Copy)
        wait(ve, made, *ready)
        return (made, tt(lo, src, hi.bitcast(F32), ALU.subtract))

    def dump(ap, marks):
        s = nc.alloc_semaphore("dumped")
        wait(se, *marks)
        n = P * ap.shape[1] * ap.shape[2]
        se.dma_start(out.rearrange("a t f -> (a t f)")[0:n].rearrange("(p k t) -> p k t", p=P, k=ap.shape[1]), ap).then_inc(s, 16)
        se.wait_ge(s, 16)

    nobody = ()

    all_slabs_emitted = all_slabs()

    const_in, x_in, vec_in = (nc.alloc_semaphore(n) for n in ("const_in", "x_in", "vec_in"))
    with sb("x_rows", [P, 4, D]) as x_rows, sb("vec_rows", [P, 4, P]) as vec_rows, \
            sb("ada_ring", [P, 3, 8, 512]) as ada_ring, sb("c_act", [P, DT]) as c_act:
        se.dma_start(const[:, :], t["const"]).then_inc(const_in, 16)
        se.dma_start(vec_rows[:, :, :], t["vecs"].rearrange("(j p) n -> p j n", p=P)).then_inc(vec_in, 16)
        se.dma_start(x_rows[:, :, :], t["x"][0].rearrange("(j p) n -> p j n", p=P)).then_inc(x_in, 16)
        ve.memset(mean_ones[:, :], 1.0 / D)
        ve.memset(eps[:, 0:1], RMS_EPS)
        ve.memset(eps[:, 1:2], LN_EPS)
        ve.memset(eps[:, 2:3], GN_EPS)
        set_up = dve.after(ve.memset(ones[:, :], 1.0))
        te.wait_ge(const_in, 16)
        te.wait_ge(vec_in, 16)
        for j in range(4):
            mm = te.transpose(bank[:, 7, P * j:P * j + P], vec_rows[:, j], ident)
        turned = pe.after(mm)
        wait(ve, turned)
        vec_ready = dve.after(ve.tensor_copy(vec[:, :], bank[:, 7]))
        wait(se, vec_ready, set_up)
        silu = act_(c_act[:, :], vec[:, VEC_AT["c"]:VEC_AT["c"] + 8], ACT.Silu)
        te.wait_ge(x_in, 16)
        x_ready = []
        copied = [None, None]
        for k in range(DT):
            if copied[k % 2]:
                wait(te, copied[k % 2])
            for j in range(4):
                mm = te.transpose(bank[:, 4 + k % 2, P * j:P * j + P], x_rows[:, j, P * k:P * k + P], ident)
            turned = pe.after(mm)
            wait(ve, turned)
            copied[k % 2] = dve.after(ve.tensor_copy(xT[:, k], bank[:, 4 + k % 2]))
            x_ready.append((copied[k % 2],))
        ada_landed = [nc.alloc_semaphore(f"ada_landed{i}") for i in range(3)]
        ada_used = Counter(nc, "ada_used")
        wait(te, silu)
        for g in range(24):
            layer, n = divmod(g, 12)
            if g >= 3:
                ge.wait_ge(ada_used.sem, g - 2)
            ge.dma_start(ada_ring[:, g % 3], t["ada_w"][layer, :, 512 * n:512 * n + 512]
                         .rearrange("(k p) n -> p k n", p=P)).then_inc(ada_landed[g % 3], 16)
        for g in range(24):
            te.wait_ge(ada_landed[g % 3], 16 * (g // 3 + 1))
            for c in range(4):
                for k in range(DT):
                    mm = te.matmul(bank[:, 6, 4 * g + c:4 * g + c + 1], ada_ring[:, g % 3, k, P * c:P * c + P],
                                   c_act[:, k:k + 1], start=k == 0, stop=k == DT - 1)
            ada_mark = ada_used.after(mm)
        wait(ve, ada_mark, vec_ready)
        mod_ready = tt(mod[:, :], bank[:, 6, 0:96], vec[:, VEC_AT["ada_b"]:VEC_AT["ada_b"] + 96], ALU.add)
        wait(ve, mod_ready)

        for layer in range(2):
            m, g = 48 * layer, 16 * layer
            stt(gain[:, g:g + 8], mod[:, m + 8:m + 16], 1.0,
                vec[:, VEC_AT["norm_mix_g"] + 8 * layer:VEC_AT["norm_mix_g"] + 8 * layer + 8], ALU.add, ALU.mult)
            stt(gain[:, g + 8:g + 16], mod[:, m + 32:m + 40], 1.0,
                vec[:, VEC_AT["norm_mlp_g"] + 8 * layer:VEC_AT["norm_mlp_g"] + 8 * layer + 8], ALU.add, ALU.mult)
        gains = tt(gain[:, 32:40], mod[:, 16:24], vec[:, VEC_AT["pool_scale"]:VEC_AT["pool_scale"] + 8], ALU.mult)
        wait(ve, gains)
        wait(se, gains)

    def modv(layer, part, k):
        a = 48 * layer + 8 * part + k
        return mod[:, a:a + 1]

    def mlp(layer, x_ready, h_hi, h_lo, u_hi, u_lo, r):
        inv = rms(xT, x_ready, r["sq"], 4, r["bank4"])
        ready = normalise(xT, inv, lambda k: gain[:, 16 * layer + 8 + k:16 * layer + 9 + k],
                          lambda k: modv(layer, 3, k), h_hi, h_lo)
        free = [r["free"]] * 4
        down_done = ()
        for half in range(2):
            per = {pe: 3, act: 8, dve: 8}
            with slab_loop(4, per) as loop:
                split_next()
                base, dbase = act.n, dve.n
                earlier = [(act, base + 2 * n + 1 - 8, loop) for n in range(4)]
                slab_products((h_hi[:, 0:4], h_lo[:, 0:4]), range(4), [[earlier[n], *free[n]] for n in range(4)],
                              ready[0:4], True, False)
                split_next()
                full = slab_products((h_hi[:, 4:8], h_lo[:, 4:8]), range(4), None, ready[4:8], False, True)
                squared, hi_done = [None] * 4, [None] * 4
                for n in range(4):
                    wait(se, full[n])
                    wait(se, (dve, dbase + 2 * n - 3, loop))
                    relu = act_(tmp[:, n % 2], bank[:, n], ACT.Relu)
                    wait(ve, relu)
                    squared = tt(r["sq"][:, n], tmp[:, n % 2], tmp[:, n % 2], ALU.mult)
                    wait(se, squared)
                    tile = bass.ds(loop.i * 4 + n, 1)
                    made = act_(u_hi[:, tile, :], r["sq"][:, n:n + 1], ACT.Copy)
                    wait(ve, made)
                    lo_done = tt(u_lo[:, tile, :], r["sq"][:, n:n + 1], u_hi[:, tile, :].bitcast(F32), ALU.subtract)
            end_loop(4)
            free = [[relu]] * 4
            new = []
            for g in range(2):
                for k in range(4):
                    full = step((u_hi[:, 4 * k:4 * k + 4], u_lo[:, 4 * k:4 * k + 4]), range(4), free,
                                [[made, lo_done]] * 4 if g == 0 else None, k == 0, k == 3)
                for n in range(4):
                    o = 4 * g + n
                    wait(ve, full[n])
                    new.append((stt(xT[:, o], bank[:, n], modv(layer, 5, o), xT[:, o], ALU.mult, ALU.add),))
                free = [[new[-4 + n][0]] for n in range(4)]
        return new

    split_next()
    with sb("h_hi", [P, DT, T], FR) as h_hi, sb("h_lo", [P, DT, T], FR) as h_lo:
        with sb("h", [P, DT, T]) as h, sb("sums", [P, 2, 2, 16 + T]) as sums, sb("pooled", [P, DT, T]) as pooled, \
                sb("pool_w", [P, 4, 2, 256]) as pool_w, sb("sq_a", [P, DT, T]) as sq:
            pool_w_in = nc.alloc_semaphore("pool_w_in")
            wait(ge, gains)
            ge.dma_start(pool_w[:, :, :, :], t["pool_w"][0].rearrange("g (k p) n -> p (g k) n", p=P)
                         .rearrange("p (g k) n -> p g k n", g=4)).then_inc(pool_w_in, 16)
            inv = rms(xT, x_ready, sq, 4, nobody)
            wait(ve, inv)
            made = []
            for k in range(DT):
                scaled = stt(tmp[:, k % 2], xT[:, k], gain[:, k:k + 1], rstd[:, :], ALU.mult, ALU.mult)
                wait(ve, scaled)
                made.append(ts(h[:, k], tmp[:, k % 2], modv(0, 0, k), None, ALU.add))
            zeroed = dve.after(ve.memset(sums[:, :, :, 0:16], 0.0))
            wait(ve, zeroed)
            pooled_ready = []
            for g, window in enumerate(POOL_WINDOWS):
                hg = h[:, 2 * g:2 * g + 2]
                wait(ve, made[2 * g + 1])
                last = dve.after(ve.tensor_copy(sums[:, 0, :, 16:], hg))
                a, w = 0, 1
                while w < window:
                    wait(ve, last)
                    last = tt(sums[:, 1 - a, :, 16:], sums[:, a, :, 16:], sums[:, a, :, 16 - w:16 + T - w], ALU.add)
                    a, w = 1 - a, 2 * w
                wait(ve, last)
                mean = stt(pooled[:, 2 * g:2 * g + 2], sums[:, a, :, 16:], 1.0 / window, hg, ALU.mult, ALU.subtract)
                inv_count = cst("pool_inv", 16 * g, 16).unsqueeze(1).broadcast_to([P, 2, 16])
                head = tt(tmp[:, :, 0:16], sums[:, a, :, 16:32], inv_count, ALU.mult)
                wait(ve, mean, head)
                pooled_ready.append(tt(pooled[:, 2 * g:2 * g + 2, 0:16], tmp[:, :, 0:16], hg[:, :, 0:16], ALU.subtract))
            te.wait_ge(pool_w_in, 16)
            x_ready = []
            for o in range(DT):
                g, n = divmod(o, 2)
                wait(te, pooled_ready[g])
                if o >= 2:
                    wait(te, x_ready[o - 2][0])
                for k in range(2):
                    mm = te.matmul(bank[:, 5 + n], pool_w[:, g, k, P * n:P * n + P], pooled[:, 2 * g + k],
                                   start=k == 0, stop=k == 1)
                full = pe.after(mm)
                wait(ve, full)
                x_ready.append((stt(xT[:, o], bank[:, 5 + n], gain[:, 32 + o:33 + o], xT[:, o], ALU.mult, ALU.add),))
        if stop == "pool":
            return dump(xT[:, :, :], [m[0] for m in x_ready])

        with sb("u_hi", [P, 16, T], FR) as u_hi, sb("u_lo", [P, 16, T], FR) as u_lo, sb("sq_b", [P, DT, T]) as sq:
            x_ready = mlp(0, x_ready, h_hi, h_lo, u_hi, u_lo, {"sq": sq, "bank4": nobody, "free": nobody})
        if stop == "mlp0":
            return dump(xT[:, :, :], [m[0] for m in x_ready])

        with sb("u", [P, DT, T]) as u, sb("v", [P, 4, D]) as v, \
                sb("g_hi", [P, DT, T], FR) as g_hi, sb("g_lo", [P, DT, T], FR) as g_lo, \
                sb("ws", [P, DT, P]) as ws, sb("wsT", [P, DT, P]) as wsT, sb("bs_row", [1, D]) as bs_row, \
                sb("bs", [P, D]) as bs, sb("stats", [P, 4, 2, 6]) as stats, sb("mv", [P, 4, 2]) as mv:
            ws_in = nc.alloc_semaphore("ws_in")
            for mark in x_ready:
                wait(ge, *mark)
            ge.dma_start(ws[:, :, :], t["sgu_w_s"][0].rearrange("h t s -> t h s")).then_inc(ws_in, 16)
            ge.dma_start(bs_row[:, :], t["sgu_b_s"]).then_inc(ws_in, 16)
            inv = rms(xT, x_ready, u, 4, nobody)
            ready = normalise(xT, inv, lambda k: gain[:, 16 + k:17 + k], lambda k: modv(1, 0, k), h_hi, h_lo)
            free = [[m[0]] for m in x_ready[4:8]]
            for g in range(2):
                step((h_hi[:, 0:4], h_lo[:, 0:4]), range(4), free, ready[0:4] if g == 0 else None, True, False)
                full = step((h_hi[:, 4:8], h_lo[:, 4:8]), range(4), free, ready[4:8] if g == 0 else None, False, True)
                free = []
                for n in range(4):
                    wait(se, full[n])
                    free.append([act_(u[:, 4 * g + n], bank[:, n], ACT.Gelu)])
            u_ready = free[3]
            for g in range(2):
                step((h_hi[:, 0:4], h_lo[:, 0:4]), range(4), free, None, True, False, weights_stationary=False)
                full = step((h_hi[:, 4:8], h_lo[:, 4:8]), range(4), free, None, False, True, weights_stationary=False)
                free = []
                for n in range(4):
                    wait(se, full[n])
                    free.append([act_(v[:, n, 512 * g:512 * g + 512], bank[:, n], ACT.Gelu)])
            te.wait_ge(ws_in, 32)
            for hh in range(DT):
                mm = te.transpose(bank[:, 4 + hh // 4, P * (hh % 4):P * (hh % 4) + P], ws[:, hh], ident)
            turned = pe.after(mm)
            wait(ve, turned)
            masked = tt(wsT[:, :, :], bank[:, 4:6].rearrange("p b (h t) -> p (b h) t", h=4),
                        cst("tril_T").unsqueeze(1).broadcast_to([P, DT, P]), ALU.mult)
            for q in range(2):
                mm = te.matmul(bank[:, 6 + q], ones[0:1, :], bs_row[0:1, 512 * q:512 * q + 512], start=True, stop=True)
            spread = pe.after(mm)
            wait(se, spread)
            bs_ready = act_(bs[:, :], bank[:, 6:8].rearrange("p b n -> p (b n)"), ACT.Copy)
            wait(te, masked, bs_ready)
            for q in range(2):
                mm = te.matmul(bank[:, 6 + q], ones[:, :], wsT[:, 4 * q:4 * q + 4].rearrange("p h t -> p (h t)"),
                               start=True, stop=True)
            summed = pe.after(mm)
            wait(ve, summed, bs_ready)
            for hh in range(DT):
                part = slice(P * hh, P * hh + P)
                qs_ready = stt(bs[:, part], bank[:, 6 + hh // 4, P * (hh % 4):P * (hh % 4) + P],
                               col("sgu_ln_b", hh), bs[:, part], ALU.mult, ALU.add)
            v_ready = []
            for n in range(4):
                wait(ve, free[n][0])
                for q in range(2):
                    st = dve.after(ve.bn_stats(stats[:, n, q], v[:, n, 512 * q:512 * q + 512]))
                wait(ve, st)
                ag = dve.after(ve.bn_aggr(mv[:, n], stats[:, n]))
                wait(se, ag)
                root = act_(mv[:, n, 1:2], mv[:, n, 1:2], ACT.Sqrt, bias=eps[:, 1:2])
                wait(ve, root, ag)
                rec = dve.after(ve.reciprocal(mv[:, n, 1:2], mv[:, n, 1:2]))
                wait(ve, rec)
                v_ready.append(ts(v[:, n], v[:, n], mv[:, n, 0:1], mv[:, n, 1:2], ALU.subtract, ALU.mult))
            wait(te, masked, *v_ready)
            wait(ve, qs_ready, *u_ready)
            gated, mix_free = [], [(), ()]
            for hh in range(DT):
                b = 4 + hh % 2
                wait(te, *mix_free[hh % 2])
                for n in range(4):
                    mm = te.matmul(bank[:, b, P * n:P * n + P], v[:, n, P * hh:P * hh + P], wsT[:, hh],
                                   start=True, stop=True)
                full_mix = pe.after(mm)
                wait(ve, full_mix)
                mixed = stt(tmp[:, hh % 2].rearrange("p (n t) -> p n t", n=4), bank[:, b].rearrange("p (n t) -> p n t", n=4),
                            col("sgu_ln_g", hh),
                            bs[:, P * hh:P * hh + P].unsqueeze(1).broadcast_to([P, 4, P]), ALU.mult, ALU.add)
                mix_free[hh % 2] = (mixed,)
                wait(ve, mixed)
                prod = tt(u[:, hh], u[:, hh], tmp[:, hh % 2], ALU.mult)
                gated.append(split_into(g_hi[:, hh], g_lo[:, hh], u[:, hh], [prod]))
            x_ready = []
            for g in range(2):
                step((g_hi[:, 0:4], g_lo[:, 0:4]), range(4), free, gated[0:4] if g == 0 else None, True, False)
                full = step((g_hi[:, 4:8], g_lo[:, 4:8]), range(4), free, gated[4:8] if g == 0 else None, False, True)
                free = []
                for n in range(4):
                    o = 4 * g + n
                    wait(ve, full[n])
                    m = stt(xT[:, o], bank[:, n], modv(1, 2, o), xT[:, o], ALU.mult, ALU.add)
                    x_ready.append((m,))
                    free.append([m])
        if stop == "sgu":
            return dump(xT[:, :, :], [m[0] for m in x_ready])
        with sb("u2_hi", [P, 16, T], FR) as u_hi, sb("u2_lo", [P, 16, T], FR) as u_lo, sb("sq_d", [P, DT, T]) as sq:
            x_ready = mlp(1, x_ready, h_hi, h_lo, u_hi, u_lo,
                          {"sq": sq, "bank4": (mixed,), "free": (x_ready[-1][0],)})
            inv = rms(xT, x_ready, sq, 4, nobody)
            wait(ve, inv)
            x_ready = [(stt(xT[:, k], xT[:, k], col("final_g", k), rstd[:, :], ALU.mult, ALU.mult),) for k in range(DT)]
            if stop == "block1":
                return dump(xT[:, :, :], [m[0] for m in x_ready])
            inv = rms(xT, x_ready, sq, 4, nobody)
            wait(ve, inv)
            ready = normalise(xT, inv, lambda k: col("norm_mix_pre_2", k), None, h_hi, h_lo)
            free = [[x_ready[-1][0]]] * 4

        mixer = ExitStack()

        def ms(name, shape, dt=F32):
            return mixer.enter_context(nc.sbuf_tensor(name, shape, dt, side="right"))

        ar = ms("ar", [P, 4, 2, T])
        rT = ar[:, :, 1]
        kkT = ms("kkT", [P, 4, T])
        vvT = ms("vvT", [P, 4, T])
        attnT = ms("attnT", [P, 4, T])
        bT = ms("bT", [P, 4, T])
        gT = ms("gT", [P, 4, T])
        bonus = ms("bonus", [P, 4, T])
        pc = ms("pc", [P, 4, 8])
        one_less = ms("one_less", [P, 18])
        z_stack, q_stack = ExitStack(), ExitStack()
        zT = z_stack.enter_context(nc.sbuf_tensor("zT", [P, 2, T], F32, side="right"))
        qT = q_stack.enter_context(nc.sbuf_tensor("qT", [P, 4, T], F32, side="right"))
        kT = q_stack.enter_context(nc.sbuf_tensor("kT", [P, T], F32, side="right"))
        vT = q_stack.enter_context(nc.sbuf_tensor("vT", [P, T], F32, side="right"))
        made = ts(one_less[:, 0:14], vec[:, VEC_AT["rwkv_shift_mix_2"]:VEC_AT["rwkv_shift_mix_2"] + 14],
                  -1.0, 1.0, ALU.mult, ALU.add)
        made = ts(one_less[:, 14:18], vec[:, VEC_AT["k_a_2"]:VEC_AT["k_a_2"] + 4], -1.0, 1.0, ALU.mult, ALU.add)
        wait(se, made)
        dest = [qT[:, i] for i in range(4)] + [kT[:, :], vT[:, :]] + [rT[:, i] for i in range(4)] + \
               [kkT[:, i] for i in range(4)] + [vvT[:, i] for i in range(4)] + [zT[:, i] for i in range(2)]
        proj = []
        for g in range(5):
            step((h_hi[:, 0:4], h_lo[:, 0:4]), range(4), free, ready[0:4] if g == 0 else None, True, False)
            full = step((h_hi[:, 4:8], h_lo[:, 4:8]), range(4), free, ready[4:8] if g == 0 else None, False, True)
            free = []
            for n in range(4):
                o = 4 * g + n
                wait(se, full[n])
                if o < 6:
                    proj.append(act_(dest[o], bank[:, n], ACT.Copy, scale=0.125 if o < 4 else 1.0))
                    free.append([proj[-1]])
                    continue
                here = act_(dest[o], bank[:, n], ACT.Copy, scale=one_less[:, o - 6:o - 5])
                wait(ve, here)
                proj.append(stt(dest[o][:, 1:], bank[:, n, 0:T - 1], col("rwkv_shift_mix_2", o - 6),
                                dest[o][:, 1:], ALU.mult, ALU.add))
                free.append([proj[-1]])
        bank_free = [free[n] for n in range(4)] + [[x_ready[-1][0]]] * 4
        proj_done = [proj[5], proj[-1]]
    if True:
        with sb("bias", [P, 8, 256]) as bias, sb("bias_rev", [P, 8, 256]) as bias_rev, sb("rel", [33, 8]) as rel, \
                sb("buckets", [33, 384]) as buckets, sb("table", [8, 384]) as table, sb("sink", [P, 8]) as sink, \
                sb("v_rows", [P, 4, P]) as v_rows, sb("scores", [P, 2, 4, 256]) as scores, \
                sb("p_t", [P, 2, 2, 512]) as p_t, sb("small", [P, 2, 5, 4]) as small:
            rel_in, table_out, bias_in = (nc.alloc_semaphore(n) for n in ("rel_in", "table_out", "bias_in"))
            wait(ge, *proj_done)
            wait(ve, *proj_done)
            outside = dve.after(ve.memset(rel[32:33, :], MASKED))
            ge.dma_start(rel[0:32, :], t["rel_bias_2"]).then_inc(rel_in, 16)
            ge.dma_start(buckets[:, :], t["buckets"]).then_inc(rel_in, 16)
            ge.dma_start(sink[:, :], t["sinks_2"].broadcast_to([P, 8])).then_inc(rel_in, 16)
            te.wait_ge(rel_in, 48)
            wait(te, outside, *bank_free[4])
            looked_up = pe.after(te.matmul(bank[0:8, 4, 0:384], rel[:, :], buckets[:, :], start=True, stop=True))
            wait(ve, looked_up)
            made = dve.after(ve.tensor_copy(table[:, :], bank[0:8, 4, 0:384]))
            wait(ge, made)
            ge.dma_start(t["scratch"], table[:, :]).then_inc(table_out, 16)
            ge.wait_ge(table_out, 16)
            ge.dma_start(bias_rev[:, :, :], bass.AP(tensor=t["scratch"].tensor, offset=0, ap=[[1, P], [384, 8], [1, 256]])).then_inc(bias_in, 16)
            te.wait_ge(bias_in, 16)
            wait(te, made, *bank_free[5], *bank_free[6], *bank_free[7])
            for q in range(4):
                mm = te.matmul(bank[:, 4 + q], cst("reverse"), bias_rev[:, 2 * q:2 * q + 2].rearrange("p h j -> p (h j)"),
                               start=True, stop=True)
            turned = pe.after(mm)
            wait(ve, turned)
            bias_ready = dve.after(ve.tensor_copy(bias[:, :, :].rearrange("p (b h) j -> p b (h j)", b=4), bank[:, 4:8]))
            wait(te, bias_ready, proj[5])
            for n in range(4):
                mm = te.transpose(bank[:, 4, P * n:P * n + P], vT[:, P * n:P * n + P], ident)
            turned = pe.after(mm)
            wait(ve, turned, bias_ready)
            v_ready = dve.after(ve.tensor_copy(v_rows[:, :, :], bank[:, 4].rearrange("p (n d) -> p n d", n=4)))
            wait(te, v_ready, *[m for b in range(4) for m in bank_free[b]])
            ve.wait_ge(rel_in, 48)
            score_free = [(), ()]
            pt_free = (v_ready,)
            out_free = [(), ()]
            p_used = [(), ()]
            ptT_used = [(), ()]
            for n in range(4):
                j0 = 128 if n == 0 else 0
                for half in range(2):
                    r0, b = 64 * half, 2 * half
                    wait(te, *score_free[half])
                    for i in range(4):
                        mm = te.matmul(bank[:, b + i // 2, 256 * (i % 2) + j0:256 * (i % 2) + 256],
                                       qT[r0:r0 + 64, i, P * n:P * n + P],
                                       kT[r0:r0 + 64, P * n - P + j0:P * n + P], start=True, stop=True)
                    scored = pe.after(mm)
                    s = scores[:, half, :, j0:]
                    sm = small[:, half]
                    wait(ve, scored, *p_used[half])
                    biased = tt(s, bank[:, b:b + 2].rearrange("p b (i j) -> p (b i) j", i=2)[:, :, j0:],
                                bias[:, 4 * half:4 * half + 4, j0:], ALU.add)
                    score_free[half] = (biased,)
                    wait(ve, biased)
                    top = dve.after(ve.tensor_reduce(sm[:, 0], s, AX, ALU.max))
                    wait(ve, top)
                    top = tt(sm[:, 0], sm[:, 0], sink[:, 4 * half:4 * half + 4], ALU.max)
                    wait(ve, top)
                    tt(sm[:, 2], sink[:, 4 * half:4 * half + 4], sm[:, 0], ALU.subtract)
                    neg = ts(sm[:, 1], sm[:, 0], -1.0, None, ALU.mult)
                    wait(se, neg)
                    for i in range(4):
                        act_(scores[:, half, i, j0:], scores[:, half, i, j0:], ACT.Exp, bias=sm[:, 1, i:i + 1],
                             accum_out=sm[:, 3, i:i + 1])
                    e = act_(sm[:, 4], sm[:, 2], ACT.Exp)
                    wait(ve, e)
                    den = tt(sm[:, 3], sm[:, 3], sm[:, 4], ALU.add)
                    wait(ve, den)
                    rec = dve.after(ve.reciprocal(sm[:, 3], sm[:, 3]))
                    wait(ve, rec)
                    probs = tt(s, s, sm[:, 3].unsqueeze(2).broadcast_to([P, 4, 256 - j0]), ALU.mult)
                    wait(te, probs, *pt_free)
                    for kk in range(j0 // 128, 2):
                        for i in range(4):
                            mm = te.transpose(bank[:, 4 + kk, P * i:P * i + P], scores[:, half, i, P * kk:P * kk + P], ident)
                    turned = pe.after(mm)
                    p_used[half] = (turned,)
                    wait(se, turned, *ptT_used[half])
                    copied = act_(p_t[:, half, j0 // 128:2], bank[:, 4 + j0 // 128:6], ACT.Copy)
                    pt_free = (copied,)
                    wait(te, copied, *out_free[half])
                    for kk in range(j0 // 128, 2):
                        mm = te.matmul(bank[r0:r0 + 64, 6 + half], v_rows[:, n - 1 + kk, r0:r0 + 64], p_t[:, half, kk],
                                       start=kk == j0 // 128, stop=kk == 1)
                    summed = pe.after(mm)
                    ptT_used[half] = (summed,)
                    wait(ve, summed)
                    got = dve.after(ve.tensor_copy(attnT[r0:r0 + 64, :, P * n:P * n + P],
                                                   bank[r0:r0 + 64, 6 + half].rearrange("p (i t) -> p i t", i=4)))
                    out_free[half] = (got,)
        attn_ready = [out_free[0][0], out_free[1][0]]
        if stop == "attn":
            return dump(attnT[:, :, :], attn_ready)
        idle = [*attn_ready, *score_free[0], *score_free[1], *pt_free]
        wait(te, *idle)

        q_stack.close()
        with sb("lora", [P, 2, 512]) as lora, sb("logd", [P, 4, T]) as logd, sb("aT", [P, 4, T]) as aT, \
                sb("cum", [P, 4, T]) as cum, sb("inverse", [P, 4, T]) as inverse, sb("sc", [P, 4, T]) as sc:
            lora_in = nc.alloc_semaphore("lora_in")
            wait(ge, *idle, *proj_done)
            ge.dma_start(lora[0:64, 0], t["w_decay_up_2"]).then_inc(lora_in, 16)
            ge.dma_start(lora[64:128, 0], t["w_iclr_up_2"]).then_inc(lora_in, 16)
            ge.dma_start(lora[:, 1], t["w_gate_up_2"]).then_inc(lora_in, 16)
            wait(se, *proj_done, *idle)
            wait(ve, *idle)
            z1 = act_(zT[0:64, 0], zT[0:64, 0], ACT.Tanh)
            z2 = act_(zT[:, 1], zT[:, 1], ACT.Sigmoid)
            te.wait_ge(lora_in, 48)
            wait(te, z1, z2)
            for i in range(4):
                mm = te.matmul(bank[:, i], lora[0:64, 0, P * i:P * i + P], zT[0:64, 0], start=True, stop=True)
            decays = pe.after(mm)
            for i in range(4):
                mm = te.matmul(bank[:, 4 + i], lora[64:128, 0, P * i:P * i + P], zT[64:128, 0], start=True, stop=True)
            rates = pe.after(mm)
            wait(se, decays)
            for i in range(4):
                d = act_(logd[:, i], bank[:, i], ACT.Sigmoid, bias=col("w0_2", i))
            wait(te, d)
            for i in range(4):
                mm = te.matmul(bank[:, i], lora[:, 1, P * i:P * i + P], zT[:, 1], start=True, stop=True)
            gates = pe.after(mm)
            wait(se, rates)
            for i in range(4):
                a_ready = act_(aT[:, i], bank[:, 4 + i], ACT.Sigmoid, bias=col("a0_2", i))
            wait(se, gates)
            g_ready = act_(gT[:, :, :], bank[:, 0:4], ACT.Copy)
            wait(ve, d)
            neg = ts(logd[:, :, :], logd[:, :, :], -EXP_M_HALF, None, ALU.mult)
            wait(ve, neg)
            for i in range(4):
                c = dve.after(ve.tensor_tensor_scan(cum[:, i], cst("chunk_start"), logd[:, i], 0.0, ALU.mult, ALU.add))
            kk = ar[:, :, 0]
            for i in range(4):
                k0 = ts(kk[:, i], kkT[:, i], col("k_k_2", i), None, ALU.mult)
            wait(se, k0)
            s2 = act_(sc[:, :, :], kk, ACT.Square)
            wait(te, s2, a_ready)
            for i in range(4):
                mm = te.matmul(bank[:, 4 + i], cst("head_ones"), sc[:, i], start=True, stop=True)
            norms = pe.after(mm)
            wait(se, norms)
            root = act_(inverse[:, :, :], bank[:, 4:8], ACT.Sqrt)
            wait(ve, root)
            m = ts(inverse[:, :, :], inverse[:, :, :], 1e-12, None, ALU.max)
            wait(ve, m)
            m = dve.after(ve.reciprocal(inverse[:, :, :], inverse[:, :, :]))
            wait(ve, m)
            m = tt(kk, kk, inverse[:, :, :], ALU.mult)
            wait(ve, a_ready, m)
            for i in range(4):
                m1 = ts(sc[:, i], aT[:, i], col("k_a_2", i), one_less[:, 14 + i:15 + i], ALU.mult, ALU.add)
            wait(ve, m1)
            knew = tt(kkT[:, :, :], kkT[:, :, :], sc[:, :, :], ALU.mult)
            m2 = tt(bT[:, :, :], kk, aT[:, :, :], ALU.mult)
            wait(ve, knew)
            for i in range(4):
                m3 = stt(sc[:, i], rT[:, i], col("r_k_2", i), kkT[:, i], ALU.mult, ALU.mult)
            wait(te, m3, root)
            for i in range(4):
                mm = te.matmul(bank[:, 4 + i], cst("head_ones"), sc[:, i], start=True, stop=True)
            sums_ = pe.after(mm)
            wait(ve, sums_)
            bonus_ready = tt(bonus[:, :, :], bank[:, 4:8], vvT[:, :, :], ALU.mult)
            wait(ve, c)
            before_t = tt(logd[:, :, :], cum[:, :, :], logd[:, :, :], ALU.subtract)
            wait(se, before_t, m)
            e2 = act_(logd[:, :, :], logd[:, :, :], ACT.Exp)
            e3 = act_(inverse[:, :, :], cum[:, :, :], ACT.Exp, scale=-1.0)
            wait(se, e3)
            e1 = act_(cum[:, :, :], cum[:, :, :], ACT.Exp)
            wait(ve, e2, m2)
            a_done = tt(kk, kk, logd[:, :, :], ALU.mult)
            wait(ve, e3)
            b_done = tt(bT[:, :, :], bT[:, :, :], inverse[:, :, :], ALU.mult)
            k_done = tt(kkT[:, :, :], kkT[:, :, :], inverse[:, :, :], ALU.mult)
            wait(ve, e1, bonus_ready)
            r_done = tt(rT, rT, cum[:, :, :], ALU.mult)
            pc_done = dve.after(ve.tensor_copy(pc[:, :, :], cum[:, :, :].rearrange("p i (c s) -> p i c s", s=64)[:, :, :, 63]))
        ready = [a_done, b_done, k_done, r_done, pc_done, bonus_ready, g_ready]

        z_stack.close()
        o_rows = ms("o_rows", [P, 4, 8, 64])
        with sb("kend", [P, 2, 4, P]) as kend, sb("rows", [P, 3, 4, P]) as rows_, sb("m_b", [P, 8, 2, P]) as m_b, \
                sb("m_k", [P, 8, 2, P]) as m_k, sb("xx", [P, 8, 2, P]) as xx, sb("ct", [P, 8, P]) as ct, \
                sb("t1", [P, 8, P]) as t1, sb("w", [P, 512]) as w, sb("zneg", [P, 512]) as zneg, \
                sb("state", [P, 4, P]) as state, sb("scaled", [P, 4, P]) as scaled:
            wait(te, *ready)
            wait(ve, *ready)
            wait(se, *ready)
            wait(ge, *ready)
            zero = dve.after(ve.memset(state[:, :, :], 0.0))
            wait(ve, zero)
            state_ready = [zero]
            all_free = [g_ready, bonus_ready]
            for j in range(4):
                tok = slice(P * j, P * j + P)
                for q, src in enumerate((kkT, bT)):
                    m = tt(kend[:, q].rearrange("p i (c s) -> p i c s", c=2),
                           src[:, :, tok].rearrange("p i (c s) -> p i c s", c=2),
                           pc[:, :, 2 * j:2 * j + 2].unsqueeze(3).broadcast_to([P, 4, 2, 64]), ALU.mult)
                wait(te, m, *all_free)
                for q in range(3):
                    for i in range(4):
                        src = kend[:, q, i] if q < 2 else vvT[:, i, tok]
                        mm = te.transpose(bank[:, q, P * i:P * i + P], src, ident)
                turned = pe.after(mm)
                wait(se, turned)
                rows_ready = act_(rows_[:, :, :, :].rearrange("p q i d -> p q (i d)"), bank[:, 0:3], ACT.Copy)
                k_rows, b_rows, v_rows2 = rows_[:, 0], rows_[:, 1], rows_[:, 2]
                hd = [(g, slice(64 * (g // 4), 64 * (g // 4) + 64), g % 4) for g in range(8)]
                wait(te, rows_ready)
                for g, rr, i in hd:
                    b = 2 * (g // 4) + i // 2
                    mm = te.matmul(bank[:, b, 256 * (i % 2):256 * (i % 2) + 256], bT[rr, i, tok], ar[rr, i, :, tok],
                                   start=True, stop=True)
                mb_done = pe.after(mm)
                for g, rr, i in hd:
                    b = 4 + 2 * (g // 4) + i // 2
                    mm = te.matmul(bank[:, b, 256 * (i % 2):256 * (i % 2) + 256], kkT[rr, i, tok], ar[rr, i, :, tok],
                                   start=True, stop=True)
                mk_done = pe.after(mm)
                masks = cst("pair_masks").rearrange("p (a t) -> p a t", a=2)
                wait(ve, mb_done)
                for g in range(8):
                    mb = tt(m_b[:, g], bank[:, g // 2, 256 * (g % 2):256 * (g % 2) + 256].rearrange("p (a t) -> p a t", a=2), masks, ALU.mult)
                wait(te, mb)
                for g, rr, i in hd:
                    mm = te.matmul(bank[:, g // 4, P * i:P * i + P], ar[rr, i, 0, tok], bT[rr, i, tok], start=True, stop=True)
                mn_done = pe.after(mm)
                wait(ve, mk_done)
                for g in range(8):
                    mk = tt(m_k[:, g], bank[:, 4 + g // 2, 256 * (g % 2):256 * (g % 2) + 256].rearrange("p (a t) -> p a t", a=2), masks, ALU.mult)

                def per_head(a):
                    return a.unsqueeze(1).broadcast_to([P, 4, P])

                lv_ready = [None, None]
                for hp in range(2):
                    g4 = slice(4 * hp, 4 * hp + 4)
                    wait(ve, mn_done, mb)
                    a1 = tt(xx[:, g4, 0], bank[:, hp].rearrange("p (g t) -> p g t", g=4), per_head(cst("level0")), ALU.mult)
                    a2 = tt(xx[:, g4, 1], m_b[:, g4, 0], per_head(cst("levels_T", 0, P)), ALU.mult)
                    wait(ve, a1, a2)
                    a3 = tt(xx[:, g4], ident.unsqueeze(1).unsqueeze(1).broadcast_to([P, 4, 2, P]), xx[:, g4], ALU.subtract)
                    lv_ready[hp] = a3
                t1_used = [None, None]
                ct_used = [None, None]
                for level in range(1, 6):
                    for hp in range(2):
                        g4 = slice(4 * hp, 4 * hp + 4)
                        wait(ge, mb)
                        if ct_used[hp]:
                            wait(ge, ct_used[hp])
                        c_ready = pool.after(ge.tensor_tensor(ct[:, g4], m_b[:, g4, 0], per_head(cst("levels_T", P * level, P)), ALU.mult))
                        wait(te, c_ready, lv_ready[hp], mk)
                        for i in range(4):
                            g = 4 * hp + i
                            mm = te.matmul(bank[:, hp, P * i:P * i + P], ct[:, g], xx[:, g, 0], start=True, stop=True)
                        t_done = pe.after(mm)
                        ct_used[hp] = t_done
                        wait(se, t_done)
                        if t1_used[hp]:
                            wait(se, t1_used[hp])
                        t_ready = act_(t1[:, g4].rearrange("p g t -> p (g t)"), bank[:, hp], ACT.Copy)
                        wait(te, t_ready)
                        for i in range(4):
                            g, b = 4 * hp + i, 2 + 2 * hp + i // 2
                            if level < 5:
                                te.matmul(bank[:, b, 256 * (i % 2):256 * (i % 2) + P], xx[:, g, 1], t1[:, g], start=True, stop=True)
                            mm = te.matmul(bank[:, b, 256 * (i % 2) + P:256 * (i % 2) + 256], t1[:, g], xx[:, g, 1], start=True, stop=True)
                        y_done = pe.after(mm)
                        t1_used[hp] = y_done
                        wait(ve, y_done)
                        y = bank[:, 2 + 2 * hp:4 + 2 * hp].rearrange("p b (g a t) -> p (b g) a t", g=2, a=2)
                        if level < 5:
                            lv_ready[hp] = tt(xx[:, g4], xx[:, g4], y, ALU.subtract)
                        else:
                            lv_ready[hp] = tt(xx[:, g4, 1], xx[:, g4, 1], y[:, :, 1], ALU.subtract)

                o_done = []
                wait(te, *lv_ready)
                z_read = None
                for cp in range(2):
                    half = slice(64 * cp, 64 * cp + 64)
                    wait(te, *state_ready)
                    for i in range(4):
                        te.matmul(bank[:, 6, P * i:P * i + P], ar[:, i, 0, tok], state[:, i], start=True, stop=False, skip_group_check=True)
                        for hp in range(2):
                            g = 4 * hp + i
                            mm = te.matmul(bank[:, 6, P * i + 64 * hp:P * i + 64 * hp + 64], m_k[:, g, 0], v_rows2[:, i, 64 * hp:64 * hp + 64],
                                           start=False, stop=hp == 1, skip_group_check=True)
                    w_done = pe.after(mm)
                    for i in range(4):
                        mm = te.matmul(bank[:, 4 + cp, P * i:P * i + P], ar[:, i, 1, tok], state[:, i], start=True, stop=True)
                    o_done.append(pe.after(mm))
                    wait(se, w_done)
                    w_ready = act_(w[:, :], bank[:, 6], ACT.Copy)
                    wait(te, w_ready)
                    for i in range(4):
                        for hp in range(2):
                            cc = slice(P * i + 64 * hp, P * i + 64 * hp + 64)
                            mm = te.matmul(bank[:, 7, cc], xx[:, 4 * hp + i, 1], w[:, cc], start=True, stop=True)
                    z_done = pe.after(mm)
                    wait(se, z_done)
                    z_ready = act_(zneg[half, :], bank[half, 7], ACT.Copy, scale=-1.0)
                    c = 2 * j + cp
                    wait(ve, o_done[-1], *state_ready)
                    keep = tt(scaled[:, :, :], state[:, :, :], pc[:, :, c:c + 1].broadcast_to([P, 4, P]), ALU.mult)
                    wait(te, z_ready)
                    for i in range(4):
                        te.matmul(bank[:, 2 + cp, P * i:P * i + P], k_rows[half, i], v_rows2[half, i], start=True, stop=False)
                        mm = te.matmul(bank[:, 2 + cp, P * i:P * i + P], b_rows[half, i], zneg[half, P * i:P * i + P], start=False, stop=True)
                    s_done = pe.after(mm)
                    wait(ve, s_done, keep)
                    state_ready = []
                    for hp in range(2):
                        rr = slice(64 * hp, 64 * hp + 64)
                        state_ready.append(tt(state[rr, :, rr], scaled[rr, :, rr],
                                              bank[rr, 2 + cp].rearrange("p (i d) -> p i d", i=4)[:, :, rr], ALU.add))
                for i in range(4):
                    for hp in range(2):
                        g = 4 * hp + i
                        cc = slice(P * i + 64 * hp, P * i + 64 * hp + 64)
                        te.matmul(bank[:, 0, cc], m_k[:, g, 1], v_rows2[:, i, 64 * hp:64 * hp + 64], start=True, stop=False)
                        mm = te.matmul(bank[:, 0, cc], m_b[:, g, 1], zneg[:, cc], start=False, stop=True)
                inner = pe.after(mm)
                wait(se, *o_done)
                orow = o_rows[:, j].rearrange("p h d -> p (h d)")
                e = []
                for cp in range(2):
                    half = slice(64 * cp, 64 * cp + 64)
                    e.append(act_(orow[half], bank[half, 4 + cp], ACT.Copy))
                wait(ve, inner, *e)
                o_sum = tt(orow, orow, bank[:, 0], ALU.add)
                all_free = [o_sum, *state_ready, inner]
                wait(ve, inner)
                wait(se, inner)
                wait(ge, inner)
        if stop == "scan":
            return dump(o_rows[:, :, :, :].rearrange("p j h d -> p j (h d)"), all_free)

        m_hi = ms("m_hi", [P, DT, T], FR)
        m_lo = ms("m_lo", [P, DT, T], FR)
        with sb("o_sq", [P, 4, 8, 64]) as o_sq, sb("gs", [P, 2, 4, 8]) as gs, sb("oT", [P, 4, T]) as oT:
            o32, q32 = (a[:, :, :, :].rearrange("p j h d -> p (j h) d") for a in (o_rows, o_sq))
            mu, var = (gs[:, q].rearrange("p j h -> p (j h)") for q in range(2))

            def spread32(a):
                return a.unsqueeze(2).broadcast_to([P, 32, 64])

            wait(ve, *all_free)
            m = dve.after(ve.tensor_reduce(mu, o32, AX, ALU.add))
            wait(ve, m)
            m = ts(mu, mu, 1.0 / 64, None, ALU.mult)
            wait(ve, m)
            m = tt(o32, o32, spread32(mu), ALU.subtract)
            wait(se, m)
            s2 = act_(q32, o32, ACT.Square)
            wait(ve, s2)
            m = dve.after(ve.tensor_reduce(var, q32, AX, ALU.add))
            wait(se, m)
            root = act_(var, var, ACT.Sqrt, scale=1.0 / 64, bias=eps[:, 2:3])
            wait(ve, root)
            m = dve.after(ve.reciprocal(var, var))
            wait(ve, m)
            m = tt(o32, o32, spread32(var), ALU.mult)
            wait(te, m)
            for i in range(4):
                for j in range(4):
                    mm = te.transpose(bank[:, 4 + i, P * j:P * j + P], o_rows[:, j].rearrange("p h d -> p (h d)")[:, P * i:P * i + P], ident)
                turned = pe.after(mm)
                wait(ve, turned)
                m = ts(oT[:, i], bank[:, 4 + i], col("ln_x_g_2", i), col("ln_x_b_2", i), ALU.mult, ALU.add)
            wait(ve, m, bonus_ready, g_ready)
            m = tt(oT[:, :, :], oT[:, :, :], bonus[:, :, :], ALU.add)
            wait(ve, m)
            m = tt(oT[:, :, :], oT[:, :, :], gT[:, :, :], ALU.mult)
            mix_ready = [split_into(m_hi[:, 0:4], m_lo[:, 0:4], attnT[:, :, :], attn_ready)] * 4
            mix_ready += [split_into(m_hi[:, 4:8], m_lo[:, 4:8], oT[:, :, :], [m])] * 4
        if stop == "mix":
            return dump(m_hi[:, :, :].bitcast(F32), mix_ready[7])

        with sb("mixed", [P, DT, T]) as mixed:
            sq = ar[:, :, :, :].rearrange("p i a t -> p (i a) t")
            free = [[turned, *all_free, m]] * 4
            mixed_ready = []
            for g in range(2):
                step((m_hi[:, 0:4], m_lo[:, 0:4]), range(4), free, mix_ready[0:4] if g == 0 else None, True, False)
                full = step((m_hi[:, 4:8], m_lo[:, 4:8]), range(4), free, mix_ready[4:8] if g == 0 else None, False, True)
                free = []
                for n in range(4):
                    wait(se, full[n], *mix_ready[7])
                    mixed_ready.append((act_(mixed[:, 4 * g + n], bank[:, n], ACT.Copy),))
                    free.append([mixed_ready[-1][0]])
            inv = rms(mixed, mixed_ready, sq, 4, nobody)
            wait(ve, inv)
            x_ready = []
            for k in range(DT):
                m = stt(mixed[:, k], mixed[:, k], col("norm_mix_post_2", k), rstd[:, :], ALU.mult, ALU.mult)
                wait(ve, m)
                x_ready.append((tt(xT[:, k], xT[:, k], mixed[:, k], ALU.add),))
            mixer_done = x_ready[-1]
        mixer.close()
        if stop == "mixer":
            return dump(xT[:, :, :], [m[0] for m in x_ready])

    with sb("f_hi", [P, DT, T], FR) as h_hi, sb("f_lo", [P, DT, T], FR) as h_lo, \
            sb("u3_hi", [P, 16, T], FR) as u_hi, sb("u3_lo", [P, 16, T], FR) as u_lo, sb("f", [P, DT, T]) as f, \
            sb("conv", [P, 4, T]) as conv:
        wait(te, *mixer_done)
        wait(se, *mixer_done)
        inv = rms(xT, x_ready, f, 4, nobody)
        ready = normalise(xT, inv, lambda k: col("norm_ffn_pre_2", k), None, h_hi, h_lo)
        free = [[mixer_done[0]]] * 4
        CW, CB = VEC_AT["conv_w_2"], VEC_AT["conv_b_2"]
        f_ready = [None] * DT
        for half in range(2):
            with slab_loop(8, {pe: 3, act: 8, dve: 12}) as loop:
                split_next()
                earlier = [(dve, dve.n + 2 * n + 2 - 12, loop) for n in range(4)]
                last_lo = (dve, dve.n, loop)
                slab_products((h_hi[:, 0:4], h_lo[:, 0:4]), range(4), [[earlier[n], *free[n]] for n in range(4)],
                              ready[0:4], True, False)
                split_next()
                full = slab_products((h_hi[:, 4:8], h_lo[:, 4:8]), range(4), None, ready[4:8], False, True)
                conv_done = []
                for n in range(4):
                    place = loop.i * 2 + (16 * half + 32 * (n // 2) + n % 2)

                    def cw(tap):
                        return vec[:, bass.ds(place + (CW + 64 * tap), 1)]

                    wait(se, full[n], last_lo)
                    here = act_(conv[:, n], bank[:, n], ACT.Identity, scale=cw(2), bias=vec[:, bass.ds(place + CB, 1)])
                    wait(ve, here)
                    one = stt(conv[:, n, 1:], bank[:, n, 0:T - 1], cw(1), conv[:, n, 1:], ALU.mult, ALU.add)
                    wait(ve, one)
                    conv_done.append(stt(conv[:, n, 2:], bank[:, n, 0:T - 2], cw(0), conv[:, n, 2:], ALU.mult, ALU.add))
                for n in range(2):
                    tile = bass.ds(loop.i * 2 + n, 1)
                    wait(se, conv_done[n])
                    act_gate = act_(conv[:, n], conv[:, n], ACT.Gelu_apprx_tanh)
                    wait(ve, act_gate, conv_done[2 + n])
                    prod = tt(conv[:, n], conv[:, n], conv[:, 2 + n], ALU.mult)
                    wait(se, prod)
                    made = act_(u_hi[:, tile, :], conv[:, n:n + 1], ACT.Copy)
                    wait(ve, made)
                    lo_done = tt(u_lo[:, tile, :], conv[:, n:n + 1], u_hi[:, tile, :].bitcast(F32), ALU.subtract)
            end_loop(8)
            free = [[conv_done[n]] for n in range(4)]
            for g in range(2):
                for k in range(4):
                    full = step((u_hi[:, 4 * k:4 * k + 4], u_lo[:, 4 * k:4 * k + 4]), range(4), free,
                                [[made, lo_done]] * 4 if g == 0 else None, k == 0, k == 3)
                for n in range(4):
                    o = 4 * g + n
                    wait(ve, full[n])
                    if half == 0:
                        f_ready[o] = dve.after(ve.tensor_copy(f[:, o], bank[:, n]))
                    else:
                        f_ready[o] = tt(f[:, o], f[:, o], bank[:, n], ALU.add)
                free = [[f_ready[4 * g + n]] for n in range(4)]
    finish = ExitStack()
    sqf = finish.enter_context(nc.sbuf_tensor("sq_f", [P, DT, T], F32))
    rows_out = finish.enter_context(nc.sbuf_tensor("rows_out", [P, 4, D], F32))
    inv = rms(f, [(m,) for m in f_ready], sqf, 4, nobody)
    wait(ve, inv)
    out_sems = []
    turned_free = [None, None]
    x_ready = []
    for k in range(DT):
        m = stt(f[:, k], f[:, k], col("norm_ffn_post_2", k), rstd[:, :], ALU.mult, ALU.mult)
        wait(ve, m)
        x_ready.append(tt(xT[:, k], xT[:, k], f[:, k], ALU.add))
    for k in range(DT):
        wait(te, x_ready[k])
        if turned_free[k % 2]:
            wait(te, turned_free[k % 2])
        for j in range(4):
            mm = te.transpose(bank[:, 6 + k % 2, P * j:P * j + P], xT[:, k, P * j:P * j + P], ident)
        turned = pe.after(mm)
        wait(se, turned)
        turned_free[k % 2] = act_(rows_out[:, :, P * k:P * k + P], bank[:, 6 + k % 2].rearrange("p (j f) -> p j f", j=4), ACT.Copy)
    stored = nc.alloc_semaphore("stored")
    wait(sy, turned_free[0], turned_free[1])
    sy.dma_start(out[0].rearrange("(j p) n -> p j n", p=P), rows_out[:, :, :]).then_inc(stored, 16)
    sy.wait_ge(stored, 16)


WEIGHTS = ["ada_w", "pool_w", "sgu_w_in", "sgu_w_s", "sgu_b_s", "sgu_w_out", "mlp_w1", "mlp_w2",
           "w_decay_up_2", "w_iclr_up_2", "w_gate_up_2", "w_out_2", "w_ffn_up_2", "w_ffn_down_2", "w_in_2",
           "rel_bias_2", "sinks_2"]
ONE_LAYER = ["sgu_w_in", "sgu_w_out", "w_decay_up_2", "w_iclr_up_2", "w_gate_up_2", "w_out_2",
             "w_ffn_up_2", "w_ffn_down_2", "w_in_2"]


def laid_out(inputs):
    arrays = {n: np.asarray(inputs[n]) for n in WEIGHTS}
    arrays["x"] = np.asarray(inputs["x"])
    for n in ONE_LAYER:
        arrays[n] = arrays[n][0]
    heads = np.concatenate([np.arange(64) + 64 * h for i in range(4) for h in (i, i + 4)])
    w_in, w_out = arrays["w_in_2"].copy(), arrays["w_out_2"].copy()
    w_in[:, :512] = arrays["w_in_2"][:, heads]
    w_out[:512] = arrays["w_out_2"][heads]
    arrays["w_in_2"], arrays["w_out_2"] = w_in, w_out
    flat = np.concatenate([np.asarray(inputs[n]).ravel() for n, _ in VECS])
    arrays["vecs"] = np.concatenate([flat, np.zeros(512 * P - flat.size, flat.dtype)]).reshape(512, P)
    arrays["const"], arrays["buckets"] = constants()
    return {n: np.ascontiguousarray(a) for n, a in arrays.items()}


def declared(nc, arrays):
    t = {n: nc.dram_tensor(f"in_{n}", a.shape, mybir.dt.from_np(a.dtype), kind="ExternalInput").ap()
         for n, a in arrays.items()}
    t["scratch"] = nc.dram_tensor("bias_table", (8, 384), F32, kind="Internal").ap()
    return t, nc.dram_tensor("out", (1, T, D), F32, kind="ExternalOutput").ap()


def kernel(**inputs):
    import concourse.bacc as bacc
    from concourse.bass_utils import run_bass_kernel_spmd
    arrays = laid_out(inputs)
    nc = bacc.Bacc("TRN2", target_bir_lowering=False, num_devices=1)
    program(nc, *declared(nc, arrays))
    r = run_bass_kernel_spmd(nc, [{f"in_{n}": a for n, a in arrays.items()}], core_ids=[0])
    return r.results[0]["out"]
```

```python
import math
from contextlib import ExitStack

import numpy as np

import concourse.bass as bass
from concourse import mybir

F32 = mybir.dt.float32
FR = mybir.dt.float32r
ACT = mybir.ActivationFunctionType
ALU = mybir.AluOpType
AX = mybir.AxisListType.X
PE, ACTE, DVE, SP = (mybir.EngineType.PE, mybir.EngineType.Activation, mybir.EngineType.DVE,
                     mybir.EngineType.SP)

P = 128
D = 1024
DT = D // P
T = 512
DFF = 4096
POOL_WINDOWS = (2, 4, 8, 16)
RMS_EPS = 1e-6
LN_EPS = 1e-5
GN_EPS = 64e-5
EXP_M_HALF = math.exp(-0.5)
MASKED = -1e30

VECS = [("c", 8), ("ada_b", 96), ("norm_mix_g", 16), ("norm_mlp_g", 16), ("pool_scale", 8),
        ("sgu_ln_g", 8), ("sgu_ln_b", 8), ("final_g", 8), ("norm_mix_pre_2", 8),
        ("norm_mix_post_2", 8), ("norm_ffn_pre_2", 8), ("norm_ffn_post_2", 8),
        ("rwkv_shift_mix_2", 14), ("w0_2", 4), ("a0_2", 4), ("k_k_2", 4), ("k_a_2", 4),
        ("r_k_2", 4), ("ln_x_g_2", 4), ("ln_x_b_2", 4), ("conv_w_2", 192), ("conv_b_2", 64)]
VEC_AT = {}
_at = 0
for _name, _rows in VECS:
    VEC_AT[_name] = _at
    _at += _rows
assert _at <= 512

CONSTS = [("ident", 128), ("head_ones", 128), ("reverse", 128), ("tril_T", 128), ("level0", 128),
          ("levels_T", 6 * 128), ("pair_masks", 256), ("chunk_start", 512), ("pool_inv", 64)]
CONST_AT = {}
_at = 0
for _name, _cols in CONSTS:
    CONST_AT[_name] = _at
    _at += _cols
CONST_COLS = _at


def constants():
    r = np.arange(P)
    row, col = r[:, None], r[None, :]
    out = np.zeros((P, CONST_COLS), np.float32)

    def put(name, a, k=0):
        out[:, CONST_AT[name] + k:CONST_AT[name] + k + a.shape[1]] = a

    same = row // 64 == col // 64
    put("ident", row == col)
    put("head_ones", same)
    put("reverse", row + col == P - 1)
    put("tril_T", row <= col)

    def lower(b):
        return (row // (2 * b) == col // (2 * b)) & (row % (2 * b) >= b) & (col % (2 * b) < b)

    put("level0", lower(1))
    for n in range(6):
        put("levels_T", lower(2 ** n).T, n * P)
    put("pair_masks", same & (row < col))
    put("pair_masks", same & (row <= col), P)
    put("chunk_start", np.broadcast_to(np.arange(T) % 64 != 0, (P, T)))
    t = np.arange(16)
    for g, w in enumerate(POOL_WINDOWS):
        put("pool_inv", np.broadcast_to((1.0 / np.minimum(t + 1.0, w)).astype(np.float32), (P, 16)), 16 * g)

    table = np.zeros((33, 384), np.float32)
    for i in range(383):
        rel = 255 - i
        if 0 <= rel < 128:
            n = np.float32(max(rel, 1))
            large = 16 + int(np.float32(np.log(n / np.float32(16))) / np.float32(math.log(8)) * np.float32(16)) \
                if rel >= 16 else 0
            table[rel if rel < 16 else min(large, 31), i] = 1
        else:
            table[32, i] = 1
    return out, table


class Counter:

    def __init__(self, nc, name):
        self.sem = nc.alloc_semaphore(name)
        self.n = 0
        self.loop = None

    def after(self, ins, by=1):
        ins.then_inc(self.sem, by)
        self.n += by
        return (self, self.n, self.loop)


class Loop:

    def __init__(self, nc, turns, per, engines):
        self.nc, self.turns, self.per, self.engines = nc, turns, per, engines

    def __enter__(self):
        self.base = {c: c.n for c in self.per}
        for c in self.per:
            c.loop = self
        self.fori = self.nc.Fori(0, self.turns, engines=self.engines)
        self.i = self.fori.__enter__()
        return self

    def __exit__(self, *e):
        self.fori.__exit__(*e)
        if e[0]:
            return
        for c, per in self.per.items():
            assert c.n == self.base[c] + per, (c.sem, c.n - self.base[c], per)
            c.n = self.base[c] + per * self.turns
            c.loop = None


def wait(eng, *marks):
    for counter, n, loop in marks:
        if loop is not None and counter.loop is loop:
            eng.wait_ge(counter.sem, loop.i * loop.per[counter] + n)
        elif loop is not None:
            eng.wait_ge(counter.sem, n + loop.per[counter] * (loop.turns - 1))
        else:
            eng.wait_ge(counter.sem, n)


def before(mark):
    counter, n, loop = mark
    return (counter, n - loop.per[counter], loop)


def program(nc, t, out, stop=None):
    pe, act, dve, pool = (Counter(nc, n) for n in ("pe_done", "act_done", "dve_done", "pool_done"))
    hi_made, lo_made, slab_used = (Counter(nc, n) for n in ("hi_made", "lo_made", "slab_used"))
    landed = [nc.alloc_semaphore(f"slab_landed{i}") for i in range(2)]
    te, se, ve, ge, sy = nc.tensor, nc.scalar, nc.vector, nc.gpsimd, nc.sync
    te.sem_inc(slab_used.sem, 1)
    slab_used.n = 1

    def sb(name, shape, dt=F32):
        return nc.sbuf_tensor(name, shape, dt)

    def alloc(name, shape, dt=F32):
        return nc.alloc_sbuf_tensor(name, shape, dt)

    xT = alloc("xT", [P, DT, T])
    raw = alloc("raw", [P, 2, 4, 512])
    w_hi = alloc("w_hi", [P, 2, 4, 512], FR)
    w_lo = alloc("w_lo", [P, 2, 4, 512], FR)
    const = alloc("const", [P, CONST_COLS])
    vec = alloc("vec", [P, 512])
    mod = alloc("mod", [P, 48 + 6 + 48])
    gain = alloc("gain", [P, 48])
    rstd_diag = alloc("rstd_diag", [P, 4, P])
    rstd_rows = alloc("rstd_rows", [P, 4])
    tmp = alloc("tmp", [P, 2, T])
    sink = alloc("sink", [P, 8])
    c_act = alloc("c_act", [P, DT])
    mean_ones = alloc("mean_ones", [P, P])
    ones = alloc("ones", [P, P])
    eps = alloc("eps", [P, 3])
    bank = nc.alloc_psum_tensor("bank", [P, 8, 512], F32)

    def cst(name, k=0, n=None):
        a = CONST_AT[name] + k
        return const[:, a:a + (n or dict(CONSTS)[name])]

    def col(name, k):
        return vec[:, VEC_AT[name] + k:VEC_AT[name] + k + 1]

    ident = cst("ident")

    slabs = {"sent": 0, "split": 0, "used": 0}
    limit = {None: 999, "pool": 0, "mlp0": 33, "sgu": 45, "block1": 77, "attn": 87, "scan": 87, "mix": 87,
             "mixer": 91}[stop]

    def send(src, index=None, base=None):
        s = slabs["sent"]
        if s >= limit:
            return
        if index is None:
            if s >= 2:
                sy.wait_ge(hi_made.sem, s - 1)
                sy.wait_ge(lo_made.sem, s - 1)
        else:
            sy.wait_ge(hi_made.sem, index * 2 + (s - 1))
            sy.wait_ge(lo_made.sem, index * 2 + (s - 1))
        parts = src if isinstance(src, list) else [(slice(0, 512), src)]
        if len(parts) == 1:
            a = parts[0][1]
            parts = [(0, 2, slice(0, 512), a[:, 0:2]), (2, 4, slice(0, 512), a[:, 2:4])]
        else:
            parts = [(0, 4, c, a) for c, a in parts]
        for k0, k1, c, a in parts:
            sy.dma_start(raw[:, s % 2, k0:k1, c], a).then_inc(landed[s % 2], 16)
        slabs["sent"] += 1

    def rows(w, k, cols):
        return w[512 * k:512 * k + 512, cols].rearrange("(k p) n -> p k n", p=P)

    def send_linear(w, kslabs, groups, k0=0):
        for g in groups:
            for k in range(kslabs):
                send(rows(w, k0 + k, slice(512 * g, 512 * g + 512)))

    def send_loop(turns, source):
        s0 = slabs["sent"]
        if s0 >= limit:
            return
        if limit < s0 + 2 * turns:
            return send(source(0, 0))
        if s0 == 0:
            for k in range(2):
                send(source(k, 0))
            slabs["sent"] = 0
        with nc.Fori(1 if s0 == 0 else 0, turns, engines=[SP]) as i:
            for k in range(2):
                send(source(k, i), index=i)
        slabs["sent"] = s0 + 2 * turns

    def split_next():
        s = slabs["split"]
        slot = s % 2
        loop = hi_made.loop
        i = 0 if loop is None else loop.i
        for eng in (se, ve):
            eng.wait_ge(landed[slot], i * 32 + 32 * (s // 2 + 1))
            if s >= 1:
                eng.wait_ge(slab_used.sem, i * 2 + s)
        made = hi_made.after(se.activation(w_hi[:, slot], raw[:, slot], ACT.Copy))
        wait(ve, made)
        lo_made.after(ve.tensor_tensor(w_lo[:, slot], raw[:, slot], w_hi[:, slot].bitcast(F32), ALU.subtract))
        slabs["split"] += 1

    TOTAL_SLABS = 2 * 32 + 8 + 4 + 10 + 4 + 32 + 16

    def slab_products(moving, banks, free, ready, first, last, weights_stationary=True):
        s = slabs["used"]
        slot = s % 2
        loop = slab_used.loop
        i = 0 if loop is None else loop.i
        te.wait_ge(hi_made.sem, i * 2 + (s + 1))
        te.wait_ge(lo_made.sem, i * 2 + (s + 1))
        hi, lo = moving
        full = []
        order = [(n, k) for k in range(4) for n in range(4)] if ready is not None and first else \
            [(n, k) for n in range(4) for k in range(4)]
        for n, k in order:
            tile = slice(P * n, P * n + P)
            if first and k == 0:
                wait(te, *free[n])
            if n == 0 and ready is not None:
                wait(te, *ready[k])
            if weights_stationary:
                three = ((w_hi[:, slot, k, tile], hi[:, k]), (w_hi[:, slot, k, tile], lo[:, k]),
                         (w_lo[:, slot, k, tile], hi[:, k]))
            else:
                three = ((hi[:, k, tile], w_hi[:, slot, k]), (hi[:, k, tile], w_lo[:, slot, k]),
                         (lo[:, k, tile], w_hi[:, slot, k]))
            for j, (a, b) in enumerate(three):
                mm = te.matmul(bank[:, banks[n]], a, b, start=first and k == 0 and j == 0,
                               stop=last and k == 3 and j == 2)
            if last and k == 3 and n < 3:
                full.append(pe.after(mm))
        full.append(slab_used.after(mm))
        slabs["used"] += 1
        return full

    def step(*args, **kw):
        if slabs["split"] < TOTAL_SLABS:
            split_next()
        return slab_products(*args, **kw)

    def slab_loop(turns, per):
        per = {**per, hi_made: 2, lo_made: 2, slab_used: 2}
        return Loop(nc, turns, per, [PE, ACTE, DVE])

    def end_loop(turns):
        for k in ("split", "used"):
            slabs[k] += 2 * (turns - 1)

    PROJ_GROUPS = (4, 2, 3, 1, 0)

    def all_slabs():
        for layer in range(2):
            if layer == 1:
                send_linear(t["sgu_w_in"], 2, range(4))
                send_linear(t["sgu_w_out"], 2, range(2))
            for half in range(2):
                w1, w2 = t["mlp_w1"][layer], t["mlp_w2"][layer]
                send_loop(4, lambda k, i: w1[512 * k:512 * k + 512, bass.ds(i * 512 + 2048 * half, 512)]
                          .rearrange("(k p) n -> p k n", p=P))
                send_linear(w2, 4, range(2), k0=4 * half)
        send_linear(t["w_in_2"], 2, PROJ_GROUPS)
        send_linear(t["w_out_2"], 2, range(2))
        for half in range(2):
            w = t["w_ffn_up_2"]
            send_loop(8, lambda k, i: [
                (slice(256 * v, 256 * v + 256),
                 w[512 * k:512 * k + 512, bass.ds(i * 256 + (2048 * half + DFF * v), 256)]
                 .rearrange("(k p) n -> p k n", p=P)) for v in range(2)])
            send_linear(t["w_ffn_down_2"], 4, range(2), k0=4 * half)
        assert stop or slabs["sent"] == TOTAL_SLABS

    def act_(*a, **k):
        return act.after(se.activation(*a, **k))

    def tt(o, a, b, op):
        return dve.after(ve.tensor_tensor(o, a, b, op))

    def ts(o, a, s1, s2, op0, op1=None):
        return dve.after(ve.tensor_scalar(o, a, s1, s2, op0, op1) if op1 else ve.tensor_scalar(o, a, s1, None, op0))

    def stt(o, a, s, b, op0, op1):
        return dve.after(ve.scalar_tensor_tensor(out=o, in0=a, scalar=s, in1=b, op0=op0, op1=op1))

    rstd_bank = bank[:, 5]
    norm = {"read": []}

    class Rms:

        def __init__(self, src, sq, free=()):
            self.src, self.sq, self.k, self.marks = src, sq, 0, []
            wait(se, *free)
            wait(te, *free)

        def add(self, *ready):
            k = self.k
            wait(se, *ready)
            if k >= 4:
                wait(se, self.marks[k - 4])
            square = act_(self.sq[:, k % 4], self.src[:, k], ACT.Square)
            wait(te, square)
            for j in range(4):
                mm = te.matmul(bank[:, 4, j:j + 1], self.sq[:, k % 4, P * j:P * j + P], mean_ones[:, 0:1],
                               start=k == 0 and j == 0, stop=k == DT - 1, skip_group_check=True)
            self.marks.append(pe.after(mm))
            self.k += 1

        def end(self):
            wait(se, self.marks[-1])
            root = act_(rstd_rows[:, :], bank[:, 4, 0:4], ACT.Sqrt, bias=eps[:, 0:1])
            wait(ve, root)
            inv = dve.after(ve.reciprocal(rstd_rows[:, :], rstd_rows[:, :]))
            wait(ve, inv)
            diag = tt(rstd_diag[:, :, :], ident.unsqueeze(1).broadcast_to([P, 4, P]),
                      rstd_rows[:, :].unsqueeze(2).broadcast_to([P, 4, P]), ALU.mult)
            wait(te, diag, *norm["read"])
            return pe.after(te.matmul(rstd_bank, ones[:, :], rstd_diag[:, :, :].rearrange("p j t -> p (j t)"),
                                      start=True, stop=True))

    def normalise(src, inv, g, shift, hi, lo, tiles=DT, free=()):
        done = []
        wait(se, *free)
        wait(ve, *free)
        wait(ve, inv)

        def scale(k):
            if k >= 2:
                wait(ve, *done[k - 2])
            return stt(tmp[:, k % 2], src[:, k], g(k), rstd_bank, ALU.mult, ALU.mult)

        scaled = scale(0)
        for k in range(tiles):
            wait(se, scaled)
            if shift:
                made = act_(hi[:, k], tmp[:, k % 2], ACT.Identity, bias=shift(k))
            else:
                made = act_(hi[:, k], tmp[:, k % 2], ACT.Copy)
            this = scaled
            if k + 1 < tiles:
                scaled = scale(k + 1)
            wait(ve, this, made)
            if shift:
                rest = stt(lo[:, k], tmp[:, k % 2], shift(k), hi[:, k].bitcast(F32), ALU.add, ALU.subtract)
            else:
                rest = tt(lo[:, k], tmp[:, k % 2], hi[:, k].bitcast(F32), ALU.subtract)
            done.append((made, rest))
        norm["read"] = [scaled]
        return done

    def split_into(hi, lo, src, ready):
        wait(se, *ready)
        made = act_(hi, src, ACT.Copy)
        wait(ve, made, *ready)
        return (made, tt(lo, src, hi.bitcast(F32), ALU.subtract))

    def dump(ap, marks):
        s = nc.alloc_semaphore("dumped")
        wait(se, *marks)
        n = P * ap.shape[1] * ap.shape[2]
        se.dma_start(out.rearrange("a t f -> (a t f)")[0:n].rearrange("(p k t) -> p k t", p=P, k=ap.shape[1]), ap).then_inc(s, 16)
        se.wait_ge(s, 16)

    nobody = ()

    def modv(layer, part, k):
        a = 54 * layer + 8 * part + k
        return mod[:, a:a + 1]

    ident_in, const_in, x_in, vec_in, pool_w_in = (nc.alloc_semaphore(n) for n in ("ident_in", "const_in", "x_in", "vec_in", "pool_w_in"))
    ADA_RING = 3
    ada_landed = [nc.alloc_semaphore(f"ada_landed{i}") for i in range(ADA_RING)]
    with sb("x_rows", [P, 4, D]) as x_rows, sb("vec_rows", [P, 4, P]) as vec_rows, \
            sb("ada_ring", [P, ADA_RING, 8, 512]) as ada_ring, sb("ada_acc", [P, 2, 512]) as ada_acc, \
            sb("ada_row", [1, 2, 512]) as ada_row, sb("h", [P, DT, 16 + T]) as h, \
            sb("sums", [P, 2, 2, 16 + T]) as sums, sb("pooled", [P, DT, T]) as pooled, \
            sb("pool_w", [P, 4, 2, 256]) as pool_w, sb("rel", [33, 8]) as rel:
        sy.dma_start(const[:, 0:P], t["const"][:, 0:P]).then_inc(ident_in, 16)
        sy.dma_start(vec_rows[:, :, :], t["vecs"].rearrange("(j p) n -> p j n", p=P)).then_inc(vec_in, 16)
        se.dma_start(x_rows[:, :, :], t["x"][0].rearrange("(j p) n -> p j n", p=P)).then_inc(x_in, 16)
        se.dma_start(const[:, P:], t["const"][:, P:]).then_inc(const_in, 16)
        rel_in, table_out = (nc.alloc_semaphore(n) for n in ("rel_in", "table_out"))
        buckets, table = tmp[0:33, 0, 0:384], tmp[0:8, 1, 0:384]
        outside = dve.after(ve.memset(rel[32:33, :], MASKED))
        ge.dma_start(rel[0:32, :], t["rel_bias_2"]).then_inc(rel_in, 16)
        ge.dma_start(buckets, t["buckets"]).then_inc(rel_in, 16)
        ge.dma_start(sink[:, :], t["sinks_2"].broadcast_to([P, 8])).then_inc(rel_in, 16)
        ge.dma_start(pool_w[:, :, :, :].rearrange("p g k n -> p (g k) n"),
                     t["pool_w"][0].rearrange("g (k p) n -> p (g k) n", p=P)).then_inc(pool_w_in, 16)
        ve.memset(mean_ones[:, :], 1.0 / D)
        for i, e in enumerate((RMS_EPS, LN_EPS, GN_EPS)):
            ve.memset(eps[:, i:i + 1], e)
        ve.memset(h[:, :, 0:16], 0.0)
        sums_zero = dve.after(ve.memset(sums[:, :, :, 0:16], 0.0))
        set_up = dve.after(ve.memset(ones[:, :], 1.0))
        te.wait_ge(ident_in, 16)
        te.wait_ge(vec_in, 16)
        for j in range(4):
            mm = te.transpose(bank[:, 7, P * j:P * j + P], vec_rows[:, j], ident)
        turned = pe.after(mm)
        wait(ve, turned)
        ve.wait_ge(ident_in, 16)
        vec_ready = dve.after(ve.tensor_copy(vec[:, :], bank[:, 7]))
        wait(se, vec_ready, set_up)
        silu = act_(c_act[:, :], vec[:, VEC_AT["c"]:VEC_AT["c"] + 8], ACT.Silu)
        te.wait_ge(x_in, 16)
        wait(te, set_up)
        norm_x = Rms(xT, pooled[:, 0:4])
        copied = []
        for k in range(DT):
            if k >= 2:
                wait(te, copied[k - 2])
            for j in range(4):
                mm = te.transpose(bank[:, k % 2, P * j:P * j + P], x_rows[:, j, P * k:P * k + P], ident)
            turned = pe.after(mm)
            wait(se, turned)
            copied.append(act_(xT[:, k], bank[:, k % 2], ACT.Copy))
        te.wait_ge(rel_in, 48)
        wait(te, outside, *copied)
        looked_up = pe.after(te.matmul(bank[0:8, 0, 0:384], rel[:, :], buckets, start=True, stop=True))
        wait(se, looked_up)
        ve.wait_ge(rel_in, 48)
        table_made = act_(table, bank[0:8, 0, 0:384], ACT.Copy)
        wait(ge, table_made)
        ge.dma_start(t["scratch"], table).then_inc(table_out, 16)

        used = [None] * 12
        acc_used = []

        def ada_arrives(eng, g):
            eng.wait_ge(ada_landed[g % ADA_RING], 16 * (g // ADA_RING + 1))

        def ada_on_dve(g):
            ada_arrives(ve, g)
            wait(ve, silu)
            a = ada_acc[:, len(acc_used) % 2]
            if len(acc_used) >= 2:
                wait(ve, acc_used[-2])
            m = ts(a, ada_ring[:, g % ADA_RING, 0], c_act[:, 0:1], None, ALU.mult)
            for k in range(1, 8):
                wait(ve, m)
                m = stt(a, ada_ring[:, g % ADA_RING, k], c_act[:, k:k + 1], a, ALU.mult, ALU.add)
            used[g] = m
            acc_used.append(None)

            def sum_on_pe(n=len(acc_used) - 1):
                wait(te, m)
                for c in range(4):
                    mm = te.matmul(bank[:, 6, 4 * g + c:4 * g + c + 1], a[:, P * c:P * c + P], ones[:, 0:1],
                                   start=True, stop=True)
                acc_used[n] = pe.after(mm)
                return acc_used[n]

            return sum_on_pe

        row_copied, row_at, rows_made, rows_turned = {}, {}, [], []

        def ada_row_on_pe(g):
            ada_arrives(te, g)
            wait(te, silu)
            if rows_made:
                wait(te, *rows_made[-2:-1])
            q = len(rows_made) % 2
            row_at[g] = q
            for k in range(8):
                mm = te.matmul(bank[0:1, 2 + q], c_act[:, k:k + 1], ada_ring[:, g % ADA_RING, k],
                               start=k == 0, stop=k == 7)
            used[g] = pe.after(mm)
            wait(se, used[g])
            if len(rows_made) >= 2:
                wait(se, rows_turned[len(rows_made) - 2])
            row_copied[g] = act_(ada_row[0:1, q], bank[0:1, 2 + q], ACT.Copy)
            rows_made.append(row_copied[g])

        def ada_row_turned(g):
            wait(te, row_copied[g])
            for c in range(4):
                mm = te.matmul(bank[:, 7, 4 * g + c:4 * g + c + 1], ada_row[0:1, row_at[g], P * c:P * c + P],
                               ones[0:1, 0:1], start=True, stop=True)
            rows_turned.append(pe.after(mm))
            return rows_turned[-1]

        def mod_columns(a, b, source, mark):
            wait(ve, mark, vec_ready)
            m = tt(mod[:, a:b], bank[:, source, a:b], vec[:, VEC_AT["ada_b"] + a:VEC_AT["ada_b"] + b], ALU.add)
            wait(ve, m)
            return m

        def gains(at, scale_at, norm_at):
            m = stt(gain[:, at:at + 8], mod[:, scale_at:scale_at + 8], 1.0, vec[:, norm_at:norm_at + 8], ALU.add, ALU.mult)
            wait(ve, m)
            return m

        ada_row_on_pe(1)
        summed0 = ada_on_dve(0)()
        for k in range(DT):
            norm_x.add(copied[k])
        ada_row_turned(1)
        ada_row_on_pe(3)
        summed2 = ada_on_dve(2)()
        row3 = ada_row_turned(3)
        inv = norm_x.end()
        for a, source in ((0, 6), (4, 7), (8, 6), (12, 7)):
            shift_ready = mod_columns(a, a + 4, source, row3)
        gains(0, 8, VEC_AT["norm_mix_g"])

        wait(ve, inv, table_made)
        ve.wait_ge(table_out, 16)
        wait(se, shift_ready)
        made = []
        for k in range(DT):
            if k >= 2:
                wait(ve, made[k - 2])
            scaled = stt(tmp[:, k % 2], xT[:, k], gain[:, k:k + 1], rstd_bank, ALU.mult, ALU.mult)
            wait(se, scaled)
            made.append(act_(h[:, k, 16:], tmp[:, k % 2], ACT.Identity, bias=modv(0, 0, k)))
        norm["read"] = [scaled]
        for g in range(4, 11):
            ada_row_on_pe(g)
            if g == 5:
                wait(te, shift_ready)
            if g > 4:
                ada_row_turned(g - 1)
        rows_ready = ada_row_turned(10)

        wait(ve, sums_zero)
        ve.wait_ge(const_in, 16)
        pooled_ready = []
        for g, window in enumerate(POOL_WINDOWS):
            source = h[:, 2 * g:2 * g + 2]
            hg = source[:, :, 16:]
            wait(ve, made[2 * g + 1])
            a, w = 0, 1
            while w < window:
                if w > 1:
                    wait(ve, last)
                last = tt(sums[:, a, :, 16:], source[:, :, 16:], source[:, :, 16 - w:16 + T - w], ALU.add)
                source = sums[:, a]
                a, w = 1 - a, 2 * w
            wait(ve, last)
            mean = stt(pooled[:, 2 * g:2 * g + 2], source[:, :, 16:], 1.0 / window, hg, ALU.mult, ALU.subtract)
            inv_count = cst("pool_inv", 16 * g, 16).unsqueeze(1).broadcast_to([P, 2, 16])
            wait(ve, made[7])
            last = tt(tmp[:, :, 0:16], source[:, :, 16:32], inv_count, ALU.mult)
            wait(ve, mean, last)
            pooled_ready.append(tt(pooled[:, 2 * g:2 * g + 2, 0:16], tmp[:, :, 0:16], hg[:, :, 0:16], ALU.subtract))
        sum11 = ada_on_dve(11)
        mod_columns(16, 44, 7, rows_ready)
        scale_ready = tt(gain[:, 32:40], mod[:, 16:24], vec[:, VEC_AT["pool_scale"]:VEC_AT["pool_scale"] + 8], ALU.mult)
        mod_columns(44, 48, 6, sum11())
        mod_ready = gains(8, 32, VEC_AT["norm_mlp_g"])
        wait(se, mod_ready)
        for g in range(12):
            if g >= ADA_RING:
                wait(sy, used[g - ADA_RING])
            sy.dma_start(ada_ring[:, g % ADA_RING], t["ada_w"][0, :, 512 * g:512 * g + 512]
                         .rearrange("(k p) n -> p k n", p=P)).then_inc(ada_landed[g % ADA_RING], 16)
        all_slabs()
        wait(ve, scale_ready)
        te.wait_ge(pool_w_in, 16)
        x_ready = []
        for o in range(DT):
            g, n = divmod(o, 2)
            wait(te, pooled_ready[g])
            if o >= 2:
                wait(te, x_ready[o - 2])
            for k in range(2):
                mm = te.matmul(bank[:, n], pool_w[:, g, k, P * n:P * n + P], pooled[:, 2 * g + k],
                               start=k == 0, stop=k == 1)
            full = pe.after(mm)
            wait(ve, full)
            x_ready.append(stt(xT[:, o], bank[:, n], gain[:, 32 + o:33 + o], xT[:, o], ALU.mult, ALU.add))
        stage0_done = [x_ready[-1], table_made, *rows_made[-2:], rows_ready]
        wait(se, *stage0_done)
        if stop == "pool":
            return dump(xT[:, :, :], x_ready)

    def project(moving, groups, free, ready, evacuate, norm=None, weights_stationary=True):
        marks = []
        for g in range(groups):
            for k, m in enumerate(moving):
                full = step(m, range(4), free, ready[4 * k:4 * k + 4] if ready and g == 0 else None,
                            k == 0, k == len(moving) - 1, weights_stationary)
                if norm and g and k == 0:
                    for o in range(4 * g - 4, 4 * g):
                        norm.add(marks[o])
            for n in range(4):
                wait(se, full[n])
                wait(ve, full[n])
                marks.append(evacuate(4 * g + n, n))
            free = [[m] for m in marks[-4:]]
        if norm:
            for o in range(4 * groups - 4, 4 * groups):
                norm.add(marks[o])
        return marks

    def quarters(hi, lo, n):
        return [(hi[:, 4 * k:4 * k + 4], lo[:, 4 * k:4 * k + 4]) for k in range(n)]

    class AdaSecond:

        def __init__(self, ring, acc):
            self.ring, self.acc = ring, acc
            self.landed = [nc.alloc_semaphore(f"ada1_landed{i}") for i in range(2)]
            self.added = Counter(nc, "ada1_added")
            self.summed = Counter(nc, "ada1_summed")
            ve.sem_inc(self.added.sem, 2)
            self.added.n = 2
            self.cleared = dve.after(ve.memset(acc[:, :], 0.0))
            wait(te, self.cleared)
            self.per = {dve: 29, self.added: 4, self.summed: 1}
            self.half = 0

        def load(self, loop, units):
            turn = loop.i + 4 * self.half
            for u in units:
                if u < 2:
                    self.start = self.added.n if u == 0 else self.start
                wait(se, (self.added, self.start + u - 1, loop))
                se.dma_start(self.ring[:, u % 2], t["ada_w"][1, :, bass.ds(turn * 768 + 192 * u, 192)]
                             .rearrange("(k p) n -> p k n", p=P)).then_inc(self.landed[u % 2], 16)

        def add(self, loop, units):
            turn = loop.i + 4 * self.half
            for u in units:
                ve.wait_ge(self.landed[u % 2], turn * 32 + 16 * (u // 2 + 1))
                part = self.acc[:, 192 * u:192 * u + 192]
                m = ts(part, self.ring[:, u % 2, 0], c_act[:, 0:1], None, ALU.mult)
                for k in range(1, 8):
                    wait(ve, m)
                    ins = ve.scalar_tensor_tensor(out=part, in0=self.ring[:, u % 2, k], scalar=c_act[:, k:k + 1],
                                                  in1=part, op0=ALU.mult, op1=ALU.add)
                    m = (dve if k < 7 else self.added).after(ins)

        def columns(self, offset):
            for c in range(6):
                mm = te.matmul(bank[:, 7, c:c + 1], self.acc[:, P * c:P * c + P], ones[:, 0:1], start=True, stop=True)
            summed = self.summed.after(mm)
            wait(ve, summed)
            b = VEC_AT["ada_b"]
            if isinstance(offset, int):
                return tt(mod[:, 48 + offset:54 + offset], bank[:, 7, 0:6], vec[:, b + 42 + offset:b + 48 + offset], ALU.add)
            return tt(mod[:, bass.ds(offset + 48, 6)], bank[:, 7, 0:6], vec[:, bass.ds(offset + (b + 42), 6)], ALU.add)

        def sum_before(self, loop):
            wait(te, (self.added, self.added.n, loop), (dve, dve.n + 1 - loop.per[dve], loop))
            self.columns(loop.i * 6 + 24 * self.half)

        def finish(self):
            wait(te, (self.added, self.added.n, None), (dve, dve.n, None))
            return self.columns(48)

    def mlp(layer, norm_x, h_hi, h_lo, u_hi, u_lo, sq, free, extra=None):
        inv = norm_x.end()
        ready = normalise(xT, inv, lambda k: gain[:, 16 * layer + 8 + k:16 * layer + 9 + k],
                          lambda k: modv(layer, 3, k), h_hi, h_lo)
        for half in range(2):
            more = extra.per if extra else {}
            own = {pe: 3, act: 8, dve: 8}
            with slab_loop(4, {**own, **{c: n + own.get(c, 0) for c, n in more.items()}}) as loop:
                relus = [(act, act.n + 2 * n + 1 - 8, loop) for n in range(4)]
                if extra:
                    extra.half = half
                    extra.load(loop, (0, 1))
                split_next()
                slab_products((h_hi[:, 0:4], h_lo[:, 0:4]), range(4), [[relus[n], *free] for n in range(4)],
                              ready[0:4] if half == 0 else None, True, False)
                if extra:
                    extra.sum_before(loop)
                split_next()
                if extra:
                    wait(ve, (extra.summed, extra.summed.n, loop))
                    extra.add(loop, (0, 1))
                    extra.load(loop, (2, 3))
                full = slab_products((h_hi[:, 4:8], h_lo[:, 4:8]), range(4), None,
                                     ready[4:8] if half == 0 else None, False, True)
                dbase = dve.n
                for n in range(4):
                    wait(se, full[n])
                    wait(se, (dve, dbase + max(2 * n - 3, 0), loop))
                    relu = act_(tmp[:, n % 2], bank[:, n], ACT.Relu)
                    wait(ve, relu)
                    squared = tt(sq[:, n], tmp[:, n % 2], tmp[:, n % 2], ALU.mult)
                    wait(se, squared)
                    tile = bass.ds(loop.i * 4 + n, 1)
                    made = act_(u_hi[:, tile, :], sq[:, n:n + 1], ACT.Copy)
                    wait(ve, made)
                    lo_done = tt(u_lo[:, tile, :], sq[:, n:n + 1], u_hi[:, tile, :].bitcast(F32), ALU.subtract)
                if extra:
                    extra.add(loop, (2, 3))
            end_loop(4)
            norm_next = Rms(xT, sq, (lo_done,)) if half else None

            def add_to_x(o, n):
                return stt(xT[:, o], bank[:, n], modv(layer, 5, o), xT[:, o], ALU.mult, ALU.add)

            marks = project(quarters(u_hi, u_lo, 4), 2, [[relu]] * 4, [[made, lo_done]] * 16, add_to_x, norm_next)
            free = [marks[-1]]
        return norm_next, marks

    split_next()
    early = ExitStack()
    h_hi, h_lo = (early.enter_context(sb(n, [P, DT, T], FR)) for n in ("h_hi", "h_lo"))
    wait(ve, *stage0_done)
    with sb("u_hi", [P, 16, T], FR) as u_hi, sb("u_lo", [P, 16, T], FR) as u_lo, sb("sq_b", [P, 4, T]) as sq, \
            sb("ada1_ring", [P, 2, 8, 192]) as ada1_ring, sb("ada1_acc", [P, 768]) as ada1_acc:
        extra = AdaSecond(ada1_ring, ada1_acc)
        norm_x = Rms(xT, sq, stage0_done)
        for m in x_ready:
            norm_x.add(m)
        norm_x, x_ready = mlp(0, norm_x, h_hi, h_lo, u_hi, u_lo, sq, stage0_done, extra)
        mod_ready = extra.finish()
        wait(ve, mod_ready)
        gains(16, 54 + 8, VEC_AT["norm_mix_g"] + 8)
        mod_ready = gains(24, 54 + 32, VEC_AT["norm_mlp_g"] + 8)
        wait(se, mod_ready)
        if stop == "mlp0":
            return dump(xT[:, :, :], x_ready)
        inv = norm_x.end()

    with sb("u", [P, DT, T]) as u, sb("v", [P, 4, D]) as v, sb("sq_c", [P, 4, T]) as sq, \
            sb("g_hi", [P, DT, T], FR) as g_hi, sb("g_lo", [P, DT, T], FR) as g_lo, \
            sb("ws", [P, DT, P]) as ws, sb("wsT", [P, DT, P]) as wsT, sb("bs_row", [1, D]) as bs_row, \
            sb("bs", [P, D]) as bs, sb("stats", [P, 4, 2, 6]) as stats, sb("mv", [P, 4, 2]) as mv:
        ws_in = nc.alloc_semaphore("ws_in")
        wait(ge, *x_ready, inv)
        ge.dma_start(ws[:, :, :], t["sgu_w_s"][0].rearrange("h t s -> t h s")).then_inc(ws_in, 16)
        ge.dma_start(bs_row[:, :], t["sgu_b_s"]).then_inc(ws_in, 16)
        wait(se, *x_ready, inv)
        ready = normalise(xT, inv, lambda k: gain[:, 16 + k:17 + k], lambda k: modv(1, 0, k), h_hi, h_lo)
        free = [[m] for m in x_ready[4:8]]
        h_moving = quarters(h_hi, h_lo, 2)
        u_ready = project(h_moving, 2, free, ready, lambda o, n: act_(u[:, o], bank[:, n], ACT.Gelu))
        v_made = project(h_moving, 2, [[m] for m in u_ready[4:8]], None,
                         lambda o, n: act_(v[:, n, 512 * (o // 4):512 * (o // 4) + 512], bank[:, n], ACT.Gelu),
                         weights_stationary=False)
        te.wait_ge(ws_in, 32)
        wait(te, *norm["read"])
        for hh in range(DT):
            mm = te.transpose(bank[:, 4 + hh // 4, P * (hh % 4):P * (hh % 4) + P], ws[:, hh], ident)
        turned = pe.after(mm)
        wait(ve, turned)
        masked = tt(wsT[:, :, :], bank[:, 4:6].rearrange("p b (h t) -> p (b h) t", h=4),
                    cst("tril_T").unsqueeze(1).broadcast_to([P, DT, P]), ALU.mult)
        for q in range(2):
            mm = te.matmul(bank[:, 6 + q], ones[0:1, :], bs_row[0:1, 512 * q:512 * q + 512], start=True, stop=True)
        spread = pe.after(mm)
        wait(se, spread)
        bs_ready = act_(bs[:, :], bank[:, 6:8].rearrange("p b n -> p (b n)"), ACT.Copy)
        wait(te, masked, bs_ready)
        for q in range(2):
            mm = te.matmul(bank[:, 6 + q], ones[:, :], wsT[:, 4 * q:4 * q + 4].rearrange("p h t -> p (h t)"),
                           start=True, stop=True)
        summed = pe.after(mm)
        wait(ve, summed, bs_ready)
        for hh in range(DT):
            part = slice(P * hh, P * hh + P)
            qs_ready = stt(bs[:, part], bank[:, 6 + hh // 4, P * (hh % 4):P * (hh % 4) + P],
                           col("sgu_ln_b", hh), bs[:, part], ALU.mult, ALU.add)
        v_ready = []
        for n in range(4):
            wait(ve, v_made[4 + n])
            for q in range(2):
                st = dve.after(ve.bn_stats(stats[:, n, q], v[:, n, 512 * q:512 * q + 512]))
            wait(ve, st)
            ag = dve.after(ve.bn_aggr(mv[:, n], stats[:, n]))
        wait(se, ag)
        root = act_(mv[:, :, 1:2], mv[:, :, 1:2], ACT.Sqrt, bias=eps[:, 1:2])
        wait(ve, root, ag)
        rec = dve.after(ve.reciprocal(mv[:, :, 1:2], mv[:, :, 1:2]))
        wait(ve, rec)
        for n in range(4):
            v_ready.append(ts(v[:, n], v[:, n], mv[:, n, 0:1], mv[:, n, 1:2], ALU.subtract, ALU.mult))
        wait(te, masked)
        wait(ve, qs_ready, *u_ready)
        gated, mix_free = [], [(), ()]
        for hh in range(DT):
            b = 4 + hh % 2
            wait(te, *mix_free[hh % 2])
            for n in range(4):
                if hh == 0:
                    wait(te, v_ready[n])
                mm = te.matmul(bank[:, b, P * n:P * n + P], v[:, n, P * hh:P * hh + P], wsT[:, hh],
                               start=True, stop=True)
            full_mix = pe.after(mm)
            wait(ve, full_mix)
            mixed = stt(tmp[:, hh % 2].rearrange("p (n t) -> p n t", n=4), bank[:, b].rearrange("p (n t) -> p n t", n=4),
                        col("sgu_ln_g", hh),
                        bs[:, P * hh:P * hh + P].unsqueeze(1).broadcast_to([P, 4, P]), ALU.mult, ALU.add)
            mix_free[hh % 2] = (mixed,)
            wait(ve, mixed)
            prod = tt(u[:, hh], u[:, hh], tmp[:, hh % 2], ALU.mult)
            gated.append(split_into(g_hi[:, hh], g_lo[:, hh], u[:, hh], [prod]))
        norm_x = Rms(xT, sq, (mixed,))
        x_ready = project(quarters(g_hi, g_lo, 2), 2, [[m] for m in v_made[4:8]], gated,
                          lambda o, n: stt(xT[:, o], bank[:, n], modv(1, 2, o), xT[:, o], ALU.mult, ALU.add), norm_x)
        if stop == "sgu":
            return dump(xT[:, :, :], x_ready)
        sgu_done = [x_ready[-1], norm_x.marks[-1]]
    with sb("u2_hi", [P, 16, T], FR) as u_hi, sb("u2_lo", [P, 16, T], FR) as u_lo, sb("sq_d", [P, 4, T]) as sq:
        wait(se, *sgu_done)
        wait(ve, *sgu_done)
        norm_x, x_ready = mlp(1, norm_x, h_hi, h_lo, u_hi, u_lo, sq, sgu_done)
        inv = norm_x.end()
        wait(ve, inv)
        free = [[x_ready[-1]]] * 4
        norm_x = Rms(xT, sq, (norm_x.marks[-1],))
        x_ready = []
        for k in range(DT):
            x_ready.append(stt(xT[:, k], xT[:, k], col("final_g", k), rstd_bank, ALU.mult, ALU.mult))
            norm_x.add(x_ready[-1])
        norm["read"] = [x_ready[-1]]
        if stop == "block1":
            return dump(xT[:, :, :], x_ready)
        inv = norm_x.end()
        ready = normalise(xT, inv, lambda k: col("norm_mix_pre_2", k), None, h_hi, h_lo)

    mixer = ExitStack()

    def ms(name, shape, dt=F32):
        return mixer.enter_context(nc.sbuf_tensor(name, shape, dt, side="right"))

    ar = ms("ar", [P, 4, 2, T])
    rT = ar[:, :, 1]
    kkT = ms("kkT", [P, 4, T])
    vvT = ms("vvT", [P, 4, T])
    attnT = ms("attnT", [P, 4, T])
    bT = ms("bT", [P, 4, T])
    gT = ms("gT", [P, 4, T])
    bonus = ms("bonus", [P, 4, T])
    pc = ms("pc", [P, 4, 8])
    one_less = ms("one_less", [P, 18])
    z_stack, q_stack = ExitStack(), ExitStack()
    cum = z_stack.enter_context(nc.sbuf_tensor("cum", [P, 4, T], F32, side="right"))
    inv_rows = z_stack.enter_context(nc.sbuf_tensor("inv_rows", [P, 4, 4, 2], F32, side="right"))
    zT = z_stack.enter_context(nc.sbuf_tensor("zT", [P, 2, T], F32, side="right"))
    qT = q_stack.enter_context(nc.sbuf_tensor("qT", [P, 4, T], F32, side="right"))
    kT = q_stack.enter_context(nc.sbuf_tensor("kT", [P, T], F32, side="right"))
    vT = q_stack.enter_context(nc.sbuf_tensor("vT", [P, T], F32, side="right"))
    made = ts(one_less[:, 0:14], vec[:, VEC_AT["rwkv_shift_mix_2"]:VEC_AT["rwkv_shift_mix_2"] + 14],
              -1.0, 1.0, ALU.mult, ALU.add)
    made = ts(one_less[:, 14:18], vec[:, VEC_AT["k_a_2"]:VEC_AT["k_a_2"] + 4], -1.0, 1.0, ALU.mult, ALU.add)
    wait(se, made)
    wait(ve, made)
    dest = [qT[:, i] for i in range(4)] + [kT[:, :], vT[:, :]] + [rT[:, i] for i in range(4)] + \
           [kkT[:, i] for i in range(4)] + [vvT[:, i] for i in range(4)] + [zT[:, i] for i in range(2)]
    proj = [None] * 20
    aT = gT
    sc = bonus
    normalised = [*ready[-1], norm_x.marks[-1], x_ready[-1]]
    lora_in = nc.alloc_semaphore("lora_in")
    bias_in = nc.alloc_semaphore("bias_in")
    lora = tmp
    bias_rev = attnT[:, :, :].rearrange("p i (h j) -> p (i h) j", h=2)
    spread_inv = qT[:, :, :].rearrange("p j (i d) -> p j i d", i=4)
    wait(ge, *normalised)
    wait(se, *normalised)
    wait(ve, *normalised)
    ge.dma_start(lora[0:64, 0], t["w_decay_up_2"]).then_inc(lora_in, 16)
    ge.dma_start(lora[64:128, 0], t["w_iclr_up_2"]).then_inc(lora_in, 16)
    ge.dma_start(lora[:, 1], t["w_gate_up_2"]).then_inc(lora_in, 16)
    ge.wait_ge(table_out, 16)
    ge.dma_start(bias_rev, bass.AP(tensor=t["scratch"].tensor, offset=0, ap=[[1, P], [384, 8], [1, 256]])).then_inc(bias_in, 16)

    R = {}

    def after_z():
        wait(se, *proj[18:20])
        R["z"] = (act_(zT[0:64, 0], zT[0:64, 0], ACT.Tanh), act_(zT[:, 1], zT[:, 1], ACT.Sigmoid))

    def turn_bias():
        te.wait_ge(bias_in, 16)
        wait(te, *proj)
        for q in range(4):
            mm = te.matmul(bank[:, q], cst("reverse"), bias_rev[:, 2 * q:2 * q + 2].rearrange("p h j -> p (h j)"),
                           start=True, stop=True)
        m = pe.after(mm)
        wait(ve, m)
        R["bias"] = dve.after(ve.tensor_copy(bias[:, :, :].rearrange("p (b h) j -> p b (h j)", b=4), bank[:, 0:4]))

    def loras():
        te.wait_ge(lora_in, 48)
        wait(te, *R["z"])
        for i in range(4):
            mm = te.matmul(bank[:, 4 + i], lora[0:64, 0, P * i:P * i + P], zT[0:64, 0], start=True, stop=True)
        m = pe.after(mm)
        wait(se, m)
        for i in range(4):
            d = act_(cum[:, i], bank[:, 4 + i], ACT.Sigmoid, bias=col("w0_2", i))
        R["d"] = d
        wait(ve, d)
        neg = ts(cum[:, :, :], cum[:, :, :], -EXP_M_HALF, None, ALU.mult)
        wait(ve, neg)
        for i in range(4):
            R["cum"] = dve.after(ve.tensor_tensor_scan(cum[:, i], cst("chunk_start"), cum[:, i], 0.0, ALU.mult, ALU.add))

    def rates():
        wait(te, R["d"])
        for i in range(4):
            mm = te.matmul(bank[:, 4 + i], lora[64:128, 0, P * i:P * i + P], zT[64:128, 0], start=True, stop=True)
        m = pe.after(mm)
        wait(se, m)
        for i in range(4):
            R["a"] = act_(aT[:, i], bank[:, 4 + i], ACT.Sigmoid, bias=col("a0_2", i))

    kk = ar[:, :, 0]

    def norms():
        wait(ve, *proj[10:14])
        for i in range(4):
            k0 = ts(kk[:, i], kkT[:, i], col("k_k_2", i), None, ALU.mult)
        wait(se, k0)
        s2 = act_(sc[:, :, :], kk, ACT.Square)
        wait(te, s2, R["a"])
        for j in range(4):
            for i in range(4):
                a = 8 * j + 2 * i
                mm = te.matmul(bank[:, 4, a:a + 2], sc[:, i, P * j:P * j + P], cst("head_ones")[:, 0:P:64],
                               start=True, stop=True)
        m = pe.after(mm)
        wait(se, m)
        rows2 = inv_rows[:, :, :, :].rearrange("p j i h -> p (j i h)")
        root = act_(rows2, bank[:, 4, 0:32], ACT.Sqrt)
        wait(ve, root)
        m = ts(rows2, rows2, 1e-12, None, ALU.max)
        wait(ve, m)
        m = dve.after(ve.reciprocal(rows2, rows2))
        wait(ve, m)
        m = dve.after(ve.tensor_copy(spread_inv.rearrange("p j i (h d) -> p (j i h) d", h=2),
                                     rows2.unsqueeze(2).broadcast_to([P, 32, 64])))
        R["spread"] = m
        R["root"] = root

    def norms_back():
        wait(te, R["spread"])
        for i in range(4):
            for j in range(4):
                mm = te.matmul(bank[:, 4 + i, P * j:P * j + P], spread_inv[:, j, i], ident, start=True, stop=True)
        m = pe.after(mm)
        wait(ve, m)
        R["kk"] = tt(kk, kk, bank[:, 4:8], ALU.mult)

    def keys():
        wait(ve, R["a"], R["root"])
        for i in range(4):
            m1 = ts(sc[:, i], aT[:, i], col("k_a_2", i), one_less[:, 14 + i:15 + i], ALU.mult, ALU.add)
        wait(ve, m1)
        R["k"] = tt(kkT[:, :, :], kkT[:, :, :], sc[:, :, :], ALU.mult)
        wait(ve, R["kk"])
        R["b"] = tt(bT[:, :, :], kk, aT[:, :, :], ALU.mult)

    def bonuses():
        wait(ve, R["k"], *proj[6:10])
        for i in range(4):
            m3 = stt(sc[:, i], rT[:, i], col("r_k_2", i), kkT[:, i], ALU.mult, ALU.mult)
        R["m3"] = m3
        wait(te, m3, R["kk"])
        for i in range(4):
            mm = te.matmul(bank[:, 4 + i], cst("head_ones"), sc[:, i], start=True, stop=True)
        m = pe.after(mm)
        wait(ve, m, *proj[14:18])
        R["bonus"] = tt(bonus[:, :, :], bank[:, 4:8], vvT[:, :, :], ALU.mult)

    kk4, cum4 = (a.rearrange("p i (c s) -> p i c s", s=64) for a in (kk, cum[:, :, :]))

    def exponentials():
        wait(se, R["b"], R["k"])
        R["e3"] = act_(aT[:, :, :], cum[:, :, :], ACT.Exp, scale=-1.0)
        wait(se, R["e3"])
        R["e1"] = act_(cum[:, :, :], cum[:, :, :], ACT.Exp)

    def with_decay():
        wait(ge, R["e3"])
        R["B"] = pool.after(ge.tensor_tensor(bT[:, :, :], bT[:, :, :], aT[:, :, :], ALU.mult))
        wait(ge, R["m3"])
        R["K"] = pool.after(ge.tensor_tensor(kkT[:, :, :], kkT[:, :, :], aT[:, :, :], ALU.mult))
        wait(ge, R["e1"])
        for i in range(4):
            R["A"] = pool.after(ge.tensor_tensor(kk4[:, i, :, 1:], kk4[:, i, :, 1:], cum4[:, i, :, 0:63], ALU.mult))
        R["R"] = pool.after(ge.tensor_tensor(rT, rT, cum[:, :, :], ALU.mult))
        R["pc"] = pool.after(ge.tensor_copy(pc[:, :, :], cum4[:, :, :, 63]))

    def gates():
        wait(te, R["bonus"])
        for i in range(4):
            mm = te.matmul(bank[:, 4 + i], lora[:, 1, P * i:P * i + P], zT[:, 1], start=True, stop=True)
        m = pe.after(mm)
        wait(se, m, R["K"])
        R["g"] = act_(gT[:, :, :], bank[:, 4:8], ACT.Copy)

    def evacuate(o, n):
        if o < 6:
            return act_(dest[o], bank[:, n], ACT.Copy, scale=0.125 if o < 4 else 1.0)
        here = act_(dest[o], bank[:, n], ACT.Copy, scale=one_less[:, o - 6:o - 5])
        wait(ve, here)
        return stt(dest[o][:, 1:], bank[:, n, 0:T - 1], col("rwkv_shift_mix_2", o - 6),
                   dest[o][:, 1:], ALU.mult, ALU.add)

    beside = {(1, 1): [loras], (2, 0): [rates], (3, 0): [norms], (3, 1): [norms_back],
              (4, 0): [keys], (4, 1): [exponentials, bonuses, with_decay]}
    for place, g in enumerate(PROJ_GROUPS):
        for k, m in enumerate(quarters(h_hi, h_lo, 2)):
            full = step(m, range(4), free, ready[4 * k:4 * k + 4] if place == 0 else None, k == 0, k == 1)
            for f in beside.get((place, k), ()):
                f()
        for n in range(4):
            wait(se, full[n])
            wait(ve, full[n])
            proj[4 * g + n] = evacuate(4 * g + n, n)
        free = [[proj[4 * g + n]] for n in range(4)]
        if place == 0:
            after_z()
    bank_free = [*proj[0:4]]
    proj_done = [*proj]
    early.close()
    softmax = ExitStack()
    bias, v_rows, scores, p_t, small = (
        softmax.enter_context(sb(n, shape)) for n, shape in
        (("bias", [P, 8, 256]), ("v_rows", [P, 4, P]), ("scores", [P, 2, 4, 256]), ("p_t", [P, 2, 2, 512]),
         ("small", [P, 2, 5, 4])))
    turn_bias()
    gates()

    wait(te, *proj_done, R["bias"])
    for n in range(4):
        mm = te.transpose(bank[:, 2, P * n:P * n + P], vT[:, P * n:P * n + P], ident)
    turned = pe.after(mm)
    wait(se, turned)
    wait(ve, *proj_done, R["bias"])
    v_ready = act_(v_rows[:, :, :], bank[:, 2].rearrange("p (n d) -> p n d", n=4), ACT.Copy)
    M = [{} for _ in range(8)]

    def read(it, what):
        return (M[it][what],) if it >= 0 else ()

    score_bank = (0, 6)

    def score(it):
        n, half = divmod(it, 2)
        j0 = 128 if n == 0 else 0
        r0 = 64 * half
        wait(te, *read(it - 2, "biased"))
        for i in range(4):
            mm = te.matmul(bank[:, score_bank[half] + i // 2, 256 * (i % 2) + j0:256 * (i % 2) + 256],
                           qT[r0:r0 + 64, i, P * n:P * n + P],
                           kT[r0:r0 + 64, P * n - P + j0:P * n + P], start=True, stop=True)
        M[it]["scored"] = pe.after(mm)

    def softmax_start(it):
        n, half = divmod(it, 2)
        j0 = 128 if n == 0 else 0
        m = M[it]
        s = scores[:, half, :, j0:]
        sm = small[:, half]
        b = score_bank[half]
        wait(ve, m["scored"], *read(it - 2, "turned"))
        m["biased"] = tt(s, bank[:, b:b + 2].rearrange("p b (i j) -> p (b i) j", i=2)[:, :, j0:],
                         bias[:, 4 * half:4 * half + 4, j0:], ALU.add)
        wait(ve, m["biased"])
        top = dve.after(ve.tensor_reduce(sm[:, 0], s, AX, ALU.max))
        wait(ve, top)
        top = tt(sm[:, 0], sm[:, 0], sink[:, 4 * half:4 * half + 4], ALU.max)
        wait(ve, top)
        tt(sm[:, 2], sink[:, 4 * half:4 * half + 4], sm[:, 0], ALU.subtract)
        neg = ts(sm[:, 1], sm[:, 0], -1.0, None, ALU.mult)
        wait(se, neg)
        for i in range(4):
            act_(scores[:, half, i, j0:], scores[:, half, i, j0:], ACT.Exp, bias=sm[:, 1, i:i + 1],
                 accum_out=sm[:, 3, i:i + 1])
        m["exps"] = act_(sm[:, 4], sm[:, 2], ACT.Exp)

    def take(it):
        n, half = divmod(it, 2)
        r0 = 64 * half
        wait(se, M[it]["summed"])
        M[it]["got"] = act_(attnT[r0:r0 + 64, :, P * n:P * n + P],
                            bank[r0:r0 + 64, 4 + half].rearrange("p (i t) -> p i t", i=4), ACT.Copy)

    def softmax_end(it):
        n, half = divmod(it, 2)
        j0 = 128 if n == 0 else 0
        r0, m = 64 * half, M[it]
        s = scores[:, half, :, j0:]
        sm = small[:, half]
        wait(ve, m["exps"])
        den = tt(sm[:, 3], sm[:, 3], sm[:, 4], ALU.add)
        wait(ve, den)
        rec = dve.after(ve.reciprocal(sm[:, 3], sm[:, 3]))
        wait(ve, rec)
        probs = tt(s, s, sm[:, 3].unsqueeze(2).broadcast_to([P, 4, 256 - j0]), ALU.mult)
        wait(te, probs, v_ready, *read(it - 1, "copied"))
        for q in range(j0 // 128, 2):
            for i in range(4):
                mm = te.transpose(bank[:, 2 + q, P * i:P * i + P], scores[:, half, i, P * q:P * q + P], ident)
        m["turned"] = pe.after(mm)
        if it < 6:
            score(it + 2)
        wait(se, m["turned"], *read(it - 2, "summed"))
        m["copied"] = act_(p_t[:, half, j0 // 128:2], bank[:, 2 + j0 // 128:4], ACT.Copy)
        if it:
            take(it - 1)
        wait(te, m["copied"], *read(it - 2, "got"))
        for q in range(j0 // 128, 2):
            mm = te.matmul(bank[r0:r0 + 64, 4 + half], v_rows[:, n - 1 + q, r0:r0 + 64], p_t[:, half, q],
                           start=q == j0 // 128, stop=q == 1)
        m["summed"] = pe.after(mm)

    score(0)
    wait(te, R["g"])
    score(1)
    softmax_start(0)
    for it in range(8):
        if it < 7:
            softmax_start(it + 1)
        softmax_end(it)
    take(7)
    attn_ready = [M[6]["got"], M[7]["got"]]
    softmax.close()
    if stop == "attn":
        return dump(attnT[:, :, :], attn_ready)
    q_stack.close()
    z_stack.close()
    bonus_ready, g_ready = R["bonus"], R["g"]
    ready = [*attn_ready, M[7]["copied"], M[7]["turned"], R["A"], R["B"], R["K"], R["R"], R["pc"], bonus_ready, g_ready]

    o_rows = ms("o_rows", [P, 4, 8, 64])
    with sb("kend", [P, 2, 4, P]) as kend, sb("rows", [P, 3, 4, P]) as rows_, sb("m_b", [P, 8, 2, P]) as m_b, \
            sb("m_k", [P, 8, 2, P]) as m_k, sb("xx", [P, 8, 2, P]) as xx, sb("ct", [P, 8, P]) as ct, \
            sb("t1", [P, 8, P]) as t1, sb("w", [P, 512]) as w, sb("zneg", [P, 512]) as zneg, \
            sb("state", [P, 4, P]) as state, sb("scaled", [P, 4, P]) as scaled:
        for e in (te, ve, se, ge):
            wait(e, *ready)
        zero = dve.after(ve.memset(state[:, :, :], 0.0))
        state_ready = [zero]
        all_free = []
        k_rows, b_rows, v_rows = rows_[:, 0], rows_[:, 1], rows_[:, 2]
        heads = [(4 * hp + i, slice(64 * hp, 64 * hp + 64), i) for hp in range(2) for i in range(4)]
        masks = cst("pair_masks").unsqueeze(1).broadcast_to([P, 2, 256])

        def per_head(a):
            return a.unsqueeze(1).broadcast_to([P, 4, P])

        def pair_products(stationary, first_bank, hp, tok):
            for g, rr, i in heads[4 * hp:4 * hp + 4]:
                mm = te.matmul(bank[:, first_bank + i // 2, 256 * (i % 2):256 * (i % 2) + 256],
                               stationary[rr, i, tok], ar[rr, i, :, tok], start=True, stop=True)
            return pe.after(mm)

        def masked_pairs(out_, first_bank, hp):
            for b in range(2):
                m = tt(out_[:, 4 * hp + 2 * b:4 * hp + 2 * b + 2].rearrange("p g a t -> p g (a t)"),
                       bank[:, first_bank + b].rearrange("p (g c) -> p g c", g=2), masks, ALU.mult)
            return m

        for j in range(4):
            tok = slice(P * j, P * j + P)
            wait(te, *all_free)
            wait(ve, *all_free)
            mb, mn = [None] * 2, [None] * 2
            for hp in range(2):
                made = pair_products(bT, 2 * hp, hp, tok)
                wait(ve, made)
                mb[hp] = masked_pairs(m_b, 2 * hp, hp)
            for hp in range(2):
                for g, rr, i in heads[4 * hp:4 * hp + 4]:
                    mm = te.matmul(bank[:, 4 + hp, P * i:P * i + P], ar[rr, i, 0, tok], bT[rr, i, tok], start=True, stop=True)
                mn[hp] = pe.after(mm)
            x_ready_ = [None, None]
            for hp in range(2):
                g4 = slice(4 * hp, 4 * hp + 4)
                wait(ve, mn[hp], mb[hp])
                a1 = tt(xx[:, g4, 0], bank[:, 4 + hp].rearrange("p (g t) -> p g t", g=4), per_head(cst("level0")), ALU.mult)
                a2 = tt(xx[:, g4, 1], m_b[:, g4, 0], per_head(cst("levels_T", 0, P)), ALU.mult)
                wait(ve, a1, a2)
                x_ready_[hp] = tt(xx[:, g4], ident.unsqueeze(1).unsqueeze(1).broadcast_to([P, 4, 2, P]), xx[:, g4], ALU.subtract)
            for q, src in enumerate((kkT, bT)):
                kend_ready = tt(kend[:, q].rearrange("p i (c s) -> p i c s", c=2),
                                src[:, :, tok].rearrange("p i (c s) -> p i c s", c=2),
                                pc[:, :, 2 * j:2 * j + 2].unsqueeze(3).broadcast_to([P, 4, 2, 64]), ALU.mult)
            marks = {"mk": [], "rows": []}

            def beside_level(level):
                if level in (1, 2):
                    hp = level - 1
                    wait(te, *marks["mk"])
                    made = pair_products(kkT, 6, hp, tok)
                    wait(ve, made)
                    marks["mk"] = [masked_pairs(m_k, 6, hp)]
                elif level == 3:
                    wait(te, kend_ready, *marks["mk"])
                    for q in range(2):
                        for i in range(4):
                            mm = te.transpose(bank[:, 6 + q, P * i:P * i + P], kend[:, q, i], ident)
                    turned = pe.after(mm)
                    wait(se, turned)
                    marks["rows"] = [act_(rows_[:, 0:2].rearrange("p q i d -> p q (i d)"), bank[:, 6:8], ACT.Copy)]
                elif level == 4:
                    wait(te, *marks["rows"])
                    for i in range(4):
                        mm = te.transpose(bank[:, 6, P * i:P * i + P], vvT[:, i, tok], ident)
                    turned = pe.after(mm)
                    wait(se, turned)
                    marks["rows"].append(act_(rows_[:, 2].rearrange("p i d -> p (i d)"), bank[:, 6], ACT.Copy))

            t_done, y_done = [(), ()], [(), ()]
            for level in range(1, 6):
                t_ready = [None, None]
                for hp in range(2):
                    g4 = slice(4 * hp, 4 * hp + 4)
                    wait(ge, mb[hp], *t_done[hp])
                    c_ready = pool.after(ge.tensor_tensor(ct[:, g4], m_b[:, g4, 0], per_head(cst("levels_T", P * level, P)), ALU.mult))
                    wait(te, c_ready, x_ready_[hp])
                    for i in range(4):
                        g = 4 * hp + i
                        mm = te.matmul(bank[:, hp, P * i:P * i + P], ct[:, g], xx[:, g, 0], start=True, stop=True)
                    t_done[hp] = (pe.after(mm),)
                    wait(se, *t_done[hp], *y_done[hp])
                    t_ready[hp] = act_(t1[:, g4].rearrange("p g t -> p (g t)"), bank[:, hp], ACT.Copy)
                for hp in range(2):
                    g4 = slice(4 * hp, 4 * hp + 4)
                    wait(te, t_ready[hp])
                    for i in range(4):
                        g, b = 4 * hp + i, 2 + 2 * hp + i // 2
                        if level < 5:
                            te.matmul(bank[:, b, 256 * (i % 2):256 * (i % 2) + P], xx[:, g, 1], t1[:, g], start=True, stop=True)
                        mm = te.matmul(bank[:, b, 256 * (i % 2) + P:256 * (i % 2) + 256], t1[:, g], xx[:, g, 1], start=True, stop=True)
                    y_done[hp] = (pe.after(mm),)
                    wait(ve, *y_done[hp])
                    y = bank[:, 2 + 2 * hp:4 + 2 * hp].rearrange("p b (g a t) -> p (b g) a t", g=2, a=2)
                    if level < 5:
                        x_ready_[hp] = tt(xx[:, g4], xx[:, g4], y, ALU.subtract)
                    else:
                        x_ready_[hp] = tt(xx[:, g4, 1], xx[:, g4, 1], y[:, :, 1], ALU.subtract)
                beside_level(level)

            wait(te, *marks["rows"], *marks["mk"], *x_ready_)
            for b, part in ((6, 0), (7, 0), (1, 1)):
                for i in range(4):
                    for hp in range(2):
                        cc = slice(P * i + 64 * hp, P * i + 64 * hp + 64)
                        te.matmul(bank[:, b, cc], m_k[:, 4 * hp + i, part], v_rows[:, i, 64 * hp:64 * hp + 64],
                                  start=i == 0 and hp == 0, stop=False, skip_group_check=True)
            halves = [slice(0, 64), slice(64, 128)]
            for cp in range(2):
                for i in range(4):
                    te.matmul(bank[:, 2 + cp, P * i:P * i + P], k_rows[halves[cp], i], v_rows[halves[cp], i],
                              start=i == 0, stop=False, skip_group_check=True)
            o_done = []
            for cp in range(2):
                half = halves[cp]
                wait(te, *state_ready)
                for i in range(4):
                    mm = te.matmul(bank[:, 6 + cp, P * i:P * i + P], ar[:, i, 0, tok], state[:, i], start=False, stop=i == 3, skip_group_check=True)
                w_done = pe.after(mm)
                for i in range(4):
                    mm = te.matmul(bank[:, 4 + cp, P * i:P * i + P], ar[:, i, 1, tok], state[:, i], start=True, stop=True)
                o_done.append(pe.after(mm))
                wait(se, w_done)
                w_ready = act_(w[:, :], bank[:, 6 + cp], ACT.Copy)
                wait(te, w_ready)
                if cp:
                    wait(te, z_ready)
                for i in range(4):
                    for hp in range(2):
                        cc = slice(P * i + 64 * hp, P * i + 64 * hp + 64)
                        mm = te.matmul(bank[:, 0, cc], xx[:, 4 * hp + i, 1], w[:, cc], start=True, stop=True)
                z_done = pe.after(mm)
                wait(se, z_done)
                z_ready = act_(zneg[half, :], bank[half, 0], ACT.Copy, scale=-1.0)
                c = 2 * j + cp
                wait(ve, *state_ready)
                keep = tt(scaled[:, :, :], state[:, :, :], pc[:, :, c:c + 1].broadcast_to([P, 4, P]), ALU.mult)
                wait(te, z_ready)
                for i in range(4):
                    mm = te.matmul(bank[:, 2 + cp, P * i:P * i + P], b_rows[half, i], zneg[half, P * i:P * i + P], start=False, stop=i == 3, skip_group_check=True)
                s_done = pe.after(mm)
                wait(ve, s_done, keep)
                state_ready = []
                for hp in range(2):
                    rr = slice(64 * hp, 64 * hp + 64)
                    state_ready.append(tt(state[rr, :, rr], scaled[rr, :, rr],
                                          bank[rr, 2 + cp].rearrange("p (i d) -> p i d", i=4)[:, :, rr], ALU.add))
            for i in range(4):
                for hp in range(2):
                    cc = slice(P * i + 64 * hp, P * i + 64 * hp + 64)
                    mm = te.matmul(bank[:, 1, cc], m_b[:, 4 * hp + i, 1], zneg[:, cc], start=False, stop=i == 3 and hp == 1, skip_group_check=True)
            inner = pe.after(mm)
            orow = o_rows[:, j].rearrange("p h d -> p (h d)")
            wait(se, *o_done)
            e = [act_(orow[halves[cp]], bank[halves[cp], 4 + cp], ACT.Copy) for cp in range(2)]
            wait(ve, inner, *e)
            o_sum = tt(orow, orow, bank[:, 1], ALU.add)
            all_free = [o_sum, *state_ready, inner, z_ready, *e]
            wait(ge, inner)
    if stop == "scan":
        return dump(o_rows[:, :, :, :].rearrange("p j h d -> p j (h d)"), all_free)

    m_hi = ms("m_hi", [P, DT, T], FR)
    m_lo = ms("m_lo", [P, DT, T], FR)
    with sb("o_sq", [P, 4, 8, 64]) as o_sq, sb("gs", [P, 2, 4, 8]) as gs, sb("oT", [P, 4, T]) as oT:
        o32, q32 = (a[:, :, :, :].rearrange("p j h d -> p (j h) d") for a in (o_rows, o_sq))
        mu, var = (gs[:, q].rearrange("p j h -> p (j h)") for q in range(2))

        def spread32(a):
            return a.unsqueeze(2).broadcast_to([P, 32, 64])

        wait(ve, *all_free)
        m = dve.after(ve.tensor_reduce(mu, o32, AX, ALU.add))
        wait(ve, m)
        m = ts(mu, mu, 1.0 / 64, None, ALU.mult)
        wait(ve, m)
        m = tt(o32, o32, spread32(mu), ALU.subtract)
        wait(se, m)
        s2 = act_(q32, o32, ACT.Square)
        wait(ve, s2)
        m = dve.after(ve.tensor_reduce(var, q32, AX, ALU.add))
        wait(se, m)
        root = act_(var, var, ACT.Sqrt, scale=1.0 / 64, bias=eps[:, 2:3])
        wait(ve, root)
        m = dve.after(ve.reciprocal(var, var))
        wait(ve, m)
        m = tt(o32, o32, spread32(var), ALU.mult)
        wait(te, m)
        for i in range(4):
            for j in range(4):
                mm = te.transpose(bank[:, 4 + i, P * j:P * j + P], o_rows[:, j].rearrange("p h d -> p (h d)")[:, P * i:P * i + P], ident)
            turned = pe.after(mm)
            wait(ve, turned)
            m = ts(oT[:, i], bank[:, 4 + i], col("ln_x_g_2", i), col("ln_x_b_2", i), ALU.mult, ALU.add)
        wait(ve, m, bonus_ready, g_ready)
        m = tt(oT[:, :, :], oT[:, :, :], bonus[:, :, :], ALU.add)
        wait(ve, m)
        m = tt(oT[:, :, :], oT[:, :, :], gT[:, :, :], ALU.mult)
        mix_ready = [split_into(m_hi[:, 0:4], m_lo[:, 0:4], attnT[:, :, :], attn_ready)] * 4
        mix_ready += [split_into(m_hi[:, 4:8], m_lo[:, 4:8], oT[:, :, :], [m])] * 4
    if stop == "mix":
        return dump(m_hi[:, :, :].bitcast(F32), mix_ready[7])

    with sb("mixed", [P, DT, T]) as mixed:
        sq = ar[:, :, :, :].rearrange("p i a t -> p (i a) t")
        wait(se, *mix_ready[7])
        wait(te, *all_free)
        norm_mix = Rms(mixed, sq, ())
        mixed_ready = project(quarters(m_hi, m_lo, 2), 2, [[turned, m]] * 4, mix_ready,
                              lambda o, n: act_(mixed[:, o], bank[:, n], ACT.Copy), norm_mix)
        inv = norm_mix.end()
        wait(ve, inv)
        norm_x = Rms(xT, sq, (norm_mix.marks[-1],))
        x_ready = []
        for k in range(DT):
            m = stt(mixed[:, k], mixed[:, k], col("norm_mix_post_2", k), rstd_bank, ALU.mult, ALU.mult)
            wait(ve, m)
            x_ready.append(tt(xT[:, k], xT[:, k], mixed[:, k], ALU.add))
            norm_x.add(x_ready[-1])
        norm["read"] = [m]
        inv = norm_x.end()
        mixer_done = [x_ready[-1], norm_x.marks[-1]]
        if stop == "mixer":
            return dump(xT[:, :, :], x_ready)
    mixer.close()
    if stop == "mixer":
        return dump(xT[:, :, :], [m[0] for m in x_ready])

    with sb("f_hi", [P, DT, T], FR) as h_hi, sb("f_lo", [P, DT, T], FR) as h_lo, \
            sb("u3_hi", [P, 16, T], FR) as u_hi, sb("u3_lo", [P, 16, T], FR) as u_lo, sb("f", [P, DT, T]) as f, \
            sb("conv", [P, 4, T]) as conv:
        wait(te, *mixer_done)
        wait(se, *mixer_done)
        ready = normalise(xT, inv, lambda k: col("norm_ffn_pre_2", k), None, h_hi, h_lo)
        free = [[mixer_done[0]]] * 4
        CW, CB = VEC_AT["conv_w_2"], VEC_AT["conv_b_2"]
        f_ready = [None] * DT
        for half in range(2):
            with slab_loop(8, {pe: 3, act: 8, dve: 12}) as loop:
                split_next()
                earlier = [(dve, dve.n + 2 * n + 2 - 12, loop) for n in range(4)]
                last_lo = (dve, dve.n, loop)
                slab_products((h_hi[:, 0:4], h_lo[:, 0:4]), range(4), [[earlier[n], *free[n]] for n in range(4)],
                              ready[0:4] if half == 0 else None, True, False)
                split_next()
                full = slab_products((h_hi[:, 4:8], h_lo[:, 4:8]), range(4), None, ready[4:8] if half == 0 else None, False, True)
                conv_done = []
                for n in range(4):
                    place = loop.i * 2 + (16 * half + 32 * (n // 2) + n % 2)

                    def cw(tap):
                        return vec[:, bass.ds(place + (CW + 64 * tap), 1)]

                    wait(se, full[n], last_lo)
                    here = act_(conv[:, n], bank[:, n], ACT.Identity, scale=cw(2), bias=vec[:, bass.ds(place + CB, 1)])
                    wait(ve, here)
                    one = stt(conv[:, n, 1:], bank[:, n, 0:T - 1], cw(1), conv[:, n, 1:], ALU.mult, ALU.add)
                    wait(ve, one)
                    conv_done.append(stt(conv[:, n, 2:], bank[:, n, 0:T - 2], cw(0), conv[:, n, 2:], ALU.mult, ALU.add))
                for n in range(2):
                    tile = bass.ds(loop.i * 2 + n, 1)
                    wait(se, conv_done[n])
                    act_gate = act_(conv[:, n], conv[:, n], ACT.Gelu_apprx_tanh)
                    wait(ve, act_gate, conv_done[2 + n])
                    prod = tt(conv[:, n], conv[:, n], conv[:, 2 + n], ALU.mult)
                    wait(se, prod)
                    made = act_(u_hi[:, tile, :], conv[:, n:n + 1], ACT.Copy)
                    wait(ve, made)
                    lo_done = tt(u_lo[:, tile, :], conv[:, n:n + 1], u_hi[:, tile, :].bitcast(F32), ALU.subtract)
            end_loop(8)
            norm_f = Rms(f, conv, (lo_done,)) if half else None

            def add_to_f(o, n):
                if half == 0:
                    return dve.after(ve.tensor_copy(f[:, o], bank[:, n]))
                return tt(f[:, o], f[:, o], bank[:, n], ALU.add)

            f_ready = project(quarters(u_hi, u_lo, 4), 2, [[conv_done[n]] for n in range(4)],
                              [[made, lo_done]] * 16, add_to_f, norm_f)
            free = [[m] for m in f_ready[4:8]]
    finish = ExitStack()
    sqf = finish.enter_context(nc.sbuf_tensor("sq_f", [P, DT, T], F32))
    rows_out = finish.enter_context(nc.sbuf_tensor("rows_out", [P, 4, D], F32))
    inv = norm_f.end()
    wait(ve, inv)
    turned_free = [None, None]
    x_ready = []
    for k in range(DT):
        m = stt(f[:, k], f[:, k], col("norm_ffn_post_2", k), rstd_bank, ALU.mult, ALU.mult)
        wait(ve, m)
        x_ready.append(tt(xT[:, k], xT[:, k], f[:, k], ALU.add))
    for k in range(DT):
        wait(te, x_ready[k])
        if turned_free[k % 2]:
            wait(te, turned_free[k % 2])
        for j in range(4):
            mm = te.transpose(bank[:, 6 + k % 2, P * j:P * j + P], xT[:, k, P * j:P * j + P], ident)
        turned = pe.after(mm)
        wait(se, turned)
        turned_free[k % 2] = act_(rows_out[:, :, P * k:P * k + P], bank[:, 6 + k % 2].rearrange("p (j f) -> p j f", j=4), ACT.Copy)
    stored = nc.alloc_semaphore("stored")
    wait(sy, turned_free[0], turned_free[1])
    sy.dma_start(out[0].rearrange("(j p) n -> p j n", p=P), rows_out[:, :, :]).then_inc(stored, 16)
    sy.wait_ge(stored, 16)


WEIGHTS = ["ada_w", "pool_w", "sgu_w_in", "sgu_w_s", "sgu_b_s", "sgu_w_out", "mlp_w1", "mlp_w2",
           "w_decay_up_2", "w_iclr_up_2", "w_gate_up_2", "w_out_2", "w_ffn_up_2", "w_ffn_down_2", "w_in_2",
           "rel_bias_2", "sinks_2"]
ONE_LAYER = ["sgu_w_in", "sgu_w_out", "w_decay_up_2", "w_iclr_up_2", "w_gate_up_2", "w_out_2",
             "w_ffn_up_2", "w_ffn_down_2", "w_in_2"]


def laid_out(inputs):
    arrays = {n: np.asarray(inputs[n]) for n in WEIGHTS}
    arrays["x"] = np.asarray(inputs["x"])
    for n in ONE_LAYER:
        arrays[n] = arrays[n][0]
    heads = np.concatenate([np.arange(64) + 64 * h for i in range(4) for h in (i, i + 4)])
    w_in, w_out = arrays["w_in_2"].copy(), arrays["w_out_2"].copy()
    w_in[:, :512] = arrays["w_in_2"][:, heads]
    w_out[:512] = arrays["w_out_2"][heads]
    arrays["w_in_2"], arrays["w_out_2"] = w_in, w_out
    flat = np.concatenate([np.asarray(inputs[n]).ravel() for n, _ in VECS])
    arrays["vecs"] = np.concatenate([flat, np.zeros(512 * P - flat.size, flat.dtype)]).reshape(512, P)
    arrays["const"], arrays["buckets"] = constants()
    return {n: np.ascontiguousarray(a) for n, a in arrays.items()}


def declared(nc, arrays):
    t = {n: nc.dram_tensor(f"in_{n}", a.shape, mybir.dt.from_np(a.dtype), kind="ExternalInput").ap()
         for n, a in arrays.items()}
    t["scratch"] = nc.dram_tensor("bias_table", (8, 384), F32, kind="Internal").ap()
    return t, nc.dram_tensor("out", (1, T, D), F32, kind="ExternalOutput").ap()


def kernel(**inputs):
    import concourse.bacc as bacc
    from concourse.bass_utils import run_bass_kernel_spmd
    arrays = laid_out(inputs)
    nc = bacc.Bacc("TRN2", target_bir_lowering=False, num_devices=1)
    program(nc, *declared(nc, arrays))
    r = run_bass_kernel_spmd(nc, [{f"in_{n}": a for n, a in arrays.items()}], core_ids=[0])
    return r.results[0]["out"]
```

```python
import math
from contextlib import ExitStack

import numpy as np

import concourse.bass as bass
from concourse import mybir

F32 = mybir.dt.float32
FR = mybir.dt.float32r
ACT = mybir.ActivationFunctionType
ALU = mybir.AluOpType
AX = mybir.AxisListType.X
PE, ACTE, DVE, SP = (mybir.EngineType.PE, mybir.EngineType.Activation, mybir.EngineType.DVE,
                     mybir.EngineType.SP)

P = 128
D = 1024
DT = D // P
T = 512
DFF = 4096
POOL_WINDOWS = (2, 4, 8, 16)
RMS_EPS = 1e-6
LN_EPS = 1e-5
GN_EPS = 64e-5
EXP_M_HALF = math.exp(-0.5)
MASKED = -1e30

VECS = [("c", 8), ("ada_b", 96), ("norm_mix_g", 16), ("norm_mlp_g", 16), ("pool_scale", 8),
        ("sgu_ln_g", 8), ("sgu_ln_b", 8), ("final_g", 8), ("norm_mix_pre_2", 8),
        ("norm_mix_post_2", 8), ("norm_ffn_pre_2", 8), ("norm_ffn_post_2", 8),
        ("rwkv_shift_mix_2", 14), ("w0_2", 4), ("a0_2", 4), ("k_k_2", 4), ("k_a_2", 4),
        ("r_k_2", 4), ("ln_x_g_2", 4), ("ln_x_b_2", 4), ("conv_w_2", 192), ("conv_b_2", 64)]
VEC_AT = {}
_at = 0
for _name, _rows in VECS:
    VEC_AT[_name] = _at
    _at += _rows
assert _at <= 512

CONSTS = [("ident", 128), ("head_ones", 128), ("reverse", 128), ("tril_T", 128), ("level0", 128),
          ("levels_T", 6 * 128), ("pair_masks", 256), ("chunk_start", 512), ("pool_inv", 64)]
CONST_AT = {}
_at = 0
for _name, _cols in CONSTS:
    CONST_AT[_name] = _at
    _at += _cols
CONST_COLS = _at


def constants():
    r = np.arange(P)
    row, col = r[:, None], r[None, :]
    out = np.zeros((P, CONST_COLS), np.float32)

    def put(name, a, k=0):
        out[:, CONST_AT[name] + k:CONST_AT[name] + k + a.shape[1]] = a

    same = row // 64 == col // 64
    put("ident", row == col)
    put("head_ones", same)
    put("reverse", row + col == P - 1)
    put("tril_T", row <= col)

    def lower(b):
        return (row // (2 * b) == col // (2 * b)) & (row % (2 * b) >= b) & (col % (2 * b) < b)

    put("level0", lower(1))
    for n in range(6):
        put("levels_T", lower(2 ** n).T, n * P)
    put("pair_masks", same & (row < col))
    put("pair_masks", same & (row <= col), P)
    put("chunk_start", np.broadcast_to(np.arange(T) % 64 != 0, (P, T)))
    t = np.arange(16)
    for g, w in enumerate(POOL_WINDOWS):
        put("pool_inv", np.broadcast_to((1.0 / np.minimum(t + 1.0, w)).astype(np.float32), (P, 16)), 16 * g)

    table = np.zeros((33, 384), np.float32)
    for i in range(383):
        rel = 255 - i
        if 0 <= rel < 128:
            n = np.float32(max(rel, 1))
            large = 16 + int(np.float32(np.log(n / np.float32(16))) / np.float32(math.log(8)) * np.float32(16)) \
                if rel >= 16 else 0
            table[rel if rel < 16 else min(large, 31), i] = 1
        else:
            table[32, i] = 1
    return out, table


class Counter:

    def __init__(self, nc, name):
        self.sem = nc.alloc_semaphore(name)
        self.n = 0
        self.loop = None

    def after(self, ins, by=1):
        ins.then_inc(self.sem, by)
        self.n += by
        return (self, self.n, self.loop)


class Loop:

    def __init__(self, nc, turns, per, engines):
        self.nc, self.turns, self.per, self.engines = nc, turns, per, engines

    def __enter__(self):
        self.base = {c: c.n for c in self.per}
        for c in self.per:
            c.loop = self
        self.fori = self.nc.Fori(0, self.turns, engines=self.engines)
        self.i = self.fori.__enter__()
        return self

    def __exit__(self, *e):
        self.fori.__exit__(*e)
        if e[0]:
            return
        for c, per in self.per.items():
            assert c.n == self.base[c] + per, (c.sem, c.n - self.base[c], per)
            c.n = self.base[c] + per * self.turns
            c.loop = None


def wait(eng, *marks):
    for counter, n, loop in marks:
        if loop is not None and counter.loop is loop:
            eng.wait_ge(counter.sem, loop.i * loop.per[counter] + n)
        elif loop is not None:
            eng.wait_ge(counter.sem, n + loop.per[counter] * (loop.turns - 1))
        else:
            eng.wait_ge(counter.sem, n)


def before(mark):
    counter, n, loop = mark
    return (counter, n - loop.per[counter], loop)


def program(nc, t, out):
    pe, act, dve, pool = (Counter(nc, n) for n in ("pe_done", "act_done", "dve_done", "pool_done"))
    hi_made, lo_made, slab_used = (Counter(nc, n) for n in ("hi_made", "lo_made", "slab_used"))
    landed = [nc.alloc_semaphore(f"slab_landed{i}") for i in range(2)]
    te, se, ve, ge, sy = nc.tensor, nc.scalar, nc.vector, nc.gpsimd, nc.sync
    te.sem_inc(slab_used.sem, 1)
    slab_used.n = 1

    def sb(name, shape, dt=F32):
        return nc.sbuf_tensor(name, shape, dt)

    def alloc(name, shape, dt=F32):
        return nc.alloc_sbuf_tensor(name, shape, dt)

    xT = alloc("xT", [P, DT, T])
    raw = alloc("raw", [P, 2, 4, 512])
    w_hi = alloc("w_hi", [P, 2, 4, 512], FR)
    w_lo = alloc("w_lo", [P, 2, 4, 512], FR)
    const = alloc("const", [P, CONST_COLS])
    vec = alloc("vec", [P, 512])
    mod = alloc("mod", [P, 48 + 6 + 48])
    gain = alloc("gain", [P, 48])
    rstd_diag = alloc("rstd_diag", [P, 4, P])
    rstd_rows = alloc("rstd_rows", [P, 4])
    tmp = alloc("tmp", [P, 2, T])
    sink = alloc("sink", [P, 8])
    c_act = alloc("c_act", [P, DT])
    mean_ones = alloc("mean_ones", [P, P])
    ones = alloc("ones", [P, P])
    eps = alloc("eps", [P, 3])
    bank = nc.alloc_psum_tensor("bank", [P, 8, 512], F32)

    def cst(name, k=0, n=None):
        a = CONST_AT[name] + k
        return const[:, a:a + (n or dict(CONSTS)[name])]

    def col(name, k):
        return vec[:, VEC_AT[name] + k:VEC_AT[name] + k + 1]

    ident = cst("ident")

    slabs = {"sent": 0, "split": 0, "used": 0}

    def send(src, index=None):
        s = slabs["sent"]
        if index is None:
            if s >= 2:
                sy.wait_ge(hi_made.sem, s - 1)
                sy.wait_ge(lo_made.sem, s - 1)
        else:
            sy.wait_ge(hi_made.sem, index * 2 + (s - 1))
            sy.wait_ge(lo_made.sem, index * 2 + (s - 1))
        parts = src if isinstance(src, list) else [(slice(0, 512), src)]
        if len(parts) == 1:
            a = parts[0][1]
            parts = [(0, 2, slice(0, 512), a[:, 0:2]), (2, 4, slice(0, 512), a[:, 2:4])]
        else:
            parts = [(0, 4, c, a) for c, a in parts]
        for k0, k1, c, a in parts:
            sy.dma_start(raw[:, s % 2, k0:k1, c], a).then_inc(landed[s % 2], 16)
        slabs["sent"] += 1

    def rows(w, k, cols):
        return w[512 * k:512 * k + 512, cols].rearrange("(k p) n -> p k n", p=P)

    def send_linear(w, kslabs, groups, k0=0):
        for g in groups:
            for k in range(kslabs):
                send(rows(w, k0 + k, slice(512 * g, 512 * g + 512)))

    def send_loop(turns, source):
        s0 = slabs["sent"]
        if s0 == 0:
            for k in range(2):
                send(source(k, 0))
            slabs["sent"] = 0
        with nc.Fori(1 if s0 == 0 else 0, turns, engines=[SP]) as i:
            for k in range(2):
                send(source(k, i), index=i)
        slabs["sent"] = s0 + 2 * turns

    def split_next():
        s = slabs["split"]
        slot = s % 2
        loop = hi_made.loop
        i = 0 if loop is None else loop.i
        for eng in (se, ve):
            eng.wait_ge(landed[slot], i * 32 + 32 * (s // 2 + 1))
            if s >= 1:
                eng.wait_ge(slab_used.sem, i * 2 + s)
        made = hi_made.after(se.activation(w_hi[:, slot], raw[:, slot], ACT.Copy))
        wait(ve, made)
        lo_made.after(ve.tensor_tensor(w_lo[:, slot], raw[:, slot], w_hi[:, slot].bitcast(F32), ALU.subtract))
        slabs["split"] += 1

    TOTAL_SLABS = 2 * 32 + 8 + 4 + 10 + 4 + 32 + 16

    def slab_products(moving, banks, free, ready, first, last, weights_stationary=True):
        s = slabs["used"]
        slot = s % 2
        loop = slab_used.loop
        i = 0 if loop is None else loop.i
        te.wait_ge(hi_made.sem, i * 2 + (s + 1))
        te.wait_ge(lo_made.sem, i * 2 + (s + 1))
        hi, lo = moving
        full = []
        order = [(n, k) for k in range(4) for n in range(4)] if ready is not None and first and loop is None else \
            [(n, k) for n in range(4) for k in range(4)]
        for n, k in order:
            tile = slice(P * n, P * n + P)
            if first and k == 0:
                wait(te, *free[n])
            if n == 0 and ready is not None:
                wait(te, *ready[k])
            if weights_stationary:
                three = ((w_hi[:, slot, k, tile], hi[:, k]), (w_hi[:, slot, k, tile], lo[:, k]),
                         (w_lo[:, slot, k, tile], hi[:, k]))
            else:
                three = ((hi[:, k, tile], w_hi[:, slot, k]), (hi[:, k, tile], w_lo[:, slot, k]),
                         (lo[:, k, tile], w_hi[:, slot, k]))
            for j, (a, b) in enumerate(three):
                mm = te.matmul(bank[:, banks[n]], a, b, start=first and k == 0 and j == 0,
                               stop=last and k == 3 and j == 2)
            if last and k == 3 and n < 3:
                full.append(pe.after(mm))
        full.append(slab_used.after(mm))
        slabs["used"] += 1
        return full

    def step(*args, **kw):
        if slabs["split"] < TOTAL_SLABS and slabs["split"] < slabs["used"] + 2:
            split_next()
        return slab_products(*args, **kw)

    def slab_loop(turns, per):
        per = {**per, hi_made: 2, lo_made: 2, slab_used: 2}
        return Loop(nc, turns, per, [PE, ACTE, DVE])

    def end_loop(turns):
        for k in ("split", "used"):
            slabs[k] += 2 * (turns - 1)

    PROJ_GROUPS = (4, 2, 3, 1, 0)

    def all_slabs():
        for layer in range(2):
            if layer == 1:
                send_linear(t["sgu_w_in"], 2, range(4))
                send_linear(t["sgu_w_out"], 2, range(2))
            for half in range(2):
                w1, w2 = t["mlp_w1"][layer], t["mlp_w2"][layer]
                send_loop(4, lambda k, i: w1[512 * k:512 * k + 512, bass.ds(i * 512 + 2048 * half, 512)]
                          .rearrange("(k p) n -> p k n", p=P))
                send_linear(w2, 4, range(2), k0=4 * half)
        send_linear(t["w_in_2"], 2, PROJ_GROUPS)
        send_linear(t["w_out_2"], 2, range(2))
        for half in range(2):
            w = t["w_ffn_up_2"]
            send_loop(8, lambda k, i: [
                (slice(256 * v, 256 * v + 256),
                 w[512 * k:512 * k + 512, bass.ds(i * 256 + (2048 * half + DFF * v), 256)]
                 .rearrange("(k p) n -> p k n", p=P)) for v in range(2)])
            send_linear(t["w_ffn_down_2"], 4, range(2), k0=4 * half)
        assert slabs["sent"] == TOTAL_SLABS

    def act_(*a, **k):
        return act.after(se.activation(*a, **k))

    def tt(o, a, b, op):
        return dve.after(ve.tensor_tensor(o, a, b, op))

    def ts(o, a, s1, s2, op0, op1=None):
        return dve.after(ve.tensor_scalar(o, a, s1, s2, op0, op1) if op1 else ve.tensor_scalar(o, a, s1, None, op0))

    def stt(o, a, s, b, op0, op1):
        return dve.after(ve.scalar_tensor_tensor(out=o, in0=a, scalar=s, in1=b, op0=op0, op1=op1))

    rstd_bank = bank[:, 5]
    norm = {"read": []}

    class Rms:

        def __init__(self, src, sq, free=(), on_pool=False):
            self.src, self.sq, self.k, self.marks, self.added, self.on_pool = src, sq, 0, [], [], on_pool
            wait(se, *free)
            wait(ge if on_pool else ve, *free)

        def add(self, *ready):
            k, total = self.k, self.sq[:, 3]
            wait(se, *ready)
            if k >= 4:
                wait(se, self.added[k - 3])
            place = self.sq[:, (k - 1) % 3] if k else total
            m = act_(place, self.src[:, k], ACT.Square)
            if k:
                wait(ge if self.on_pool else ve, m, self.added[-1])
                m = pool.after(ge.tensor_tensor(total, total, place, ALU.add)) if self.on_pool else \
                    tt(total, total, place, ALU.add)
            self.added.append(m)
            self.k += 1
            if self.k == DT:
                wait(te, m)
                for j in range(4):
                    mm = te.matmul(bank[:, 4, j:j + 1], total[:, P * j:P * j + P], mean_ones[:, 0:1],
                                   start=True, stop=True)
                self.marks.append(pe.after(mm))

        def end(self):
            wait(se, self.marks[-1])
            root = act_(rstd_rows[:, :], bank[:, 4, 0:4], ACT.Sqrt, bias=eps[:, 0:1])
            wait(ve, root)
            inv = dve.after(ve.reciprocal(rstd_rows[:, :], rstd_rows[:, :]))
            wait(ve, inv)
            diag = tt(rstd_diag[:, :, :], ident.unsqueeze(1).broadcast_to([P, 4, P]),
                      rstd_rows[:, :].unsqueeze(2).broadcast_to([P, 4, P]), ALU.mult)
            wait(te, diag, *norm["read"])
            return pe.after(te.matmul(rstd_bank, ones[:, :], rstd_diag[:, :, :].rearrange("p j t -> p (j t)"),
                                      start=True, stop=True))

    def normalise(src, inv, g, shift, hi, lo, tiles=DT, free=()):
        done = []
        wait(se, *free)
        wait(ve, *free)
        wait(ve, inv)

        def scale(k):
            if k >= 2:
                wait(ve, *done[k - 2])
            return stt(tmp[:, k % 2], src[:, k], g(k), rstd_bank, ALU.mult, ALU.mult)

        scaled = scale(0)
        for k in range(tiles):
            wait(se, scaled)
            if shift:
                made = act_(hi[:, k], tmp[:, k % 2], ACT.Identity, bias=shift(k))
            else:
                made = act_(hi[:, k], tmp[:, k % 2], ACT.Copy)
            this = scaled
            if k + 1 < tiles:
                scaled = scale(k + 1)
            wait(ve, this, made)
            if shift:
                rest = stt(lo[:, k], tmp[:, k % 2], shift(k), hi[:, k].bitcast(F32), ALU.add, ALU.subtract)
            else:
                rest = tt(lo[:, k], tmp[:, k % 2], hi[:, k].bitcast(F32), ALU.subtract)
            done.append((made, rest))
        norm["read"] = [scaled]
        return done

    def split_into(hi, lo, src, ready):
        wait(se, *ready)
        made = act_(hi, src, ACT.Copy)
        wait(ve, made, *ready)
        return (made, tt(lo, src, hi.bitcast(F32), ALU.subtract))

    def modv(layer, part, k):
        a = 54 * layer + 8 * part + k
        return mod[:, a:a + 1]

    ident_in, const_in, x_in, vec_in, pool_w_in = (nc.alloc_semaphore(n) for n in ("ident_in", "const_in", "x_in", "vec_in", "pool_w_in"))
    ADA_RING = 4
    ada_landed = [nc.alloc_semaphore(f"ada_landed{i}") for i in range(ADA_RING)]
    with sb("x_rows", [P, 4, D]) as x_rows, sb("vec_rows", [P, 4, P]) as vec_rows, \
            sb("ada_ring", [P, ADA_RING - 1, 8, 512]) as ada_ring, sb("ada_acc", [P, 2, 512]) as ada_acc, \
            sb("ada_row", [1, 2, 512]) as ada_row, sb("h", [P, DT, 16 + T]) as h, \
            sb("sums", [P, 2, 2, 16 + T]) as sums, sb("pooled", [P, DT, T]) as pooled, \
            sb("pool_w", [P, 4, 2, 256]) as pool_w, sb("rel", [33, 8]) as rel:
        sy.dma_start(const[:, 0:P], t["const"][:, 0:P]).then_inc(ident_in, 16)
        sy.dma_start(vec_rows[:, :, :], t["vecs"].rearrange("(j p) n -> p j n", p=P)).then_inc(vec_in, 16)
        se.dma_start(x_rows[:, :, :], t["x"][0].rearrange("(j p) n -> p j n", p=P)).then_inc(x_in, 16)
        se.dma_start(const[:, P:], t["const"][:, P:]).then_inc(const_in, 16)
        rel_in, table_out = (nc.alloc_semaphore(n) for n in ("rel_in", "table_out"))
        buckets, table = pooled[0:33, 6, 0:384], pooled[0:8, 7, 0:384]
        outside = dve.after(ve.memset(rel[32:33, :], MASKED))
        ge.dma_start(rel[0:32, :], t["rel_bias_2"]).then_inc(rel_in, 16)
        ge.dma_start(buckets, t["buckets"]).then_inc(rel_in, 16)
        ge.dma_start(sink[:, :], t["sinks_2"].broadcast_to([P, 8])).then_inc(rel_in, 16)
        ge.dma_start(pool_w[:, :, :, :].rearrange("p g k n -> p (g k) n"),
                     t["pool_w"][0].rearrange("g (k p) n -> p (g k) n", p=P)).then_inc(pool_w_in, 16)
        ve.memset(mean_ones[:, :], 1.0 / D)
        for i, e in enumerate((RMS_EPS, LN_EPS, GN_EPS)):
            ve.memset(eps[:, i:i + 1], e)
        ve.memset(h[:, :, 0:16], 0.0)
        sums_zero = dve.after(ve.memset(sums[:, :, :, 0:16], 0.0))
        set_up = dve.after(ve.memset(ones[:, :], 1.0))
        te.wait_ge(ident_in, 16)
        te.wait_ge(vec_in, 16)
        for j in range(4):
            mm = te.transpose(bank[:, 7, P * j:P * j + P], vec_rows[:, j], ident)
        turned = pe.after(mm)
        wait(ve, turned)
        ve.wait_ge(ident_in, 16)
        vec_ready = dve.after(ve.tensor_copy(vec[:, :], bank[:, 7]))
        wait(se, vec_ready, set_up)
        silu = act_(c_act[:, :], vec[:, VEC_AT["c"]:VEC_AT["c"] + 8], ACT.Silu)
        te.wait_ge(x_in, 16)
        wait(te, set_up)
        norm_x = Rms(xT, pooled[:, 0:4], on_pool=True)
        copied = []
        for k in range(DT):
            if k >= 2:
                wait(te, copied[k - 2])
            for j in range(4):
                mm = te.transpose(bank[:, k % 2, P * j:P * j + P], x_rows[:, j, P * k:P * k + P], ident)
            turned = pe.after(mm)
            wait(se, turned)
            copied.append(act_(xT[:, k], bank[:, k % 2], ACT.Copy))
        x_turned = turned

        def ada_slot(g):
            n = g % ADA_RING
            return ada_ring[:, n] if n < ADA_RING - 1 else x_rows[:, :, :].rearrange("p j (a n) -> p (j a) n", a=2)


        used = [None] * 12
        acc_used = []

        def ada_arrives(eng, g):
            eng.wait_ge(ada_landed[g % ADA_RING], 16 * (g // ADA_RING + 1))

        def ada_on_dve(g):
            ada_arrives(ve, g)
            wait(ve, silu)
            a = ada_acc[:, len(acc_used) % 2]
            if len(acc_used) >= 2:
                wait(ve, acc_used[-2])
            m = ts(a, ada_slot(g)[:, 0], c_act[:, 0:1], None, ALU.mult)
            for k in range(1, 8):
                wait(ve, m)
                m = stt(a, ada_slot(g)[:, k], c_act[:, k:k + 1], a, ALU.mult, ALU.add)
            used[g] = m
            acc_used.append(None)

            def sum_on_pe(n=len(acc_used) - 1):
                wait(te, m)
                for c in range(4):
                    mm = te.matmul(bank[:, 6, 4 * g + c:4 * g + c + 1], a[:, P * c:P * c + P], ones[:, 0:1],
                                   start=True, stop=True)
                acc_used[n] = pe.after(mm)
                return acc_used[n]

            return sum_on_pe

        row_copied, row_at, rows_made, rows_turned = {}, {}, [], []

        def ada_row_on_pe(g):
            ada_arrives(te, g)
            wait(te, silu)
            q = len(rows_made) % 2
            row_at[g] = q
            for k in range(8):
                mm = te.matmul(bank[0:1, 2 + q], c_act[:, k:k + 1], ada_slot(g)[:, k],
                               start=k == 0, stop=k == 7)
            used[g] = pe.after(mm)
            rows_made.append(used[g])

        def ada_row_turned(g):
            q = row_at[g]
            wait(se, used[g])
            row_copied[g] = act_(ada_row[0:1, q], bank[0:1, 2 + q], ACT.Copy)
            wait(te, row_copied[g])
            for c in range(4):
                mm = te.matmul(bank[:, 7, 4 * g + c:4 * g + c + 1], ada_row[0:1, row_at[g], P * c:P * c + P],
                               ones[0:1, 0:1], start=True, stop=True)
            rows_turned.append(pe.after(mm))
            return rows_turned[-1]

        def mod_columns(a, b, source, mark):
            wait(ve, mark, vec_ready)
            m = tt(mod[:, a:b], bank[:, source, a:b], vec[:, VEC_AT["ada_b"] + a:VEC_AT["ada_b"] + b], ALU.add)
            wait(ve, m)
            return m

        def gains(at, scale_at, norm_at):
            m = stt(gain[:, at:at + 8], mod[:, scale_at:scale_at + 8], 1.0, vec[:, norm_at:norm_at + 8], ALU.add, ALU.mult)
            wait(ve, m)
            return m

        sum0 = ada_on_dve(0)
        ada_row_on_pe(1)
        for k in range(DT):
            norm_x.add(copied[k])
        sum0()
        ada_on_dve(2)()
        inv = norm_x.end()
        row1 = ada_row_turned(1)
        te.wait_ge(rel_in, 48)
        wait(te, outside, *copied)
        looked_up = pe.after(te.matmul(bank[0:8, 0, 0:384], rel[:, :], buckets, start=True, stop=True))
        wait(se, looked_up)
        ve.wait_ge(rel_in, 48)
        table_made = act_(table, bank[0:8, 0, 0:384], ACT.Copy)
        wait(ge, table_made)
        ge.dma_start(t["scratch"], table).then_inc(table_out, 16)
        summed3 = ada_on_dve(3)()
        wait(ve, summed3)
        for a, b, source in ((0, 4, 6), (4, 8, 7), (8, 16, 6)):
            shift_ready = mod_columns(a, b, source, row1)
        gains(0, 8, VEC_AT["norm_mix_g"])

        wait(ve, inv)
        wait(se, shift_ready)
        made = []
        for k in range(DT):
            if k >= 2:
                wait(ve, made[k - 2])
            scaled = stt(tmp[:, k % 2], xT[:, k], gain[:, k:k + 1], rstd_bank, ALU.mult, ALU.mult)
            wait(se, scaled)
            made.append(act_(h[:, k, 16:], tmp[:, k % 2], ACT.Identity, bias=modv(0, 0, k)))
        norm["read"] = [scaled]
        ada_row_on_pe(4)
        wait(te, shift_ready)
        ve.wait_ge(const_in, 16)
        wait(ge, sums_zero)
        pooled_ready, window_sums = [], []

        def add_windows(g):
            source = h[:, 2 * g:2 * g + 2]
            wait(ge, made[2 * g + 1])
            if g:
                wait(ge, pooled_ready[g - 1])
            a, w, m = 0, 1, None
            while w < POOL_WINDOWS[g]:
                if m:
                    wait(ge, m)
                m = pool.after(ge.tensor_tensor(sums[:, a, :, 16:], source[:, :, 16:], source[:, :, 16 - w:16 + T - w], ALU.add))
                source = sums[:, a]
                a, w = 1 - a, 2 * w
            window_sums.append((source, m))

        def subtract_means(g):
            source, m = window_sums[g]
            hg = h[:, 2 * g:2 * g + 2, 16:]
            wait(ve, m)
            if g == 3:
                wait(ve, looked_up)
                ve.wait_ge(table_out, 16)
            mean = stt(pooled[:, 2 * g:2 * g + 2], source[:, :, 16:], 1.0 / POOL_WINDOWS[g], hg, ALU.mult, ALU.subtract)
            inv_count = cst("pool_inv", 16 * g, 16).unsqueeze(1).broadcast_to([P, 2, 16])
            wait(ve, made[7])
            first = tt(tmp[:, :, 0:16], source[:, :, 16:32], inv_count, ALU.mult)
            wait(ve, mean, first)
            pooled_ready.append(tt(pooled[:, 2 * g:2 * g + 2, 0:16], tmp[:, :, 0:16], hg[:, :, 0:16], ALU.subtract))

        x_ready = []

        def mix_pool(g):
            full = []
            for n in range(2):
                if g:
                    wait(te, x_ready[2 * g - 2 + n])
                for k in range(2):
                    mm = te.matmul(bank[:, n], pool_w[:, g, k, P * n:P * n + P], pooled[:, 2 * g + k],
                                   start=k == 0, stop=k == 1)
                full.append(pe.after(mm))
            return full

        def take_pool(g, full):
            for n in range(2):
                o = 2 * g + n
                wait(ve, full[n])
                x_ready.append(stt(xT[:, o], bank[:, n], gain[:, 32 + o:33 + o], xT[:, o], ALU.mult, ALU.add))

        add_windows(0)
        sum5 = ada_on_dve(5)
        row4 = ada_row_turned(4)
        summed5 = sum5()
        subtract_means(0)
        add_windows(1)
        sum6 = ada_on_dve(6)
        wait(ve, summed5)
        mod_columns(16, 20, 7, row4)
        mod_columns(20, 24, 6, row4)
        scale_ready = tt(gain[:, 32:40], mod[:, 16:24], vec[:, VEC_AT["pool_scale"]:VEC_AT["pool_scale"] + 8], ALU.mult)
        wait(ve, scale_ready)
        wait(te, scale_ready)
        sum6()
        te.wait_ge(pool_w_in, 16)
        wait(te, pooled_ready[0])
        full = mix_pool(0)
        subtract_means(1)
        add_windows(2)
        sum7 = ada_on_dve(7)
        take_pool(0, full)
        sum7()
        wait(te, pooled_ready[1])
        full = mix_pool(1)
        ada_row_on_pe(8)
        subtract_means(2)
        add_windows(3)
        take_pool(1, full)
        wait(te, pooled_ready[2])
        full = mix_pool(2)
        sum9 = ada_on_dve(9)
        subtract_means(3)
        take_pool(2, full)
        row8 = ada_row_turned(8)
        sum9()
        wait(te, pooled_ready[3])
        full = mix_pool(3)
        sum10 = ada_on_dve(10)
        take_pool(3, full)
        sum10()
        summed = ada_on_dve(11)()
        wait(ve, summed)
        for a, b, source in ((24, 32, 6), (32, 36, 7), (36, 48, 6)):
            rows_ready = mod_columns(a, b, source, row8)
        mod_ready = gains(8, 32, VEC_AT["norm_mlp_g"])
        wait(se, mod_ready)
        for g in range(12):
            if g >= ADA_RING:
                wait(sy, used[g - ADA_RING])
            elif g == ADA_RING - 1:
                wait(sy, x_turned)
            sy.dma_start(ada_slot(g), t["ada_w"][0, :, 512 * g:512 * g + 512]
                         .rearrange("(k p) n -> p k n", p=P)).then_inc(ada_landed[g % ADA_RING], 16)
        all_slabs()
        stage0_done = [x_ready[-1], table_made, *rows_made[-2:], rows_ready]
        wait(se, *stage0_done)

    def project(moving, groups, free, ready, evacuate, norm=None, weights_stationary=True, beside=None):
        marks = []
        for g in range(groups):
            for k, m in enumerate(moving):
                full = step(m, range(4), free, ready[4 * k:4 * k + 4] if ready and g == 0 else None,
                            k == 0, k == len(moving) - 1, weights_stationary)
                if beside:
                    beside(k)
                if norm and g and k == 0:
                    for o in range(4 * g - 4, 4 * g):
                        norm.add(marks[o])
            for n in range(4):
                wait(se, full[n])
                wait(ve, full[n])
                marks.append(evacuate(4 * g + n, n))
            free = [[m] for m in marks[-4:]]
        if norm:
            for o in range(4 * groups - 4, 4 * groups):
                norm.add(marks[o])
        return marks

    def quarters(hi, lo, n):
        return [(hi[:, 4 * k:4 * k + 4], lo[:, 4 * k:4 * k + 4]) for k in range(n)]

    class AdaSecond:
        LOADS = 24

        def __init__(self, ring, acc):
            self.ring, self.acc = ring, acc
            self.landed = [nc.alloc_semaphore(f"ada1_landed{i}") for i in range(2)]
            self.added, self.summed = [], []
            self.sent = 0
            wait(ge, *stage0_done)
            self.load()
            self.load()

        def load(self):
            u = self.sent
            if u < self.LOADS:
                if u >= 2:
                    wait(ge, self.added[u - 2])
                ge.dma_start(self.ring[:, u % 2], t["ada_w"][1, :, 256 * u:256 * u + 256]
                             .rearrange("(k p) n -> p k n", p=P)).then_inc(self.landed[u % 2], 16)
                self.sent += 1

        def add(self):
            u = len(self.added)
            ve.wait_ge(self.landed[u % 2], 16 * (u // 2 + 1))
            a = self.acc[:, u % 4]
            if u >= 4:
                wait(ve, self.summed[u - 4])
            m = ts(a, self.ring[:, u % 2, 0], c_act[:, 0:1], None, ALU.mult)
            for k in range(1, 8):
                wait(ve, m)
                m = stt(a, self.ring[:, u % 2, k], c_act[:, k:k + 1], a, ALU.mult, ALU.add)
            self.added.append(m)
            self.load()

        def sum(self):
            for u in range(len(self.summed), len(self.added)):
                wait(te, self.added[u])
                for c in range(2):
                    mm = te.matmul(bank[:, 7, 2 * u + c:2 * u + c + 1], self.acc[:, u % 4, P * c:P * c + P],
                                   ones[:, 0:1], start=True, stop=True)
                self.summed.append(pe.after(mm))

        def beside(self, k):
            self.sum()
            for _ in range(2 - k % 2):
                self.add()

        def finish(self):
            self.sum()
            assert len(self.summed) == self.LOADS
            wait(ve, self.summed[-1])
            b = VEC_AT["ada_b"] + 48
            return tt(mod[:, 54:102], bank[:, 7, 0:48], vec[:, b:b + 48], ALU.add)

    def mlp(layer, norm_x, h_hi, h_lo, u_hi, u_lo, sq, free, extra=None):
        inv = norm_x.end()
        ready = normalise(xT, inv, lambda k: gain[:, 16 * layer + 8 + k:16 * layer + 9 + k],
                          lambda k: modv(layer, 3, k), h_hi, h_lo)
        for half in range(2):
            with slab_loop(4, {pe: 3, act: 8, dve: 8}) as loop:
                relus = [(act, act.n + 2 * n + 1 - 8, loop) for n in range(4)]
                split_next()
                slab_products((h_hi[:, 0:4], h_lo[:, 0:4]), range(4), [[relus[n], *free] for n in range(4)],
                              ready[0:4] if half == 0 else None, True, False)
                split_next()
                full = slab_products((h_hi[:, 4:8], h_lo[:, 4:8]), range(4), None,
                                     ready[4:8] if half == 0 else None, False, True)
                dbase = dve.n
                for n in range(4):
                    wait(se, full[n])
                    wait(se, (dve, dbase + max(2 * n - 3, 0), loop))
                    relu = act_(tmp[:, n % 2], bank[:, n], ACT.Relu)
                    wait(ve, relu)
                    squared = tt(sq[:, n], tmp[:, n % 2], tmp[:, n % 2], ALU.mult)
                    wait(se, squared)
                    tile = bass.ds(loop.i * 4 + n, 1)
                    made = act_(u_hi[:, tile, :], sq[:, n:n + 1], ACT.Copy)
                    wait(ve, made)
                    lo_done = tt(u_lo[:, tile, :], sq[:, n:n + 1], u_hi[:, tile, :].bitcast(F32), ALU.subtract)
            end_loop(4)
            norm_next = Rms(xT, sq, (lo_done,)) if half else None

            def add_to_x(o, n):
                return stt(xT[:, o], bank[:, n], modv(layer, 5, o), xT[:, o], ALU.mult, ALU.add)

            earlier = [before(made), before(lo_done)]
            marks = project(quarters(u_hi, u_lo, 4), 2, [[relu]] * 4, [earlier] * 12 + [[made, lo_done]] * 4, add_to_x, norm_next,
                            beside=extra.beside if extra else None)
            free = [marks[-1]]
        return norm_next, marks

    split_next()
    early = ExitStack()
    h_hi, h_lo = (early.enter_context(sb(n, [P, DT, T], FR)) for n in ("h_hi", "h_lo"))
    wait(ve, *stage0_done)
    with sb("u_hi", [P, 16, T], FR) as u_hi, sb("u_lo", [P, 16, T], FR) as u_lo, sb("sq_b", [P, 4, T]) as sq, \
            sb("ada1_ring", [P, 2, 8, 256]) as ada1_ring, sb("ada1_acc", [P, 4, 256]) as ada1_acc:
        extra = AdaSecond(ada1_ring, ada1_acc)
        norm_x = Rms(xT, sq, stage0_done, on_pool=True)
        for m in x_ready:
            norm_x.add(m)
        norm_x, x_ready = mlp(0, norm_x, h_hi, h_lo, u_hi, u_lo, sq, stage0_done, extra)
        mod_ready = extra.finish()
        wait(ve, mod_ready)
        gains(16, 54 + 8, VEC_AT["norm_mix_g"] + 8)
        mod_ready = gains(24, 54 + 32, VEC_AT["norm_mlp_g"] + 8)
        wait(se, mod_ready)
        inv = norm_x.end()

    with sb("u", [P, DT, T]) as u, sb("v", [P, 4, D]) as v, sb("sq_c", [P, 4, T]) as sq, \
            sb("g_hi", [P, DT, T], FR) as g_hi, sb("g_lo", [P, DT, T], FR) as g_lo, \
            sb("ws", [P, DT, P]) as ws, sb("wsT", [P, DT, P]) as wsT, sb("bs_row", [1, D]) as bs_row, \
            sb("bs", [P, D]) as bs, sb("stats", [P, 4, 2, 6]) as stats, sb("mv", [P, 4, 2]) as mv:
        ws_in = nc.alloc_semaphore("ws_in")
        wait(ge, *x_ready, inv)
        ge.dma_start(ws[:, :, :], t["sgu_w_s"][0].rearrange("h t s -> t h s")).then_inc(ws_in, 16)
        ge.dma_start(bs_row[:, :], t["sgu_b_s"]).then_inc(ws_in, 16)
        wait(se, *x_ready, inv)
        ready = normalise(xT, inv, lambda k: gain[:, 16 + k:17 + k], lambda k: modv(1, 0, k), h_hi, h_lo)
        free = [[m] for m in x_ready[4:8]]
        h_moving = quarters(h_hi, h_lo, 2)
        u_ready = project(h_moving, 2, free, ready, lambda o, n: act_(u[:, o], bank[:, n], ACT.Gelu))
        v_made = project(h_moving, 2, [[m] for m in u_ready[4:8]], None,
                         lambda o, n: act_(v[:, n, 512 * (o // 4):512 * (o // 4) + 512], bank[:, n], ACT.Gelu),
                         weights_stationary=False)
        te.wait_ge(ws_in, 32)
        wait(te, *norm["read"])
        for hh in range(DT):
            mm = te.transpose(bank[:, 4 + hh // 4, P * (hh % 4):P * (hh % 4) + P], ws[:, hh], ident)
        turned = pe.after(mm)
        wait(ve, turned)
        masked = tt(wsT[:, :, :], bank[:, 4:6].rearrange("p b (h t) -> p (b h) t", h=4),
                    cst("tril_T").unsqueeze(1).broadcast_to([P, DT, P]), ALU.mult)
        for q in range(2):
            mm = te.matmul(bank[:, 6 + q], ones[0:1, :], bs_row[0:1, 512 * q:512 * q + 512], start=True, stop=True)
        spread = pe.after(mm)
        wait(se, spread)
        bs_ready = act_(bs[:, :], bank[:, 6:8].rearrange("p b n -> p (b n)"), ACT.Copy)
        wait(te, masked, bs_ready)
        for q in range(2):
            mm = te.matmul(bank[:, 6 + q], ones[:, :], wsT[:, 4 * q:4 * q + 4].rearrange("p h t -> p (h t)"),
                           start=True, stop=True)
        summed = pe.after(mm)
        wait(ve, summed, bs_ready)
        for hh in range(DT):
            part = slice(P * hh, P * hh + P)
            qs_ready = stt(bs[:, part], bank[:, 6 + hh // 4, P * (hh % 4):P * (hh % 4) + P],
                           col("sgu_ln_b", hh), bs[:, part], ALU.mult, ALU.add)
        v_ready = []
        for n in range(4):
            wait(ve, v_made[4 + n])
            for q in range(2):
                st = dve.after(ve.bn_stats(stats[:, n, q], v[:, n, 512 * q:512 * q + 512]))
            wait(ve, st)
            ag = dve.after(ve.bn_aggr(mv[:, n], stats[:, n]))
        wait(se, ag)
        root = act_(mv[:, :, 1:2], mv[:, :, 1:2], ACT.Sqrt, bias=eps[:, 1:2])
        wait(ve, root, ag)
        rec = dve.after(ve.reciprocal(mv[:, :, 1:2], mv[:, :, 1:2]))
        wait(ve, rec)
        for n in range(4):
            v_ready.append(ts(v[:, n], v[:, n], mv[:, n, 0:1], mv[:, n, 1:2], ALU.subtract, ALU.mult))
        wait(te, masked)
        wait(ve, qs_ready, *u_ready)
        gated, mix_free = [], [(), ()]
        for hh in range(DT):
            b = 4 + hh % 2
            wait(te, *mix_free[hh % 2])
            for n in range(4):
                if hh == 0:
                    wait(te, v_ready[n])
                mm = te.matmul(bank[:, b, P * n:P * n + P], v[:, n, P * hh:P * hh + P], wsT[:, hh],
                               start=True, stop=True)
            full_mix = pe.after(mm)
            wait(ve, full_mix)
            mixed = stt(tmp[:, hh % 2].rearrange("p (n t) -> p n t", n=4), bank[:, b].rearrange("p (n t) -> p n t", n=4),
                        col("sgu_ln_g", hh),
                        bs[:, P * hh:P * hh + P].unsqueeze(1).broadcast_to([P, 4, P]), ALU.mult, ALU.add)
            mix_free[hh % 2] = (mixed,)
            wait(ve, mixed)
            prod = tt(u[:, hh], u[:, hh], tmp[:, hh % 2], ALU.mult)
            gated.append(split_into(g_hi[:, hh], g_lo[:, hh], u[:, hh], [prod]))
        norm_x = Rms(xT, sq, (mixed,))
        x_ready = project(quarters(g_hi, g_lo, 2), 2, [[m] for m in v_made[4:8]], gated,
                          lambda o, n: stt(xT[:, o], bank[:, n], modv(1, 2, o), xT[:, o], ALU.mult, ALU.add), norm_x)
        sgu_done = [x_ready[-1], norm_x.marks[-1]]
    with sb("u2_hi", [P, 16, T], FR) as u_hi, sb("u2_lo", [P, 16, T], FR) as u_lo, sb("sq_d", [P, 4, T]) as sq:
        wait(se, *sgu_done)
        wait(ve, *sgu_done)
        norm_x, x_ready = mlp(1, norm_x, h_hi, h_lo, u_hi, u_lo, sq, sgu_done)
        inv = norm_x.end()
        wait(ve, inv)
        free = [[x_ready[-1]]] * 4
        norm_x = Rms(xT, sq, (norm_x.marks[-1],), on_pool=True)
        x_ready = []
        for k in range(DT):
            x_ready.append(stt(xT[:, k], xT[:, k], col("final_g", k), rstd_bank, ALU.mult, ALU.mult))
            norm_x.add(x_ready[-1])
        norm["read"] = [x_ready[-1]]
        inv = norm_x.end()
        ready = normalise(xT, inv, lambda k: col("norm_mix_pre_2", k), None, h_hi, h_lo)

    mixer = ExitStack()

    def ms(name, shape, dt=F32):
        return mixer.enter_context(nc.sbuf_tensor(name, shape, dt, side="right"))

    ar = ms("ar", [P, 4, 2, T])
    rT = ar[:, :, 1]
    kkT = ms("kkT", [P, 4, T])
    vvT = ms("vvT", [P, 4, T])
    attnT = ms("attnT", [P, 4, T])
    bT = ms("bT", [P, 4, T])
    gT = ms("gT", [P, 4, T])
    bonus = ms("bonus", [P, 4, T])
    pc = ms("pc", [P, 4, 8])
    one_less = ms("one_less", [P, 18])
    z_stack, q_stack = ExitStack(), ExitStack()
    cum = z_stack.enter_context(nc.sbuf_tensor("cum", [P, 4, T], F32, side="right"))
    inv_rows = z_stack.enter_context(nc.sbuf_tensor("inv_rows", [P, 4, 4, 2], F32, side="right"))
    zT = z_stack.enter_context(nc.sbuf_tensor("zT", [P, 2, T], F32, side="right"))
    qT = q_stack.enter_context(nc.sbuf_tensor("qT", [P, 4, T], F32, side="right"))
    kT = q_stack.enter_context(nc.sbuf_tensor("kT", [P, T], F32, side="right"))
    vT = q_stack.enter_context(nc.sbuf_tensor("vT", [P, T], F32, side="right"))
    made = ts(one_less[:, 0:14], vec[:, VEC_AT["rwkv_shift_mix_2"]:VEC_AT["rwkv_shift_mix_2"] + 14],
              -1.0, 1.0, ALU.mult, ALU.add)
    made = ts(one_less[:, 14:18], vec[:, VEC_AT["k_a_2"]:VEC_AT["k_a_2"] + 4], -1.0, 1.0, ALU.mult, ALU.add)
    wait(se, made)
    wait(ve, made)
    dest = [qT[:, i] for i in range(4)] + [kT[:, :], vT[:, :]] + [rT[:, i] for i in range(4)] + \
           [kkT[:, i] for i in range(4)] + [vvT[:, i] for i in range(4)] + [zT[:, i] for i in range(2)]
    proj = [None] * 20
    aT = gT
    sc = bonus
    normalised = [*ready[-1], norm_x.marks[-1], x_ready[-1]]
    lora_in = nc.alloc_semaphore("lora_in")
    bias_in = nc.alloc_semaphore("bias_in")
    lora = tmp
    bias_rev = attnT[:, :, :].rearrange("p i (h j) -> p (i h) j", h=2)
    spread_inv = qT[:, :, :].rearrange("p j (i d) -> p j i d", i=4)
    wait(ge, *normalised)
    wait(se, *normalised)
    wait(ve, *normalised)
    ge.dma_start(lora[0:64, 0], t["w_decay_up_2"]).then_inc(lora_in, 16)
    ge.dma_start(lora[64:128, 0], t["w_iclr_up_2"]).then_inc(lora_in, 16)
    ge.dma_start(lora[:, 1], t["w_gate_up_2"]).then_inc(lora_in, 16)
    ge.wait_ge(table_out, 16)
    ge.dma_start(bias_rev, bass.AP(tensor=t["scratch"].tensor, offset=0, ap=[[1, P], [384, 8], [1, 256]])).then_inc(bias_in, 16)

    R = {}

    def after_z():
        wait(se, *proj[18:20])
        R["z"] = (act_(zT[0:64, 0], zT[0:64, 0], ACT.Tanh), act_(zT[:, 1], zT[:, 1], ACT.Sigmoid))

    def turn_bias():
        te.wait_ge(bias_in, 16)
        wait(te, *proj)
        for q in range(4):
            mm = te.matmul(bank[:, q], cst("reverse"), bias_rev[:, 2 * q:2 * q + 2].rearrange("p h j -> p (h j)"),
                           start=True, stop=True)
        m = pe.after(mm)
        wait(ve, m)
        R["bias"] = dve.after(ve.tensor_copy(bias[:, :, :].rearrange("p (b h) j -> p b (h j)", b=4), bank[:, 0:4]))

    def loras():
        te.wait_ge(lora_in, 48)
        wait(te, *R["z"])
        for i in range(4):
            mm = te.matmul(bank[:, 4 + i], lora[0:64, 0, P * i:P * i + P], zT[0:64, 0], start=True, stop=True)
        m = pe.after(mm)
        wait(se, m)
        for i in range(4):
            d = act_(cum[:, i], bank[:, 4 + i], ACT.Sigmoid, bias=col("w0_2", i))
        R["d"] = d
        wait(ve, d)
        neg = ts(cum[:, :, :], cum[:, :, :], -EXP_M_HALF, None, ALU.mult)
        wait(ve, neg)
        for i in range(4):
            R["cum"] = dve.after(ve.tensor_tensor_scan(cum[:, i], cst("chunk_start"), cum[:, i], 0.0, ALU.mult, ALU.add))

    def rates():
        wait(te, R["d"])
        for i in range(4):
            mm = te.matmul(bank[:, 4 + i], lora[64:128, 0, P * i:P * i + P], zT[64:128, 0], start=True, stop=True)
        m = pe.after(mm)
        wait(se, m)
        for i in range(4):
            R["a"] = act_(aT[:, i], bank[:, 4 + i], ACT.Sigmoid, bias=col("a0_2", i))

    kk = ar[:, :, 0]

    def norms():
        wait(ve, *proj[10:14])
        for i in range(4):
            k0 = ts(kk[:, i], kkT[:, i], col("k_k_2", i), None, ALU.mult)
        wait(se, k0)
        s2 = act_(sc[:, :, :], kk, ACT.Square)
        wait(te, s2, R["a"])
        for j in range(4):
            for i in range(4):
                a = 8 * j + 2 * i
                mm = te.matmul(bank[:, 4, a:a + 2], sc[:, i, P * j:P * j + P], cst("head_ones")[:, 0:P:64],
                               start=True, stop=True)
        m = pe.after(mm)
        wait(se, m)
        rows2 = inv_rows[:, :, :, :].rearrange("p j i h -> p (j i h)")
        root = act_(rows2, bank[:, 4, 0:32], ACT.Sqrt)
        wait(ve, root)
        m = ts(rows2, rows2, 1e-12, None, ALU.max)
        wait(ve, m)
        m = dve.after(ve.reciprocal(rows2, rows2))
        wait(ve, m)
        m = dve.after(ve.tensor_copy(spread_inv.rearrange("p j i (h d) -> p (j i h) d", h=2),
                                     rows2.unsqueeze(2).broadcast_to([P, 32, 64])))
        R["spread"] = m
        R["root"] = root

    def norms_back():
        wait(te, R["spread"])
        for i in range(4):
            for j in range(4):
                mm = te.matmul(bank[:, 4 + i, P * j:P * j + P], spread_inv[:, j, i], ident, start=True, stop=True)
        m = pe.after(mm)
        wait(ve, m)
        R["kk"] = tt(kk, kk, bank[:, 4:8], ALU.mult)

    def keys():
        wait(ve, R["a"], R["root"])
        for i in range(4):
            m1 = ts(sc[:, i], aT[:, i], col("k_a_2", i), one_less[:, 14 + i:15 + i], ALU.mult, ALU.add)
        wait(ve, m1)
        R["k"] = tt(kkT[:, :, :], kkT[:, :, :], sc[:, :, :], ALU.mult)
        wait(ve, R["kk"])
        R["b"] = tt(bT[:, :, :], kk, aT[:, :, :], ALU.mult)

    def bonuses():
        wait(ve, R["k"], *proj[6:10])
        for i in range(4):
            m3 = stt(sc[:, i], rT[:, i], col("r_k_2", i), kkT[:, i], ALU.mult, ALU.mult)
        R["m3"] = m3
        wait(te, m3, R["kk"])
        for i in range(4):
            mm = te.matmul(bank[:, 4 + i], cst("head_ones"), sc[:, i], start=True, stop=True)
        m = pe.after(mm)
        wait(ve, m, *proj[14:18])
        R["bonus"] = tt(bonus[:, :, :], bank[:, 4:8], vvT[:, :, :], ALU.mult)

    kk4, cum4 = (a.rearrange("p i (c s) -> p i c s", s=64) for a in (kk, cum[:, :, :]))

    def exponentials():
        wait(se, R["b"], R["k"])
        R["e3"] = act_(aT[:, :, :], cum[:, :, :], ACT.Exp, scale=-1.0)
        wait(se, R["e3"])
        R["e1"] = act_(cum[:, :, :], cum[:, :, :], ACT.Exp)

    def with_decay():
        wait(ge, R["e3"])
        R["B"] = pool.after(ge.tensor_tensor(bT[:, :, :], bT[:, :, :], aT[:, :, :], ALU.mult))
        wait(ge, R["m3"])
        R["K"] = pool.after(ge.tensor_tensor(kkT[:, :, :], kkT[:, :, :], aT[:, :, :], ALU.mult))
        wait(ge, R["e1"])
        for i in range(4):
            R["A"] = pool.after(ge.tensor_tensor(kk4[:, i, :, 1:], kk4[:, i, :, 1:], cum4[:, i, :, 0:63], ALU.mult))
        R["R"] = pool.after(ge.tensor_tensor(rT, rT, cum[:, :, :], ALU.mult))
        R["pc"] = pool.after(ge.tensor_copy(pc[:, :, :], cum4[:, :, :, 63]))

    def gates():
        wait(te, R["bonus"])
        for i in range(4):
            mm = te.matmul(bank[:, 4 + i], lora[:, 1, P * i:P * i + P], zT[:, 1], start=True, stop=True)
        m = pe.after(mm)
        wait(se, m, R["K"])
        R["g"] = act_(gT[:, :, :], bank[:, 4:8], ACT.Copy)

    def evacuate(o, n):
        if o < 6:
            return act_(dest[o], bank[:, n], ACT.Copy, scale=0.125 if o < 4 else 1.0)
        here = act_(dest[o], bank[:, n], ACT.Copy, scale=one_less[:, o - 6:o - 5])
        wait(ve, here)
        return stt(dest[o][:, 1:], bank[:, n, 0:T - 1], col("rwkv_shift_mix_2", o - 6),
                   dest[o][:, 1:], ALU.mult, ALU.add)

    beside = {(1, 1): [loras], (2, 0): [rates], (3, 0): [norms], (3, 1): [norms_back],
              (4, 0): [keys], (4, 1): [exponentials, bonuses, with_decay]}
    for place, g in enumerate(PROJ_GROUPS):
        for k, m in enumerate(quarters(h_hi, h_lo, 2)):
            full = step(m, range(4), free, ready[4 * k:4 * k + 4] if place == 0 else None, k == 0, k == 1)
            for f in beside.get((place, k), ()):
                f()
        for n in range(4):
            wait(se, full[n])
            wait(ve, full[n])
            proj[4 * g + n] = evacuate(4 * g + n, n)
        free = [[proj[4 * g + n]] for n in range(4)]
        if place == 0:
            after_z()
    early.close()
    softmax = ExitStack()
    bias, v_rows, scores, p_t, small = (
        softmax.enter_context(sb(n, shape)) for n, shape in
        (("bias", [P, 8, 256]), ("v_rows", [P, 4, P]), ("scores", [P, 2, 4, 256]), ("p_t", [P, 2, 2, 512]),
         ("small", [P, 2, 5, 4])))
    turn_bias()
    gates()

    wait(te, *proj, R["bias"])
    for n in range(4):
        mm = te.transpose(bank[:, 2, P * n:P * n + P], vT[:, P * n:P * n + P], ident)
    turned = pe.after(mm)
    wait(se, turned)
    wait(ve, *proj, R["bias"])
    v_ready = act_(v_rows[:, :, :], bank[:, 2].rearrange("p (n d) -> p n d", n=4), ACT.Copy)
    M = [{} for _ in range(8)]

    def read(it, what):
        return (M[it][what],) if it >= 0 else ()

    score_bank = (0, 6)

    def score(it):
        n, half = divmod(it, 2)
        j0 = 128 if n == 0 else 0
        r0 = 64 * half
        wait(te, *read(it - 2, "biased"))
        for i in range(4):
            mm = te.matmul(bank[:, score_bank[half] + i // 2, 256 * (i % 2) + j0:256 * (i % 2) + 256],
                           qT[r0:r0 + 64, i, P * n:P * n + P],
                           kT[r0:r0 + 64, P * n - P + j0:P * n + P], start=True, stop=True)
        M[it]["scored"] = pe.after(mm)

    def softmax_start(it):
        n, half = divmod(it, 2)
        j0 = 128 if n == 0 else 0
        m = M[it]
        s = scores[:, half, :, j0:]
        sm = small[:, half]
        b = score_bank[half]
        wait(ve, m["scored"], *read(it - 2, "turned"))
        m["biased"] = tt(s, bank[:, b:b + 2].rearrange("p b (i j) -> p (b i) j", i=2)[:, :, j0:],
                         bias[:, 4 * half:4 * half + 4, j0:], ALU.add)
        wait(ve, m["biased"])
        top = dve.after(ve.tensor_reduce(sm[:, 0], s, AX, ALU.max))
        wait(ve, top)
        top = tt(sm[:, 0], sm[:, 0], sink[:, 4 * half:4 * half + 4], ALU.max)
        wait(ve, top)
        tt(sm[:, 2], sink[:, 4 * half:4 * half + 4], sm[:, 0], ALU.subtract)
        neg = ts(sm[:, 1], sm[:, 0], -1.0, None, ALU.mult)
        wait(se, neg)
        for i in range(4):
            act_(scores[:, half, i, j0:], scores[:, half, i, j0:], ACT.Exp, bias=sm[:, 1, i:i + 1],
                 accum_out=sm[:, 3, i:i + 1])
        m["exps"] = act_(sm[:, 4], sm[:, 2], ACT.Exp)

    def take(it):
        n, half = divmod(it, 2)
        r0 = 64 * half
        wait(se, M[it]["summed"])
        M[it]["got"] = act_(attnT[r0:r0 + 64, :, P * n:P * n + P],
                            bank[r0:r0 + 64, 4 + half].rearrange("p (i t) -> p i t", i=4), ACT.Copy)

    def softmax_end(it):
        n, half = divmod(it, 2)
        j0 = 128 if n == 0 else 0
        r0, m = 64 * half, M[it]
        s = scores[:, half, :, j0:]
        sm = small[:, half]
        wait(ve, m["exps"])
        den = tt(sm[:, 3], sm[:, 3], sm[:, 4], ALU.add)
        wait(ve, den)
        rec = dve.after(ve.reciprocal(sm[:, 3], sm[:, 3]))
        wait(ve, rec)
        probs = tt(s, s, sm[:, 3].unsqueeze(2).broadcast_to([P, 4, 256 - j0]), ALU.mult)
        wait(te, probs, v_ready, *read(it - 1, "copied"))
        for q in range(j0 // 128, 2):
            for i in range(4):
                mm = te.transpose(bank[:, 2 + q, P * i:P * i + P], scores[:, half, i, P * q:P * q + P], ident)
        m["turned"] = pe.after(mm)
        if it < 6:
            score(it + 2)
        wait(se, m["turned"], *read(it - 2, "summed"))
        m["copied"] = act_(p_t[:, half, j0 // 128:2], bank[:, 2 + j0 // 128:4], ACT.Copy)
        if it:
            take(it - 1)
        wait(te, m["copied"], *read(it - 2, "got"))
        for q in range(j0 // 128, 2):
            mm = te.matmul(bank[r0:r0 + 64, 4 + half], v_rows[:, n - 1 + q, r0:r0 + 64], p_t[:, half, q],
                           start=q == j0 // 128, stop=q == 1)
        m["summed"] = pe.after(mm)

    score(0)
    wait(te, R["g"])
    score(1)
    softmax_start(0)
    for it in range(8):
        if it < 7:
            softmax_start(it + 1)
        softmax_end(it)
    take(7)
    attn_ready = [M[6]["got"], M[7]["got"]]
    softmax.close()
    q_stack.close()
    z_stack.close()
    bonus_ready, g_ready = R["bonus"], R["g"]
    ready = [*attn_ready, M[7]["copied"], M[7]["turned"], R["A"], R["B"], R["K"], R["R"], R["pc"], bonus_ready, g_ready]

    o_rows = ms("o_rows", [P, 4, 8, 64])
    with sb("kend", [P, 2, 4, P]) as kend, sb("rows", [P, 3, 4, P]) as rows_, sb("m_b", [P, 8, 2, P]) as m_b, \
            sb("m_k", [P, 8, 2, P]) as m_k, sb("xx", [P, 8, 2, P]) as xx, sb("ct", [P, 8, P]) as ct, \
            sb("t1", [P, 8, P]) as t1, sb("zneg", [P, 512]) as zneg, sb("vz", [P, 2, 4, P]) as vz, \
            sb("state", [P, 4, P]) as state, sb("scaled", [P, 4, P]) as scaled:
        for e in (te, ve, se, ge):
            wait(e, *ready)
        zero = dve.after(ve.memset(state[:, :, :], 0.0))
        state_ready = [zero]
        halves = [slice(0, 64), slice(64, 128)]
        w = tmp[:, :].rearrange("p h (i d) -> p h i d", i=4)
        clear_w = dve.after(ve.memset(w, 0.0))
        clear = dve.after(ve.memset(vz[:, :, :, :], 0.0))
        wait(se, clear_w, clear)

        def padded(o, src, scale=1.0):
            for hp in range(2):
                cc = slice(64 * hp, 64 * hp + 64)
                m = act_(o[:, hp, :, cc], src[:, :, cc], ACT.Copy, scale=scale)
            return m

        last = {"o": [], "z": [], "all": []}
        k_rows, b_rows, v_rows = rows_[:, 0], rows_[:, 1], rows_[:, 2]
        heads = [(4 * hp + i, slice(64 * hp, 64 * hp + 64), i) for hp in range(2) for i in range(4)]

        def per_head(a):
            return a.unsqueeze(1).broadcast_to([P, 4, P])

        def pair_products(stationary, first_bank, hp, tok):
            for g, rr, i in heads[4 * hp:4 * hp + 4]:
                mm = te.matmul(bank[:, first_bank + i // 2, 256 * (i % 2):256 * (i % 2) + 256],
                               stationary[rr, i, tok], ar[rr, i, :, tok], start=True, stop=True)
            return pe.after(mm)

        def masked(out_, first_bank, hp, part):
            return tt(out_[:, 4 * hp:4 * hp + 4, part],
                      bank[:, first_bank:first_bank + 2].rearrange("p b (g a t) -> p (b g) a t", g=2, a=2)[:, :, part],
                      per_head(cst("pair_masks", P * part, P)), ALU.mult)

        for j in range(4):
            tok = slice(P * j, P * j + P)
            mb, mn, pairs = [None] * 2, [None] * 2, [None] * 2
            x_ready_ = [None, None]
            pairs[0] = last["pairs"] if j else pair_products(bT, 6, 0, tok)
            wait(te, *last["z"], *last["o"], *state_ready)
            for hp in range(2):
                if hp:
                    pairs[1] = pair_products(bT, 4, 1, tok)
                for g, rr, i in heads[4 * hp:4 * hp + 4]:
                    mm = te.matmul(bank[:, 2 * hp, P * i:P * i + P], ar[rr, i, 0, tok], bT[rr, i, tok], start=True, stop=True)
                mn[hp] = pe.after(mm)
            wait(ve, *last["all"])
            for hp in range(2):
                g4 = slice(4 * hp, 4 * hp + 4)
                wait(ve, pairs[hp])
                mb[hp] = masked(m_b, 6 - 2 * hp, hp, 0)
                wait(ve, mn[hp], mb[hp])
                a1 = tt(xx[:, g4, 0], bank[:, 2 * hp].rearrange("p (g t) -> p g t", g=4), per_head(cst("level0")), ALU.mult)
                a2 = tt(xx[:, g4, 1], m_b[:, g4, 0], per_head(cst("levels_T", 0, P)), ALU.mult)
                wait(ve, a1, a2)
                x_ready_[hp] = tt(xx[:, g4], ident.unsqueeze(1).unsqueeze(1).broadcast_to([P, 4, 2, P]), xx[:, g4], ALU.subtract)
            for hp in range(2):
                mb_r = masked(m_b, 6 - 2 * hp, hp, 1)
            wait(te, *last["all"])
            for q, src in enumerate((kkT, bT)):
                kend_ready = tt(kend[:, q].rearrange("p i (c s) -> p i c s", c=2),
                                src[:, :, tok].rearrange("p i (c s) -> p i c s", c=2),
                                pc[:, :, 2 * j:2 * j + 2].unsqueeze(3).broadcast_to([P, 4, 2, 64]), ALU.mult)
            marks = {"mk": [], "rows": []}

            def beside_level(level):
                if level in (1, 2):
                    hp = level - 1
                    wait(te, mb_r, *marks["mk"])
                    made = pair_products(kkT, 6, hp, tok)
                    wait(ve, made)
                    masked(m_k, 6, hp, 0)
                    marks["mk"] = [masked(m_k, 6, hp, 1)]
                elif level == 3:
                    wait(te, kend_ready, *marks["mk"])
                    for q in range(2):
                        for i in range(4):
                            mm = te.transpose(bank[:, 6 + q, P * i:P * i + P], kend[:, q, i], ident)
                    turned = pe.after(mm)
                    wait(se, turned)
                    marks["rows"] = [act_(rows_[:, 0:2].rearrange("p q i d -> p q (i d)"), bank[:, 6:8], ACT.Copy)]
                elif level == 4:
                    wait(te, *marks["rows"])
                    for i in range(4):
                        mm = te.transpose(bank[:, 6, P * i:P * i + P], vvT[:, i, tok], ident)
                    turned = pe.after(mm)
                    wait(se, turned)
                    marks["rows"].append(act_(rows_[:, 2].rearrange("p i d -> p (i d)"), bank[:, 6], ACT.Copy))
                    marks["rows"].append(padded(vz, bank[:, 6].rearrange("p (i d) -> p i d", i=4)))

            t_done, y_done = [(), ()], [(), ()]
            for level in range(1, 6):
                t_ready = [None, None]
                for hp in range(2):
                    g4 = slice(4 * hp, 4 * hp + 4)
                    wait(ge, mb[hp], *t_done[hp])
                    c_ready = pool.after(ge.tensor_tensor(ct[:, g4], m_b[:, g4, 0], per_head(cst("levels_T", P * level, P)), ALU.mult))
                    wait(te, c_ready, x_ready_[hp])
                    for i in range(4):
                        g = 4 * hp + i
                        mm = te.matmul(bank[:, hp, P * i:P * i + P], ct[:, g], xx[:, g, 0], start=True, stop=True)
                    t_done[hp] = (pe.after(mm),)
                    wait(se, *t_done[hp], *y_done[hp])
                    t_ready[hp] = act_(t1[:, g4].rearrange("p g t -> p (g t)"), bank[:, hp], ACT.Copy)
                for hp in range(2):
                    g4 = slice(4 * hp, 4 * hp + 4)
                    wait(te, t_ready[hp], mb_r)
                    for i in range(4):
                        g, b = 4 * hp + i, 2 + 2 * hp + i // 2
                        if level < 5:
                            te.matmul(bank[:, b, 256 * (i % 2):256 * (i % 2) + P], xx[:, g, 1], t1[:, g], start=True, stop=True)
                        mm = te.matmul(bank[:, b, 256 * (i % 2) + P:256 * (i % 2) + 256], t1[:, g], xx[:, g, 1], start=True, stop=True)
                    y_done[hp] = (pe.after(mm),)
                    wait(ve, *y_done[hp])
                    y = bank[:, 2 + 2 * hp:4 + 2 * hp].rearrange("p b (g a t) -> p (b g) a t", g=2, a=2)
                    if level < 5:
                        x_ready_[hp] = tt(xx[:, g4], xx[:, g4], y, ALU.subtract)
                    else:
                        x_ready_[hp] = tt(xx[:, g4, 1], xx[:, g4, 1], y[:, :, 1], ALU.subtract)
                beside_level(level)

            wait(te, *marks["rows"], *marks["mk"], *x_ready_)

            def with_values(b, part):
                for i in range(4):
                    for hp in range(2):
                        mm = te.matmul(bank[:, b, P * i:P * i + P], m_k[:, 4 * hp + i, part], vz[:, hp, i],
                                       start=i == 0 and hp == 0, stop=False, skip_group_check=True)
                return pe.after(mm)

            def keys_part(cp):
                for i in range(4):
                    te.matmul(bank[:, 2 + cp, P * i:P * i + P], k_rows[halves[cp], i], v_rows[halves[cp], i],
                              start=i == 0, stop=False, skip_group_check=True)

            o_done = []
            with_values(6, 0)
            for cp in range(2):
                half = halves[cp]
                wait(te, *state_ready)
                for i in range(4):
                    mm = te.matmul(bank[:, 6 + cp, P * i:P * i + P], ar[:, i, 0, tok], state[:, i], start=False, stop=i == 3, skip_group_check=True)
                w_done = pe.after(mm)
                for i in range(4):
                    mm = te.matmul(bank[:, 4 + cp, P * i:P * i + P], ar[:, i, 1, tok], state[:, i], start=True, stop=True)
                o_done.append(pe.after(mm))
                wait(se, w_done)
                w_ready = padded(w, bank[:, 6 + cp].rearrange("p (i d) -> p i d", i=4))
                wait(te, w_ready)
                if cp:
                    wait(te, z_ready)
                for i in range(4):
                    for hp in range(2):
                        mm = te.matmul(bank[:, 0, P * i:P * i + P], xx[:, 4 * hp + i, 1], w[:, hp, i],
                                       start=hp == 0, stop=hp == 1)
                z_done = pe.after(mm)
                wait(se, z_done)
                z_ready = act_(zneg[half, :], bank[half, 0], ACT.Copy, scale=-1.0)
                keys_part(cp)
                c = 2 * j + cp
                wait(ve, *state_ready)
                keep = tt(scaled[:, :, :], state[:, :, :], pc[:, :, c:c + 1].broadcast_to([P, 4, P]), ALU.mult)
                wait(te, z_ready)
                for i in range(4):
                    mm = te.matmul(bank[:, 2 + cp, P * i:P * i + P], b_rows[half, i], zneg[half, P * i:P * i + P], start=False, stop=i == 3, skip_group_check=True)
                s_done = pe.after(mm)
                wait(ve, s_done, keep)
                state_ready = []
                for hp in range(2):
                    rr = slice(64 * hp, 64 * hp + 64)
                    state_ready.append(tt(state[rr, :, rr], scaled[rr, :, rr],
                                          bank[rr, 2 + cp].rearrange("p (i d) -> p i d", i=4)[:, :, rr], ALU.add))
                if cp == 0:
                    with_values(7, 0)
                    vz_read = with_values(1, 1)
            wait(se, z_ready, vz_read)
            z_padded = padded(vz, zneg[:, :].rearrange("p (i d) -> p i d", i=4))
            if j < 3:
                last["pairs"] = pair_products(bT, 6, 0, slice(P * j + P, P * j + 2 * P))
            wait(te, z_padded)
            for i in range(4):
                for hp in range(2):
                    mm = te.matmul(bank[:, 1, P * i:P * i + P], m_b[:, 4 * hp + i, 1], vz[:, hp, i], start=False, stop=i == 3 and hp == 1, skip_group_check=True)
            inner = pe.after(mm)
            orow = o_rows[:, j].rearrange("p h d -> p (h d)")
            wait(se, *o_done)
            e = [act_(orow[halves[cp]], bank[halves[cp], 4 + cp], ACT.Copy) for cp in range(2)]
            wait(ve, inner, *e)
            o_sum = tt(orow, orow, bank[:, 1], ALU.add)
            last = {"pairs": last.get("pairs"), "o": e, "z": [z_ready], "all": [o_sum, *state_ready, inner, z_ready, *e]}
            wait(ge, inner)

    m_hi = ms("m_hi", [P, DT, T], FR)
    m_lo = ms("m_lo", [P, DT, T], FR)
    with sb("o_sq", [P, 4, 8, 64]) as o_sq, sb("gs", [P, 2, 4, 8]) as gs, sb("oT", [P, 4, T]) as oT:
        o32, q32 = (a[:, :, :, :].rearrange("p j h d -> p (j h) d") for a in (o_rows, o_sq))
        mu, var = (gs[:, q].rearrange("p j h -> p (j h)") for q in range(2))

        def spread32(a):
            return a.unsqueeze(2).broadcast_to([P, 32, 64])

        wait(ve, *last["all"])
        m = dve.after(ve.tensor_reduce(mu, o32, AX, ALU.add))
        wait(ve, m)
        m = ts(mu, mu, 1.0 / 64, None, ALU.mult)
        wait(ve, m)
        m = tt(o32, o32, spread32(mu), ALU.subtract)
        wait(se, m)
        s2 = act_(q32, o32, ACT.Square)
        wait(ve, s2)
        m = dve.after(ve.tensor_reduce(var, q32, AX, ALU.add))
        wait(se, m)
        root = act_(var, var, ACT.Sqrt, scale=1.0 / 64, bias=eps[:, 2:3])
        wait(ve, root)
        m = dve.after(ve.reciprocal(var, var))
        wait(ve, m)
        m = tt(o32, o32, spread32(var), ALU.mult)
        wait(te, m)
        for i in range(4):
            for j in range(4):
                mm = te.transpose(bank[:, 4 + i, P * j:P * j + P], o_rows[:, j].rearrange("p h d -> p (h d)")[:, P * i:P * i + P], ident)
            turned = pe.after(mm)
            wait(ve, turned)
            m = ts(oT[:, i], bank[:, 4 + i], col("ln_x_g_2", i), col("ln_x_b_2", i), ALU.mult, ALU.add)
        wait(ve, m, bonus_ready, g_ready)
        m = tt(oT[:, :, :], oT[:, :, :], bonus[:, :, :], ALU.add)
        wait(ve, m)
        m = tt(oT[:, :, :], oT[:, :, :], gT[:, :, :], ALU.mult)
        mix_ready = [split_into(m_hi[:, 0:4], m_lo[:, 0:4], attnT[:, :, :], attn_ready)] * 4
        mix_ready += [split_into(m_hi[:, 4:8], m_lo[:, 4:8], oT[:, :, :], [m])] * 4

    with sb("mixed", [P, DT, T]) as mixed:
        sq = ar[:, :, :, :].rearrange("p i a t -> p (i a) t")
        wait(se, *mix_ready[7])
        wait(te, *last["all"])
        norm_mix = Rms(mixed, sq, ())
        mixed_ready = project(quarters(m_hi, m_lo, 2), 2, [[turned, m]] * 4, mix_ready,
                              lambda o, n: act_(mixed[:, o], bank[:, n], ACT.Copy), norm_mix)
        inv = norm_mix.end()
        wait(ve, inv)
        norm_x = Rms(xT, sq, (norm_mix.marks[-1],), on_pool=True)
        x_ready = []
        for k in range(DT):
            m = stt(mixed[:, k], mixed[:, k], col("norm_mix_post_2", k), rstd_bank, ALU.mult, ALU.mult)
            wait(ve, m)
            x_ready.append(tt(xT[:, k], xT[:, k], mixed[:, k], ALU.add))
            norm_x.add(x_ready[-1])
        norm["read"] = [m]
        inv = norm_x.end()
        mixer_done = [x_ready[-1], norm_x.marks[-1]]
    mixer.close()

    with sb("f_hi", [P, DT, T], FR) as h_hi, sb("f_lo", [P, DT, T], FR) as h_lo, \
            sb("u3_hi", [P, 16, T], FR) as u_hi, sb("u3_lo", [P, 16, T], FR) as u_lo, sb("f", [P, DT, T]) as f, \
            sb("conv", [P, 4, T]) as conv:
        wait(te, *mixer_done)
        wait(se, *mixer_done)
        ready = normalise(xT, inv, lambda k: col("norm_ffn_pre_2", k), None, h_hi, h_lo)
        free = [[mixer_done[0]]] * 4
        CW, CB = VEC_AT["conv_w_2"], VEC_AT["conv_b_2"]
        f_ready = [None] * DT
        for half in range(2):
            split_next()
            with slab_loop(8, {pe: 3, act: 8, dve: 12}) as loop:
                earlier = [(dve, dve.n + 2 * n + 2 - 12, loop) for n in range(4)]
                last_lo = (dve, dve.n, loop)
                slab_products((h_hi[:, 0:4], h_lo[:, 0:4]), range(4), [[earlier[n], *free[n]] for n in range(4)],
                              ready[0:4] if half == 0 else None, True, False)
                split_next()
                full = slab_products((h_hi[:, 4:8], h_lo[:, 4:8]), range(4), None, ready[4:8] if half == 0 else None, False, True)
                conv_done = []
                for n in range(4):
                    place = loop.i * 2 + (16 * half + 32 * (n // 2) + n % 2)

                    def cw(tap):
                        return vec[:, bass.ds(place + (CW + 64 * tap), 1)]

                    wait(se, full[n], last_lo)
                    here = act_(conv[:, n], bank[:, n], ACT.Identity, scale=cw(2), bias=vec[:, bass.ds(place + CB, 1)])
                    wait(ve, here)
                    one = stt(conv[:, n, 1:], bank[:, n, 0:T - 1], cw(1), conv[:, n, 1:], ALU.mult, ALU.add)
                    wait(ve, one)
                    conv_done.append(stt(conv[:, n, 2:], bank[:, n, 0:T - 2], cw(0), conv[:, n, 2:], ALU.mult, ALU.add))
                split_next()
                for n in range(2):
                    tile = bass.ds(loop.i * 2 + n, 1)
                    wait(se, conv_done[n])
                    act_gate = act_(conv[:, n], conv[:, n], ACT.Gelu_apprx_tanh)
                    wait(ve, act_gate, conv_done[2 + n])
                    prod = tt(conv[:, n], conv[:, n], conv[:, 2 + n], ALU.mult)
                    wait(se, prod)
                    made = act_(u_hi[:, tile, :], conv[:, n:n + 1], ACT.Copy)
                    wait(ve, made)
                    lo_done = tt(u_lo[:, tile, :], conv[:, n:n + 1], u_hi[:, tile, :].bitcast(F32), ALU.subtract)
            end_loop(8)
            norm_f = Rms(f, conv, (lo_done,)) if half else None

            def add_to_f(o, n):
                if half == 0:
                    return dve.after(ve.tensor_copy(f[:, o], bank[:, n]))
                return tt(f[:, o], f[:, o], bank[:, n], ALU.add)

            f_ready = project(quarters(u_hi, u_lo, 4), 2, [[conv_done[n]] for n in range(4)],
                              [[before(before(m)) for m in (made, lo_done)]] * 12 + [[made, lo_done]] * 4, add_to_f, norm_f)
            free = [[m] for m in f_ready[4:8]]
    finish = ExitStack()
    sqf = finish.enter_context(nc.sbuf_tensor("sq_f", [P, DT, T], F32))
    rows_out = finish.enter_context(nc.sbuf_tensor("rows_out", [P, 4, D], F32))
    inv = norm_f.end()
    wait(ve, inv)
    turned_free = [None, None]
    stored = nc.alloc_semaphore("stored")
    x_ready = []
    for k in range(DT):
        m = stt(f[:, k], f[:, k], col("norm_ffn_post_2", k), rstd_bank, ALU.mult, ALU.mult)
        wait(ve, m)
        x_ready.append(tt(xT[:, k], xT[:, k], f[:, k], ALU.add))
    for k in range(DT):
        wait(te, x_ready[k])
        if turned_free[k % 2]:
            wait(te, turned_free[k % 2])
        for j in range(4):
            mm = te.transpose(bank[:, 6 + k % 2, P * j:P * j + P], xT[:, k, P * j:P * j + P], ident)
        turned = pe.after(mm)
        wait(se, turned)
        turned_free[k % 2] = act_(rows_out[:, :, P * k:P * k + P], bank[:, 6 + k % 2].rearrange("p (j f) -> p j f", j=4), ACT.Copy)
        if k % 4 == 3:
            half = slice(P * (k - 3), P * (k + 1))
            wait(sy, *turned_free)
            sy.dma_start(out[0].rearrange("(j p) n -> p j n", p=P)[:, :, half], rows_out[:, :, half]).then_inc(stored, 16)
    sy.wait_ge(stored, 32)


WEIGHTS = ["ada_w", "pool_w", "sgu_w_in", "sgu_w_s", "sgu_b_s", "sgu_w_out", "mlp_w1", "mlp_w2",
           "w_decay_up_2", "w_iclr_up_2", "w_gate_up_2", "w_out_2", "w_ffn_up_2", "w_ffn_down_2", "w_in_2",
           "rel_bias_2", "sinks_2"]
ONE_LAYER = ["sgu_w_in", "sgu_w_out", "w_decay_up_2", "w_iclr_up_2", "w_gate_up_2", "w_out_2",
             "w_ffn_up_2", "w_ffn_down_2", "w_in_2"]


def laid_out(inputs):
    arrays = {n: np.asarray(inputs[n]) for n in WEIGHTS}
    arrays["x"] = np.asarray(inputs["x"])
    for n in ONE_LAYER:
        arrays[n] = arrays[n][0]
    heads = np.concatenate([np.arange(64) + 64 * h for i in range(4) for h in (i, i + 4)])
    w_in, w_out = arrays["w_in_2"].copy(), arrays["w_out_2"].copy()
    w_in[:, :512] = arrays["w_in_2"][:, heads]
    w_out[:512] = arrays["w_out_2"][heads]
    arrays["w_in_2"], arrays["w_out_2"] = w_in, w_out
    flat = np.concatenate([np.asarray(inputs[n]).ravel() for n, _ in VECS])
    arrays["vecs"] = np.concatenate([flat, np.zeros(512 * P - flat.size, flat.dtype)]).reshape(512, P)
    arrays["const"], arrays["buckets"] = constants()
    return {n: np.ascontiguousarray(a) for n, a in arrays.items()}


def declared(nc, arrays):
    t = {n: nc.dram_tensor(f"in_{n}", a.shape, mybir.dt.from_np(a.dtype), kind="ExternalInput").ap()
         for n, a in arrays.items()}
    t["scratch"] = nc.dram_tensor("bias_table", (8, 384), F32, kind="Internal").ap()
    return t, nc.dram_tensor("out", (1, T, D), F32, kind="ExternalOutput").ap()


def kernel(**inputs):
    import concourse.bacc as bacc
    from concourse.bass_utils import run_bass_kernel_spmd
    arrays = laid_out(inputs)
    nc = bacc.Bacc("TRN2", target_bir_lowering=False, num_devices=1)
    program(nc, *declared(nc, arrays))
    r = run_bass_kernel_spmd(nc, [{f"in_{n}": a for n, a in arrays.items()}], core_ids=[0])
    return r.results[0]["out"]
```
